# Optimizing a Trainium2 kernel written in Bass

```python
import jax, jax.numpy as jnp
from jax import lax
import numpy as np

D_MODEL = 1024
BATCH = 1
SEQ = 256
DEPTH = 2

D_FF = 2816
GDN_HEADS = 8
GDN_DK = 128
GDN_DV = 128
GDN_CONV = 4
CHUNK = 64
CNV_CH = 1024
CNV_K = 31
W_Q = GDN_HEADS * GDN_DK
W_K = GDN_HEADS * GDN_DK
W_V = GDN_HEADS * GDN_DV
W_Z = GDN_HEADS * GDN_DV
W_BETA = GDN_HEADS
W_A = GDN_HEADS
W_GLU = 2 * CNV_CH
W_GATE = 2 * D_MODEL
SPLITS = [int(s) for s in np.cumsum([W_Q + W_K + W_V, W_Z, W_BETA, W_A, W_GLU])]
P_IN = W_Q + W_K + W_V + W_Z + W_BETA + W_A + W_GLU + W_GATE
RMS_EPS = 1e-6
LN_EPS = 1e-5


def rmsnorm(x, w):
    xf = x.astype(jnp.float32)
    y = xf * lax.rsqrt(jnp.mean(xf * xf, axis=-1, keepdims=True) + RMS_EPS)
    return (y * w.astype(jnp.float32)).astype(x.dtype)

def layernorm(x, g, b):
    xf = x.astype(jnp.float32)
    mu = jnp.mean(xf, axis=-1, keepdims=True)
    var = jnp.mean(jnp.square(xf - mu), axis=-1, keepdims=True)
    y = (xf - mu) * lax.rsqrt(var + LN_EPS)
    return (y * g.astype(jnp.float32) + b.astype(jnp.float32)).astype(x.dtype)

def l2norm(x):
    return x * lax.rsqrt(jnp.sum(x * x, axis=-1, keepdims=True) + 1e-6)

def causal_dwconv(x, w):
    k, c = w.shape
    return lax.conv_general_dilated(
        x, w[:, None, :].astype(x.dtype), window_strides=(1,), padding=[(k - 1, 0)],
        dimension_numbers=("NWC", "WIO", "NWC"), feature_group_count=c)

def swiglu_ffn(h, w_in, w_out):
    gate, up = jnp.split(h @ w_in, 2, axis=-1)
    return (jax.nn.silu(gate) * up) @ w_out

def chunk_gated_delta_rule(q, k, v, g, beta):
    b, l, h, dk = q.shape
    dv = v.shape[-1]
    n = l // CHUNK

    def to_chunks(t):
        return t.reshape(b, n, CHUNK, h, -1).transpose(0, 3, 1, 2, 4)

    q, k, v = to_chunks(q), to_chunks(k), to_chunks(v)
    g = g.reshape(b, n, CHUNK, h).transpose(0, 3, 1, 2)
    beta = beta.reshape(b, n, CHUNK, h).transpose(0, 3, 1, 2)
    G = jnp.cumsum(g, axis=-1)
    causal = jnp.tril(jnp.ones((CHUNK, CHUNK), dtype=bool))
    strict = jnp.tril(jnp.ones((CHUNK, CHUNK), dtype=bool), k=-1)
    diff = G[..., :, None] - G[..., None, :]
    decay = jnp.where(causal, jnp.exp(jnp.where(causal, diff, 0.0)), 0.0)
    kk = jnp.einsum("bhncd,bhnsd->bhncs", k, k)
    a_mat = jnp.where(strict, kk * decay * beta[..., :, None], 0.0)
    lhs = jnp.eye(CHUNK, dtype=jnp.float32) + a_mat
    rhs = jnp.concatenate([v * beta[..., None], k * (beta * jnp.exp(G))[..., None]], axis=-1)
    sol = lax.linalg.triangular_solve(lhs, rhs, left_side=True, lower=True, unit_diagonal=True)
    u, w = sol[..., :dv], sol[..., dv:]
    qk = jnp.einsum("bhncd,bhnsd->bhncs", q, k) * decay
    q_dec = q * jnp.exp(G)[..., None]
    k_dec = k * jnp.exp(G[..., -1:] - G)[..., None]
    chunk_decay = jnp.exp(G[..., -1])

    xs = tuple(jnp.moveaxis(t, 2, 0) for t in (q_dec, k_dec, u, w, qk, chunk_decay))

    def step(state, inp):
        q_c, k_c, u_c, w_c, qk_c, d_c = inp
        v_new = u_c - jnp.einsum("bhck,bhkv->bhcv", w_c, state)
        o_c = jnp.einsum("bhck,bhkv->bhcv", q_c, state) + jnp.einsum("bhcs,bhsv->bhcv", qk_c, v_new)
        state = state * d_c[..., None, None] + jnp.einsum("bhck,bhcv->bhkv", k_c, v_new)
        return state, o_c

    s0 = jnp.zeros((b, h, dk, dv), jnp.float32)
    _, o = lax.scan(step, s0, xs)
    return o.transpose(1, 0, 3, 2, 4).reshape(b, l, h, dv)

def gated_deltanet(qkv, z, beta_logit, a_logit, conv_w, a_log, dt_bias, norm_w, w_o):
    b, l, _ = qkv.shape
    qkv = jax.nn.silu(causal_dwconv(qkv, conv_w))
    q, k, v = jnp.split(qkv.astype(jnp.float32), [W_Q, W_Q + W_K], axis=-1)
    q = l2norm(q.reshape(b, l, GDN_HEADS, GDN_DK)) * (GDN_DK ** -0.5)
    k = l2norm(k.reshape(b, l, GDN_HEADS, GDN_DK))
    v = v.reshape(b, l, GDN_HEADS, GDN_DV)
    beta = jax.nn.sigmoid(beta_logit.astype(jnp.float32))
    g = -jnp.exp(a_log.astype(jnp.float32)) * jax.nn.softplus(
        a_logit.astype(jnp.float32) + dt_bias.astype(jnp.float32))
    o = chunk_gated_delta_rule(q, k, v, g, beta)
    zf = z.astype(jnp.float32).reshape(b, l, GDN_HEADS, GDN_DV)
    o = rmsnorm(o, norm_w) * jax.nn.silu(zf)
    return o.reshape(b, l, GDN_HEADS * GDN_DV).astype(qkv.dtype) @ w_o

def conformer_conv(glu_in, pw1_b, dw_w, dw_b, ln_g, ln_b, w_o, b_o):
    a, gate = jnp.split(glu_in + pw1_b, 2, axis=-1)
    h = a * jax.nn.sigmoid(gate)
    h = causal_dwconv(h, dw_w) + dw_b
    h = jax.nn.silu(layernorm(h, ln_g, ln_b))
    return h @ w_o + b_o

def first_inputs(seed: int = 0) -> dict:
    key = jax.random.key(seed)
    ks = iter(jax.random.split(key, 40))

    def nrm(shape, scale):
        return jax.random.normal(next(ks), shape, jnp.float32) * scale

    def gain(shape):
        return 1.0 + 0.02 * jax.random.normal(next(ks), shape, jnp.float32)

    L = DEPTH
    inp = {}
    inp["x"] = nrm((BATCH, SEQ, D_MODEL), 1.0)
    inp["ffn1_norm_pre"] = gain((L, D_MODEL))
    inp["ffn1_norm_post"] = gain((L, D_MODEL))
    inp["ffn1_w_in"] = nrm((L, D_MODEL, 2 * D_FF), D_MODEL ** -0.5)
    inp["ffn1_w_out"] = nrm((L, D_FF, D_MODEL), D_FF ** -0.5)
    inp["mix_norm_pre"] = gain((L, D_MODEL))
    inp["mix_norm_post"] = gain((L, D_MODEL))
    inp["mix_w_in"] = nrm((L, D_MODEL, P_IN), D_MODEL ** -0.5)
    inp["gdn_conv_w"] = nrm((L, GDN_CONV, W_Q + W_K + W_V), GDN_CONV ** -0.5)
    inp["gdn_a_log"] = jnp.log(jax.random.uniform(next(ks), (L, GDN_HEADS), jnp.float32, 1.0, 16.0))
    dt = jnp.exp(jax.random.uniform(next(ks), (L, GDN_HEADS), jnp.float32, np.log(1e-3), np.log(1e-1)))
    inp["gdn_dt_bias"] = dt + jnp.log(-jnp.expm1(-dt))
    inp["gdn_norm_w"] = gain((L, GDN_DV))
    inp["gdn_w_o"] = nrm((L, GDN_HEADS * GDN_DV, D_MODEL), (GDN_HEADS * GDN_DV) ** -0.5)
    inp["cnv_pw1_b"] = nrm((L, W_GLU), 0.02)
    inp["cnv_dw_w"] = nrm((L, CNV_K, CNV_CH), CNV_K ** -0.5)
    inp["cnv_dw_b"] = nrm((L, CNV_CH), 0.02)
    inp["cnv_ln_g"] = gain((L, CNV_CH))
    inp["cnv_ln_b"] = nrm((L, CNV_CH), 0.02)
    inp["cnv_w_o"] = nrm((L, CNV_CH, D_MODEL), CNV_CH ** -0.5)
    inp["cnv_b_o"] = nrm((L, D_MODEL), 0.02)
    inp["mix_w_out"] = nrm((L, D_MODEL, D_MODEL), D_MODEL ** -0.5)
    inp["ffn2_norm_pre"] = gain((L, D_MODEL))
    inp["ffn2_norm_post"] = gain((L, D_MODEL))
    inp["ffn2_w_in"] = nrm((L, D_MODEL, 2 * D_FF), D_MODEL ** -0.5)
    inp["ffn2_w_out"] = nrm((L, D_FF, D_MODEL), D_FF ** -0.5)
    return inp

def first_block(x, ffn1_norm_pre, ffn1_norm_post, ffn1_w_in, ffn1_w_out,
              mix_norm_pre, mix_norm_post, mix_w_in,
              gdn_conv_w, gdn_a_log, gdn_dt_bias, gdn_norm_w, gdn_w_o,
              cnv_pw1_b, cnv_dw_w, cnv_dw_b, cnv_ln_g, cnv_ln_b, cnv_w_o, cnv_b_o,
              mix_w_out,
              ffn2_norm_pre, ffn2_norm_post, ffn2_w_in, ffn2_w_out):
    for i in range(DEPTH):
        f = swiglu_ffn(rmsnorm(x, ffn1_norm_pre[i]), ffn1_w_in[i], ffn1_w_out[i])
        x = x + 0.5 * rmsnorm(f, ffn1_norm_post[i])

        h = rmsnorm(x, mix_norm_pre[i])
        p = h @ mix_w_in[i]
        qkv, z, beta_logit, a_logit, glu_in, gates = jnp.split(p, SPLITS, axis=-1)
        y_a = gated_deltanet(qkv, z, beta_logit, a_logit, gdn_conv_w[i], gdn_a_log[i],
                             gdn_dt_bias[i], gdn_norm_w[i], gdn_w_o[i])
        y_b = conformer_conv(glu_in, cnv_pw1_b[i], cnv_dw_w[i], cnv_dw_b[i],
                             cnv_ln_g[i], cnv_ln_b[i], cnv_w_o[i], cnv_b_o[i])
        g_a, g_b = jnp.split(jax.nn.sigmoid(gates), 2, axis=-1)
        y = (g_a * y_a + g_b * y_b) @ mix_w_out[i]
        x = x + rmsnorm(y, mix_norm_post[i])

        f = swiglu_ffn(rmsnorm(x, ffn2_norm_pre[i]), ffn2_w_in[i], ffn2_w_out[i])
        x = x + 0.5 * rmsnorm(f, ffn2_norm_post[i])
    return x


DEPTH_2 = 4

N_MIXERS = 3
N_GLA = (DEPTH_2 + 2) // 3
N_MLA = (DEPTH_2 + 1) // 3
N_CONV = DEPTH_2 // 3
ALPHA = (2 * DEPTH_2) ** 0.25
BETA = (8 * DEPTH_2) ** -0.25
PLE_DIM = 256
D_FF_2 = 4 * D_MODEL
MAX_OFFSET = 4096

GLA_HEADS = 4
GLA_DK = D_MODEL // 2 // GLA_HEADS
GLA_DV = D_MODEL // GLA_HEADS
GLA_GATE_RANK = 16
GLA_TAU = 16.0
GLA_HK = GLA_HEADS * GLA_DK
GLA_HV = GLA_HEADS * GLA_DV
GLA_SPLITS = [GLA_HK, 2 * GLA_HK, 2 * GLA_HK + GLA_HV, 2 * GLA_HK + GLA_HV + D_MODEL]
GLA_IN = 2 * GLA_HK + GLA_HV + D_MODEL + GLA_GATE_RANK

MLA_HEADS = 8
MLA_NOPE = 128
MLA_ROPE = 64
MLA_V = 128
MLA_Q_RANK = 256
MLA_KV_RANK = 256
MLA_IN = MLA_Q_RANK + MLA_KV_RANK + MLA_ROPE
ROPE_BASE = 10000.0
Q_BLOCK = 128

CONV_WIDTH = 3


def layer_norm(x, g, b):
    xf = x.astype(jnp.float32)
    mu = jnp.mean(xf, -1, keepdims=True)
    var = jnp.mean(jnp.square(xf - mu), -1, keepdims=True)
    return ((xf - mu) * lax.rsqrt(var + LN_EPS) * g + b).astype(x.dtype)

def rms_norm(x, g):
    xf = x.astype(jnp.float32)
    return (xf * lax.rsqrt(jnp.mean(xf * xf, -1, keepdims=True) + RMS_EPS) * g).astype(x.dtype)

def rope(x, cos, sin):
    x1, x2 = jnp.split(x, 2, axis=-1)
    return jnp.concatenate([x1 * cos - x2 * sin, x2 * cos + x1 * sin], axis=-1)

def gla_mixer(x, w_in, w_gate_up, b_gate, norm_g, w_out):
    B_, S_, _ = x.shape
    nc = S_ // CHUNK
    q, k, v, r, g_lr = jnp.split(x @ w_in, GLA_SPLITS, axis=-1)
    log_a = jax.nn.log_sigmoid((g_lr @ w_gate_up + b_gate).astype(jnp.float32)) / GLA_TAU

    def to_chunks(t, d):
        return t.astype(jnp.float32).reshape(B_, nc, CHUNK, GLA_HEADS, d).transpose(1, 0, 3, 2, 4)

    qc = to_chunks(q, GLA_DK) * GLA_DK ** -0.5
    kc = to_chunks(k, GLA_DK)
    vc = to_chunks(v, GLA_DV)
    lc = to_chunks(log_a, GLA_DK)

    def step(state, inp):
        q_, k_, v_, la = inp
        L = jnp.cumsum(la, axis=2)
        decay = jnp.exp(-jnp.abs(L[:, :, :, None, :] - L[:, :, None, :, :]))
        scores = jnp.einsum('bhtd,bhsd,bhtsd->bhts', q_, k_, decay)
        o = scores @ v_ + (q_ * jnp.exp(L)) @ state
        L_end = L[:, :, -1:, :]
        state = (jnp.exp(L_end[:, :, 0, :, None]) * state
                 + jnp.einsum('bhsd,bhse->bhde', k_ * jnp.exp(L_end - L), v_))
        return state, o

    s0 = jnp.zeros((B_, GLA_HEADS, GLA_DK, GLA_DV), jnp.float32)
    _, o = lax.scan(step, s0, (qc, kc, vc, lc))
    o = o.transpose(1, 0, 3, 2, 4).reshape(B_, S_, GLA_HEADS, GLA_DV)
    o = rms_norm(o, norm_g).reshape(B_, S_, GLA_HV) * jax.nn.silu(r.astype(jnp.float32))
    return o.astype(x.dtype) @ w_out

def mla_mixer(x, cos, sin, w_in, q_norm, kv_norm, w_uq, w_ukv, w_out):
    B_, S_, _ = x.shape
    c_q, c_kv, k_rope = jnp.split(x @ w_in, [MLA_Q_RANK, MLA_Q_RANK + MLA_KV_RANK], axis=-1)
    q = (rms_norm(c_q, q_norm) @ w_uq).reshape(B_, S_, MLA_HEADS, MLA_NOPE + MLA_ROPE)
    kv = (rms_norm(c_kv, kv_norm) @ w_ukv).reshape(B_, S_, MLA_HEADS, MLA_NOPE + MLA_V)
    q_nope, q_rope = jnp.split(q, [MLA_NOPE], axis=-1)
    k_nope, v = jnp.split(kv, [MLA_NOPE], axis=-1)
    q_rope = rope(q_rope, cos[:, :, None, :], sin[:, :, None, :])
    k_rope = rope(k_rope, cos, sin)
    qf = jnp.concatenate([q_nope.astype(jnp.float32), q_rope.astype(jnp.float32)], axis=-1)
    qf = qf * (MLA_NOPE + MLA_ROPE) ** -0.5
    kf = jnp.concatenate([k_nope.astype(jnp.float32),
                          jnp.broadcast_to(k_rope.astype(jnp.float32)[:, :, None, :],
                                           (B_, S_, MLA_HEADS, MLA_ROPE))], axis=-1)
    n_qb = S_ // Q_BLOCK
    q_blocks = qf.reshape(B_, n_qb, Q_BLOCK, MLA_HEADS, MLA_NOPE + MLA_ROPE).transpose(1, 0, 2, 3, 4)
    key_chunk = jnp.arange(S_) // CHUNK

    def attend(args):
        qb, bi = args
        q_chunk = (bi * Q_BLOCK + jnp.arange(Q_BLOCK)) // CHUNK
        s = jnp.einsum('bqhd,bkhd->bhqk', qb, kf)
        s = jnp.where(key_chunk[None, :] <= q_chunk[:, None], s, -jnp.inf)
        pr = jax.nn.softmax(s, axis=-1)
        return jnp.einsum('bhqk,bkhd->bqhd', pr.astype(v.dtype), v)

    o = lax.map(attend, (q_blocks, jnp.arange(n_qb)))
    o = o.transpose(1, 0, 2, 3, 4).reshape(B_, S_, MLA_HEADS * MLA_V)
    return o.astype(x.dtype) @ w_out

def conv_mixer(x, w_in, conv_w, w_out):
    b, c, u = jnp.split(x @ w_in, 3, axis=-1)
    z = lax.conv_general_dilated(c * u, conv_w[:, None, :], window_strides=(1,),
                                 padding=[(CONV_WIDTH - 1, 0)],
                                 dimension_numbers=('NWC', 'WIO', 'NWC'),
                                 feature_group_count=D_MODEL)
    return (b * z) @ w_out

def sq_relu_mlp(x, w1, w2):
    return jnp.square(jax.nn.relu(x @ w1)) @ w2

def second_inputs(seed: int = 0) -> dict:
    key = jax.random.key(seed)
    ks = jax.random.split(key, 24)

    def nrm(i, shape, scale):
        return jax.random.normal(ks[i], shape, jnp.float32) * scale

    x = nrm(0, (BATCH, SEQ, D_MODEL), 1.0)
    p = nrm(1, (DEPTH_2, BATCH, SEQ, PLE_DIM), 1.0)
    offsets = jax.random.randint(ks[2], (BATCH, 1), 0, MAX_OFFSET, dtype=jnp.int32)
    positions = (offsets + jnp.arange(SEQ, dtype=jnp.int32)[None, :]).astype(jnp.int32)
    return {
        'x': x,
        'p': p,
        'positions': positions,
        'gla_w_in': nrm(3, (N_GLA, D_MODEL, GLA_IN), D_MODEL ** -0.5),
        'gla_w_gate_up': nrm(4, (N_GLA, GLA_GATE_RANK, GLA_HK), GLA_GATE_RANK ** -0.5),
        'gla_b_gate': nrm(5, (N_GLA, GLA_HK), 0.1),
        'gla_norm_g': 1.0 + nrm(6, (N_GLA, GLA_DV), 0.01),
        'gla_w_out': nrm(7, (N_GLA, GLA_HV, D_MODEL), GLA_HV ** -0.5 * BETA),
        'mla_w_in': nrm(8, (N_MLA, D_MODEL, MLA_IN), D_MODEL ** -0.5),
        'mla_q_norm': 1.0 + nrm(9, (N_MLA, MLA_Q_RANK), 0.01),
        'mla_kv_norm': 1.0 + nrm(10, (N_MLA, MLA_KV_RANK), 0.01),
        'mla_w_uq': nrm(11, (N_MLA, MLA_Q_RANK, MLA_HEADS * (MLA_NOPE + MLA_ROPE)), MLA_Q_RANK ** -0.5),
        'mla_w_ukv': nrm(12, (N_MLA, MLA_KV_RANK, MLA_HEADS * (MLA_NOPE + MLA_V)), MLA_KV_RANK ** -0.5),
        'mla_w_out': nrm(13, (N_MLA, MLA_HEADS * MLA_V, D_MODEL), (MLA_HEADS * MLA_V) ** -0.5 * BETA),
        'conv_w_in': nrm(14, (N_CONV, D_MODEL, 3 * D_MODEL), D_MODEL ** -0.5),
        'conv_w': nrm(15, (N_CONV, CONV_WIDTH, D_MODEL), CONV_WIDTH ** -0.5),
        'conv_w_out': nrm(16, (N_CONV, D_MODEL, D_MODEL), D_MODEL ** -0.5 * BETA),
        'ln_g': 1.0 + nrm(17, (DEPTH_2, 2, D_MODEL), 0.01),
        'ln_b': nrm(18, (DEPTH_2, 2, D_MODEL), 0.01),
        'mlp_w1': nrm(19, (DEPTH_2, D_MODEL, D_FF_2), D_MODEL ** -0.5),
        'mlp_w2': nrm(20, (DEPTH_2, D_FF_2, D_MODEL), D_FF_2 ** -0.5 * BETA),
        'ple_w_gate': nrm(21, (DEPTH_2, D_MODEL, D_MODEL), D_MODEL ** -0.5),
        'ple_w_proj': nrm(22, (DEPTH_2, PLE_DIM, D_MODEL), PLE_DIM ** -0.5),
    }

def second_block(x, p, positions, gla_w_in, gla_w_gate_up, gla_b_gate, gla_norm_g, gla_w_out,
              mla_w_in, mla_q_norm, mla_kv_norm, mla_w_uq, mla_w_ukv, mla_w_out,
              conv_w_in, conv_w, conv_w_out, ln_g, ln_b, mlp_w1, mlp_w2,
              ple_w_gate, ple_w_proj):
    inv_freq = ROPE_BASE ** (-jnp.arange(0, MLA_ROPE // 2, dtype=jnp.float32) * (2.0 / MLA_ROPE))
    ang = positions.astype(jnp.float32)[..., None] * inv_freq
    cos, sin = jnp.cos(ang), jnp.sin(ang)
    for i in range(DEPTH_2):
        j = i // N_MIXERS
        kind = i % N_MIXERS
        if kind == 0:
            h = gla_mixer(x, gla_w_in[j], gla_w_gate_up[j], gla_b_gate[j], gla_norm_g[j], gla_w_out[j])
        elif kind == 1:
            h = mla_mixer(x, cos, sin, mla_w_in[j], mla_q_norm[j], mla_kv_norm[j],
                          mla_w_uq[j], mla_w_ukv[j], mla_w_out[j])
        else:
            h = conv_mixer(x, conv_w_in[j], conv_w[j], conv_w_out[j])
        x = layer_norm(ALPHA * x + h, ln_g[i, 0], ln_b[i, 0])
        x = layer_norm(ALPHA * x + sq_relu_mlp(x, mlp_w1[i], mlp_w2[i]), ln_g[i, 1], ln_b[i, 1])
        x = x + jax.nn.sigmoid(x @ ple_w_gate[i]) * (p[i] @ ple_w_proj[i])
    return x


def setup_inputs(seed=0):
    out = dict(first_inputs(seed))
    for name, value in second_inputs(seed + 1).items():
        if name != "x":
            out[name + "_2"] = value
    return out


def reference(
    x, ffn1_norm_pre, ffn1_norm_post, ffn1_w_in, ffn1_w_out, mix_norm_pre, mix_norm_post,
    mix_w_in, gdn_conv_w, gdn_a_log, gdn_dt_bias, gdn_norm_w, gdn_w_o, cnv_pw1_b, cnv_dw_w,
    cnv_dw_b, cnv_ln_g, cnv_ln_b, cnv_w_o, cnv_b_o, mix_w_out, ffn2_norm_pre, ffn2_norm_post,
    ffn2_w_in, ffn2_w_out, p_2, positions_2, gla_w_in_2, gla_w_gate_up_2, gla_b_gate_2,
    gla_norm_g_2, gla_w_out_2, mla_w_in_2, mla_q_norm_2, mla_kv_norm_2, mla_w_uq_2, mla_w_ukv_2,
    mla_w_out_2, conv_w_in_2, conv_w_2, conv_w_out_2, ln_g_2, ln_b_2, mlp_w1_2, mlp_w2_2,
    ple_w_gate_2, ple_w_proj_2,
):
    x = first_block(
        x, ffn1_norm_pre, ffn1_norm_post, ffn1_w_in, ffn1_w_out, mix_norm_pre, mix_norm_post,
        mix_w_in, gdn_conv_w, gdn_a_log, gdn_dt_bias, gdn_norm_w, gdn_w_o, cnv_pw1_b, cnv_dw_w,
        cnv_dw_b, cnv_ln_g, cnv_ln_b, cnv_w_o, cnv_b_o, mix_w_out, ffn2_norm_pre,
        ffn2_norm_post, ffn2_w_in, ffn2_w_out,
    )
    return second_block(
        x, p_2, positions_2, gla_w_in_2, gla_w_gate_up_2, gla_b_gate_2, gla_norm_g_2,
        gla_w_out_2, mla_w_in_2, mla_q_norm_2, mla_kv_norm_2, mla_w_uq_2, mla_w_ukv_2,
        mla_w_out_2, conv_w_in_2, conv_w_2, conv_w_out_2, ln_g_2, ln_b_2, mlp_w1_2, mlp_w2_2,
        ple_w_gate_2, ple_w_proj_2,
    )


_drawn_inputs = setup_inputs


def setup_inputs(seed=0):
    import zlib

    import numpy as np

    out = dict(_drawn_inputs(seed))
    spreads = {}
    factors = {'ffn1_norm_pre': 3.005,
     'ffn1_norm_post': 4.3,
     'mix_norm_post': 3.378,
     'gdn_norm_w': 4.89,
     'cnv_pw1_b': 4.12,
     'cnv_ln_g': 4.02,
     'cnv_ln_b': 4.433,
     'cnv_b_o': 2.833,
     'ffn2_norm_pre': 5.16,
     'ffn2_norm_post': 7.564,
     'gla_b_gate_2': 8.0,
     'gla_norm_g_2': 8.0,
     'mla_q_norm_2': 8.0,
     'mla_kv_norm_2': 8.0}
    for name, (base, spread) in spreads.items():
        noise = np.random.default_rng([zlib.crc32(name.encode()), seed]).standard_normal(out[name].shape)
        drawn = base * np.exp(spread * noise) if base else spread * noise
        out[name] = __import__('jax').numpy.asarray(drawn.astype(out[name].dtype))
    for name, factor in factors.items():
        out[name] = (out[name] * factor).astype(out[name].dtype)
    return out
```

```python
from contextlib import ExitStack

import numpy as np

import concourse.bass as bass
from concourse import mybir

F32 = mybir.dt.float32
F32R = mybir.dt.float32r
I32 = mybir.dt.int32
ALU = mybir.AluOpType
ACT = mybir.ActivationFunctionType
AX = mybir.AxisListType

P = 128
D = 1024
SEQ = 256
NT = SEQ // P
KC = D // P
UW = 1024
NS = 4
BANK = 512

L1, L2 = 2, 4
FF1 = 2816
FF1_C = FF1 // P
FF1_HALF = FF1_C // 2
FF2_C = 4 * D // P
FF2_HALF = 11
GH, GDK = 8, 128
CH = 64
CONV1 = 4
CONVB = 31
LH, LDV = 4, 256
MH, MN, MR = 8, 128, 64
RMS_EPS, LN_EPS, L2_EPS = 1e-6, 1e-5, 1e-6
ALPHA = (2 * L2) ** 0.25
TAU = 16.0
KINDS = ["gla", "mla", "conv", "gla"]
LEVELS = [1, 2, 4, 8, 16, 32]
NORM_SCALE = float(GDK) ** -0.5
MLA_SCALE = float(MN + MR) ** -0.5


class Columns:

    def __init__(self):
        self.at, self.n, self.parts = {}, 0, []

    def add(self, name, key, count):
        self.at[key] = self.n
        self.parts.append((name, key, count))
        self.n += count


def column_layout():
    c = Columns()
    for i in range(L1):
        c.add("ffn1_norm_pre", ("ffn1", i), KC)
        c.add("mix_norm_pre", ("mix", i), KC)
        c.add("ffn2_norm_pre", ("ffn2", i), KC)
        c.add("gdn_conv_w", ("convw", i), 24 * CONV1)
        c.add("cnv_pw1_b", ("pw1b", i), 16)
        c.add("cnv_dw_w", ("dww", i), KC * CONVB)
        c.add("cnv_dw_b", ("dwb", i), KC)
        c.add("cnv_ln_g", ("lng", i), KC)
        c.add("cnv_ln_b", ("lnb", i), KC)
    c.add("mla_q_norm_2", ("qnorm", 0), 2)
    c.add("mla_kv_norm_2", ("kvnorm", 0), 2)
    c.add("conv_w_2", ("conv3", 0), KC * 3)
    return c


def row_layout():
    rows = []
    for i in range(L1):
        rows.append([("ffn1_norm_post", i)])
        rows.append([("cnv_b_o", i)])
        rows.append([("mix_norm_post", i)])
        rows.append([("ffn2_norm_post", i)])
    for i in range(L2):
        rows.append([("ln_g_2", i, 0), ("ln_b_2", i, 0)])
        rows.append([("ln_g_2", i, 1), ("ln_b_2", i, 1)])
    return rows


def unit_list():
    u = []

    def feature(w, i, col, k=KC, chunks=1):
        u.append(("T", w, i, col, k, chunks))

    def rows(w, i, kc, col=0, width=UW):
        u.append(("R", w, i, kc, col, width))

    def ffn1(a, b, i):
        for half in range(2):
            for c in range(half * FF1_HALF, (half + 1) * FF1_HALF):
                feature(a, i, c * P)
                feature(a, i, FF1 + c * P)
            for c in range(half * FF1_HALF, (half + 1) * FF1_HALF):
                rows(b, i, c)

    for i in range(L1):
        ffn1("ffn1_w_in", "ffn1_w_out", i)
        for c in range(24):
            feature("mix_w_in", i, c * P)
        for k in range(KC):
            rows("mix_w_in", i, k, 3072)
        rows("mix_w_in", i, 0, 4096, 16)
        for k in range(KC):
            rows("mix_w_in", i, k, 4112 + 2048)
        for k in range(KC):
            rows("mix_w_in", i, k, 4112 + 3072)
        for c in range(KC):
            feature("mix_w_in", i, 4112 + c * P)
            feature("mix_w_in", i, 4112 + 1024 + c * P)
        for w in ("cnv_w_o", "gdn_w_o", "mix_w_out"):
            for k in range(KC):
                rows(w, i, k)
        ffn1("ffn2_w_in", "ffn2_w_out", i)
    for i, kind in enumerate(KINDS):
        j = i // 3
        if kind == "gla":
            for c in range(8):
                feature("gla_w_in_2", j, c * P)
            for k in range(KC):
                rows("gla_w_in_2", j, k, 1024)
            for k in range(KC):
                rows("gla_w_in_2", j, k, 2048)
            rows("gla_w_in_2", j, 0, 3072, 16)
            for k in range(KC):
                rows("gla_w_out_2", j, k)
        elif kind == "mla":
            for k in range(0, KC, 2):
                rows("mla_w_in_2", j, k, 0, 512)
            rows("mla_w_in_2", j, 0, 512, MR)
            for c in range(0, MH, 4):
                feature("mla_uq_nope", j, c * P, 2, 4)
            rows("mla_uq_rope", j, 0, 0, 512)
            for c in range(0, MH, 4):
                feature("mla_uk", j, c * P, 2, 4)
            for k in range(2):
                rows("mla_uv", j, k)
            for k in range(KC):
                rows("mla_w_out_2", j, k)
        else:
            for c in range(KC):
                feature("conv_w_in_2", j, D + c * P)
                feature("conv_w_in_2", j, 2 * D + c * P)
            for c in range(KC):
                feature("conv_w_in_2", j, c * P)
            for k in range(KC):
                rows("conv_w_out_2", j, k)
        for first in range(0, FF2_C, FF2_HALF):
            part = range(first, min(first + FF2_HALF, FF2_C))
            for c in part:
                feature("mlp_w1_2", i, c * P)
            for c in part:
                rows("mlp_w2_2", i, c)
        for k in range(KC):
            rows("ple_w_gate_2", i, k)
        for k in range(2):
            rows("ple_w_proj_2", i, k)
    return u


C_ID, C_INC, C_STRICT, C_SAME, C_IND0, C_IND1, C_MEAN, C_LVL, C_SYM, N_CONST = 0, 1, 2, 3, 4, 5, 6, 7, 13, 19


def constants():
    s, c = np.arange(P)[:, None], np.arange(P)[None, :]
    same = (s // CH) == (c // CH)
    mats = [s == c, same & (s <= c), same & (s < c), same, (s < CH) & (c >= 0), (s >= CH) & (c >= 0)]
    out = [m.astype(np.float32) for m in mats] + [np.full((P, P), 1.0 / D, np.float32)]
    lower = [((s // (2 * b)) == (c // (2 * b))) & (s % (2 * b) < b) & (c % (2 * b) >= b) for b in LEVELS]
    out += [m.astype(np.float32) for m in lower]
    out += [(m | m.T).astype(np.float32) for m in lower]
    return np.ascontiguousarray(np.stack(out, 1))


def attention_mask():
    q, k = np.arange(SEQ)[:, None] // CH, np.arange(SEQ)[None, :] // CH
    m = np.where(k <= q, 0.0, -1e30).astype(np.float32)
    return np.ascontiguousarray(m.reshape(NT, P, SEQ).transpose(1, 0, 2))


def stage_list():
    s, prev = [], "x_in"
    r = 0
    for i in range(L1):
        for part in ("ffn1", "mix", "ffn2"):
            tag = f"{part}.{i}"
            s.append(("norm", tag, prev, (part, i)))
            if part == "mix":
                s += [("qkv", tag, i), ("project", tag + ".z", 4), ("project16", tag), ("project", tag + ".ga", 0),
                      ("project", tag + ".gb", 4), ("glu", tag, i), ("conv31", tag, i),
                      ("project", tag + ".cnv", 4), ("cnv_end", tag, r), ("delta", tag, i),
                      ("turn", tag + ".y", None), ("project", tag + ".gdn", 4), ("blend", tag),
                      ("turn", tag + ".o", None), ("project", tag + ".out", 4), ("post", tag, r + 1, 1.0)]
                r += 2
            else:
                s += [("ffn", tag, FF1_C, FF1_HALF, True), ("post", tag, r, 0.5)]
                r += 1
            prev = tag
    for i, kind in enumerate(KINDS):
        tag = f"{kind}.{i}"
        s += [("turn_x", tag, prev), (kind, tag, i // 3), ("project", tag + ".out", 4), ("ln", tag, r),
              ("turn_x", f"mlp.{i}", tag), ("ffn", f"mlp.{i}", FF2_C, FF2_HALF, False), ("ln", f"mlp.{i}", r + 1),
              ("turn_x", f"ple.{i}", f"mlp.{i}"), ("project", f"ple.{i}.g", 4), ("ple", f"ple.{i}", i)]
        prev, r = f"ple.{i}", r + 2
    return s


class Signals:

    def __init__(self, nc, ctx, plan):
        self.nc, self.ctx, self.plan = nc, ctx, plan
        self.sems, self.count, self.at = {}, {}, {}

    def sem(self, name):
        if name not in self.sems:
            self.sems[name] = self.ctx.enter_context(self.nc.semaphore(name))
            self.count[name] = 0
        return self.sems[name]

    def up(self, name, *keys, by=1):
        sem = self.sem(name)
        self.count[name] += by
        for key in keys:
            self.at[name, key] = self.count[name]
        return sem, by

    def reached(self, name, key):
        return self.sem(name), self.plan[name, key] if self.plan else 1


def emit(nc, io, plan, last=None):
    UNITS = unit_list()
    STAGES = stage_list()[:last]
    NU = plan["units"] if plan else len(UNITS)
    COLS, ROWS = column_layout(), row_layout()
    ctx = ExitStack()
    with ctx:
        sg = Signals(nc, ctx, plan)
        up, when = sg.up, sg.reached

        def sb(name, shape, dt=F32, stack=ctx):
            return stack.enter_context(nc.sbuf_tensor(name, shape, dt))

        w_raw = sb("w_raw", [P, NS, UW])
        w_hi = sb("w_hi_part", [P, NS, UW], F32R)
        w_lo = sb("w_lo_part", [P, NS, UW], F32R)
        x = sb("x_res", [P, NT, D])
        xn = sb("xn", [P, NT, D])
        h_hi = sb("h_hi_part", [P, KC, SEQ], F32R)
        h_lo = sb("h_lo_part", [P, KC, SEQ], F32R)
        const = sb("const", [P, N_CONST, P])
        cols = sb("cols", [P, COLS.n])
        row = sb("row", [P, 2, 2, D])
        neghalf = sb("neghalf", [P, SEQ])
        st = sb("stats", [P, 4, 32])
        ident = const[:, C_ID, :]

        ff = ExitStack()
        hid_hi = sb("hid_hi_part", [P, FF2_HALF, SEQ], F32R, ff)
        hid_lo = sb("hid_lo_part", [P, FF2_HALF, SEQ], F32R, ff)
        act_out = sb("act_out", [P, 2, SEQ], F32, ff)
        hid = sb("hid", [P, 2, SEQ], F32, ff)
        ple_g = sb("ple_g", [P, NT, D], F32, ff)
        ple_p = sb("ple_p", [P, 2, SEQ], F32, ff)
        ple_hi = sb("ple_hi_part", [P, 2, SEQ], F32R, ff)
        ple_lo = sb("ple_lo_part", [P, 2, SEQ], F32R, ff)
        ff.close()

        m1 = ExitStack()
        qkvT = sb("qkvT", [P, 24, SEQ], F32, m1)
        zs = sb("zs", [P, NT, D], F32, m1)
        ga = sb("ga", [P, NT, D], F32, m1)
        gb = sb("gb", [P, NT, D], F32, m1)
        small = sb("small", [P, 24, 16], F32, m1)
        gate = sb("gdn_gate", [P, 12, 40], F32, m1)
        gnw = sb("gdn_norm", [P, 1, GDK], F32, m1)
        cv = ExitStack()
        pre = sb("conv_pre", [P, 2, CONV1 - 1 + SEQ], F32, cv)
        cacc = sb("conv_acc", [P, 2, SEQ], F32, cv)
        glu = sb("glu", [P, KC, CONVB - 1 + SEQ], F32, cv)
        hc = sb("hc", [P, KC, SEQ], F32, cv)
        hsq = sb("hsq", [P, KC, SEQ], F32, cv)
        sig = sb("sig", [P, 2, SEQ], F32, cv)
        lnr = sb("lnr", [P, SEQ], F32, cv)
        cv.close()
        W = [sb(f"gdn_w{n}", [P, GH, GDK], F32, m1) for n in range(8)]
        rhs = sb("gdn_rhs", [P, GH, 2 * GDK], F32, m1)
        state = sb("gdn_state", [P, GH, GDK], F32, m1)
        m1.close()

        m2 = ExitStack()
        lqT = sb("lqT", [P, LH, SEQ], F32, m2)
        lkT = sb("lkT", [P, LH, SEQ], F32, m2)
        lv = sb("lv", [P, NT, D], F32, m2)
        lr = sb("lr", [P, NT, D], F32, m2)
        lg = sb("lg", [P, NT, 16], F32, m2)
        lgT = sb("lgT", [17, SEQ], F32, m2)
        wgu = sb("wgu", [17, 512], F32, m2)
        la = sb("la", [P, NT, 512], F32, m2)
        lb_ = sb("lb", [P, NT, 512], F32, m2)
        LT = sb("LT", [P, LH, SEQ], F32, m2)
        ld = sb("ld", [P, LH, SEQ], F32, m2)
        lqe = sb("lqe", [P, LH, SEQ], F32, m2)
        lke = sb("lke", [P, LH, SEQ], F32, m2)
        lsc = sb("lsc", [P, NT, LH, P], F32, m2)
        lkd = sb("lkd", [P, NT, LH, P], F32, m2)
        lst = sb("lst", [P, LH, LDV], F32, m2)
        lend = sb("lend", [P, LH, 4], F32, m2)
        gln = sb("gla_norm", [P, 1, LDV], F32, m2)
        m2.close()

        m3 = ExitStack()
        mc = sb("mc", [P, NT, 512], F32, m3)
        mkr = sb("mkr", [P, NT, 2 * MR], F32, m3)
        mkrT = sb("mkrT", [P, SEQ], F32, m3)
        mcn = sb("mcn", [P, NT, 512], F32, m3)
        mqnT = sb("mqnT", [P, MH, SEQ], F32, m3)
        mknT = sb("mknT", [P, MH, SEQ], F32, m3)
        mqr = sb("mqr", [P, NT, 512], F32, m3)
        mqr2 = sb("mqr2", [P, NT, 512], F32, m3)
        mqrT = sb("mqrT", [P, 4, SEQ], F32, m3)
        mv = sb("mv", [P, NT, D], F32, m3)
        msc = sb("msc", [P, MH, SEQ], F32, m3)
        mpT = sb("mpT", [P, MH, NT, P], F32, m3)
        mask = sb("mask", [P, NT, SEQ], F32, m3)
        rope = sb("rope", [P, NT, 8, 32], F32, m3)
        invf = sb("invf", [P, 32], F32, m3)
        posi = sb("posi", [P, NT], I32, m3)
        posf = sb("posf", [P, NT], F32, m3)
        mst = sb("mst", [P, 4, MH], F32, m3)
        m3.close()

        m4 = ExitStack()
        cpad = sb("cpad", [P, KC, 2 + SEQ], F32, m4)
        cz = sb("cz", [P, KC, SEQ], F32, m4)
        ctmp = sb("ctmp", [P, 2, SEQ], F32, m4)
        m4.close()

        ps = ctx.enter_context(nc.psum_tensor("ps", [P, 8, BANK], F32))

        def acc(bank, t):
            return ps[:, bank + 2 * t:bank + 2 * t + 2, :].rearrange("p a b -> p (a b)")

        def pair(bank):
            return ps[:, bank:bank + 2, :].rearrange("p a (b c) -> p (a b) c", c=P)

        w_in = [sg.sem(f"w_in{n}") for n in range(NS)]

        def col(key, n):
            at = COLS.at[key] + n
            return cols[:, at:at + 1]

        def wide(ap, n):
            return ap.rearrange("p (a b) -> p a b", b=1).to_broadcast([P, ap.shape[1], n])

        def slot_of(h):
            return (h % 2) * (MH // 2) + h // 2

        def over(ap, n):
            return ap.rearrange("p (a b) -> p a b", a=1).to_broadcast([P, n, ap.shape[1]])

        block = ctx.enter_context(nc.Block())

        @block.sync
        def _(sp):
            sp.dma_start(x[:, :, :], io["x"]).then_inc(sg.sem("x_in"), 16)
            sp.dma_start(const[:, :, :], io["const"]).then_inc(sg.sem("const_in"), 16)
            sp.dma_start(cols[:, :], io["cols"]).then_inc(sg.sem("cols_in"), 16)
            for s in range(NS):
                sp.dma_start(w_raw[:, s, :], io["weights"][s]).then_inc(w_in[s], 16)
            rounds = NU // NS
            with sp.Fori(1, rounds) as r:
                for s in range(NS):
                    sp.wait_ge(sg.sem("w_lo"), r * NS + (s + 1 - NS))
                    sp.dma_start(w_raw[:, s, :], io["weights"][r * NS + s]).then_inc(w_in[s], 16)
            for n in range(rounds * NS, NU):
                sp.wait_ge(sg.sem("w_lo"), n + 1 - NS)
                sp.dma_start(w_raw[:, n % NS, :], io["weights"][n]).then_inc(w_in[n % NS], 16)
            for t in range(NT):
                sp.wait_ge(*when("x_new", ("end", t)))
                sp.dma_start(io["out"][:, t], x[:, t, :]).then_inc(sg.sem("stored"), 16)
            sp.wait_ge(sg.sem("stored"), 16 * NT)

        @block.tensor
        def _(pe):
            used = [0]

            def mm(out, lhsT, rhs_, start=True, stop=True):
                return nc.tensor.matmul(out, lhsT, rhs_, start=start, stop=stop, skip_group_check=True)

            def next_unit():
                u = used[0]
                used[0] += 1
                pe.wait_ge(sg.sem("w_lo"), u + 1)
                return u % NS

            def feature_chunk(s, out, hi, lo, k_n, first=0, ready=None):
                for k in range(k_n):
                    if ready:
                        pe.wait_ge(*when("h_lo", (ready, k | 1)))
                    b = slice((first + k) * P, (first + k + 1) * P)
                    mm(out, w_hi[:, s, b], hi[:, k, :], k == 0, False)
                    mm(out, w_hi[:, s, b], lo[:, k, :], False, False)
                    last_ = mm(out, w_lo[:, s, b], hi[:, k, :], False, k == k_n - 1)
                return last_

            def row_chunk(s, outs, hi, lo, first, start, stop_, width=BANK, n_out=2):
                for t in range(NT):
                    tok = slice(t * P, (t + 1) * P)
                    for n in range(n_out):
                        c = slice(first + n * width, first + (n + 1) * width)
                        mm(outs(t, n), hi[:, tok], w_hi[:, s, c], start, False)
                        mm(outs(t, n), hi[:, tok], w_lo[:, s, c], False, False)
                        last_ = mm(outs(t, n), lo[:, tok], w_hi[:, s, c], False, stop_)
                return last_

            def project(tag, bank, source=None, ready=None, more=None):
                if more:
                    pe.wait_ge(*when(*more))
                for k in range(KC):
                    if ready:
                        pe.wait_ge(*when("h_lo", (ready, k | 1)))
                    s = next_unit()
                    last_ = row_chunk(s, lambda t, n: ps[:, bank + 2 * t + n, :], h_hi[:, k, :], h_lo[:, k, :],
                                      0, k == 0, k == KC - 1)
                    last_.then_inc(*up("w_used", *([("product", tag)] if k == KC - 1 else [])))

            def turn(tag, src, ready):
                for t in range(NT):
                    pe.wait_ge(*when(ready[0], (ready[1], t)))
                    for c in range(KC):
                        at = (c % 2) * SEQ + t * P
                        last_ = nc.tensor.transpose(ps[:, c // 2, at:at + P], src[:, t, c * P:(c + 1) * P], ident)
                        if t == NT - 1:
                            last_.then_inc(*up("turned", (tag, c)))

            def norm(tag, prev, key):
                turn(tag, xn, ("xn", tag))

            def turn_x(tag, prev):
                if prev.startswith("ple"):
                    pe.wait_ge(*when("x_new", (prev, 1)))
                turn(tag, x, ("x_new", prev))

            def turn_y(tag, key):
                turn(tag, xn, ("y", tag))

            def ffn(tag, n, half, gated):
                chunk = 0
                for first in range(0, n, half):
                    part = range(first, min(first + half, n))
                    for c in part:
                        if chunk >= 4:
                            pe.wait_ge(*when("hid_gated" if gated else "relu", (tag, chunk - 4)))
                        s = next_unit()
                        last_ = feature_chunk(s, ps[:, chunk % 4, 0:SEQ], h_hi, h_lo, KC,
                                              ready=tag if chunk == 0 else None)
                        if gated:
                            last_.then_inc(*up("w_used"))
                            s = next_unit()
                            last_ = feature_chunk(s, ps[:, chunk % 4, SEQ:2 * SEQ], h_hi, h_lo, KC)
                        last_.then_inc(*up("w_used", ("up", tag, chunk)))
                        chunk += 1
                    for j, c in enumerate(part):
                        pe.wait_ge(*when("hid_lo", (tag, c)))
                        s = next_unit()
                        last_ = row_chunk(s, lambda t, m: ps[:, 4 + 2 * t + m, :], hid_hi[:, j, :], hid_lo[:, j, :],
                                          0, c == 0, c == n - 1)
                        last_.then_inc(*up("w_used", *([("product", tag)] if c == n - 1 else [])))

            def post(tag, r, factor):
                pass

            def ln(tag, r):
                pass

            def qkv(tag, i):
                for c in range(24):
                    if c >= 4:
                        pe.wait_ge(*when("pre", (tag, c - 4)))
                    s = next_unit()
                    last_ = feature_chunk(s, ps[:, c % 4, 0:SEQ], h_hi, h_lo, KC, ready=tag if c == 0 else None)
                    last_.then_inc(*up("w_used", ("qkv", tag, c)))

            def project16(tag):
                if tag.startswith("mix"):
                    pe.wait_ge(*when("pre", (tag, 23)))
                s = next_unit()
                for t in range(NT):
                    for k in range(KC):
                        tok, c = slice(t * P, (t + 1) * P), slice(k * 16, (k + 1) * 16)
                        out = ps[:, t, 0:16]
                        mm(out, h_hi[:, k, tok], w_hi[:, s, c], k == 0, False)
                        mm(out, h_hi[:, k, tok], w_lo[:, s, c], False, False)
                        last_ = mm(out, h_lo[:, k, tok], w_hi[:, s, c], False, k == KC - 1)
                last_.then_inc(*up("w_used", ("small", tag)))

            def glu_(tag, i):
                for c in range(KC):
                    if c == 0:
                        pe.wait_ge(*when("evacuated", (tag + ".ga", 1)))
                    if c >= 4:
                        pe.wait_ge(*when("glu", (tag, c - 4)))
                    s = next_unit()
                    feature_chunk(s, ps[:, c % 4, 0:SEQ], h_hi, h_lo, KC).then_inc(*up("w_used"))
                    s = next_unit()
                    last_ = feature_chunk(s, ps[:, c % 4, SEQ:2 * SEQ], h_hi, h_lo, KC)
                    last_.then_inc(*up("w_used", ("glu", tag, c)))

            def conv31(tag, i):
                for c in range(KC):
                    pe.wait_ge(*when("conv", (tag, c)))
                    last_ = mm(ps[:, 0, 0:SEQ], const[:, C_MEAN, :], hc[:, c, :], c == 0, c == KC - 1)
                last_.then_inc(*up("ln_mean", tag))
                pe.wait_ge(*when("ln_square", tag))
                for c in range(KC):
                    last_ = mm(ps[:, 1, 0:SEQ], const[:, C_MEAN, :], hsq[:, c, :], c == 0, c == KC - 1)
                last_.then_inc(*up("ln_var", tag))

            def cnv_end(tag, r):
                pass

            def blend(tag):
                pass

            def heads(bank, f, n=GH):
                for h in range(n):
                    last_ = f(pair(bank)[:, h, :], h)
                return last_

            def delta(tag, i):
                for t in range(NT):
                    tok = slice(t * P, (t + 1) * P)
                    key = (tag, t)
                    tr = nc.tensor.transpose
                    if t == 0:
                        pe.wait_ge(*when("silu_qkv", (tag, 23)))
                        pe.wait_ge(*when("cnv_y", (tag, 1)))
                        pe.wait_ge(*when("decays", tag))
                    else:
                        pe.wait_ge(*when("state", (tag, 1)))
                    for n in range(3):
                        heads(2 * n, lambda o, h: tr(o, qkvT[:, n * GH + h, tok], ident)).then_inc(*up("turned", ("tm", key, n)))
                    if t == 1:
                        pe.wait_ge(*when("y_raw", (tag, 0)))
                    g = gate[:, 2 * t + 1, 0:GH]
                    for n, m in enumerate((C_INC, C_SAME, C_IND0, C_IND1)):
                        last_ = mm(ps[:, 6, n * GH:(n + 1) * GH], const[:, m, :], g)
                    last_.then_inc(*up("sums", key))
                    pe.wait_ge(*when("sums_out", key))
                    heads(6, lambda o, h: mm(o, g[:, h:h + 1].to_broadcast([P, P]), const[:, C_INC, :])).then_inc(*up("grow", key))
                    for n, (w, name) in enumerate(((0, "qn"), (1, "kn"), (4, "kb"), (5, "qd"))):
                        pe.wait_ge(*when(name, key))
                        if n == 2:
                            pe.wait_ge(*when("vb", key))
                        if n == 3:
                            pe.wait_ge(*when("dif", key))
                        heads(2 * n, lambda o, h: tr(o, W[w][:, h, :], ident)).then_inc(*up("turned", ("hm", key, n)))
                    pe.wait_ge(*when("hm", (key, 2)))
                    heads(0, lambda o, h: mm(o, W[1][:, h, :], W[4][:, h, :])).then_inc(*up("kk", key))
                    heads(2, lambda o, h: mm(o, W[1][:, h, :], W[0][:, h, :])).then_inc(*up("qk", key))
                    for n in range(len(LEVELS)):
                        pe.wait_ge(*when("level_m", (key, n)))
                        if n == 0:
                            pe.wait_ge(*when("qk_out", key))
                            pe.wait_ge(*when("hm", (key, 3)))
                        else:
                            pe.wait_ge(*when("tt", (key, n - 1)))
                        heads(0, lambda o, h: mm(o, W[4][:, h, :], W[0][:, h, :])).then_inc(*up("mt", (key, n)))
                        pe.wait_ge(*when("x_out", (key, n)))
                        if n < len(LEVELS) - 1:
                            heads(2, lambda o, h: mm(o, W[1][:, h, :], W[6][:, h, :])).then_inc(*up("tmt", (key, n)))
                        heads(4, lambda o, h: mm(o, W[6][:, h, :], W[1][:, h, :])).then_inc(*up("tmtT", (key, n)))
                    pe.wait_ge(*when("tt", (key, len(LEVELS) - 1)))
                    heads(0, lambda o, h: mm(o, W[1][:, h, :], rhs[:, h, 0:GDK])).then_inc(*up("u", key))
                    heads(2, lambda o, h: mm(o, rhs[:, h, GDK:2 * GDK], W[1][:, h, :])).then_inc(*up("wT", key))
                    for j in range(2):
                        ci = 2 * t + j
                        r = slice(j * CH, (j + 1) * CH)
                        if ci > 0:
                            pe.wait_ge(*when("wT_out", key))
                            pe.wait_ge(*when("state", (tag, ci - 1)))
                            for h in range(GH):
                                last_ = mm(pair(4)[r, h, :], W[4][:, h, r], state[:, h, :])
                            last_.then_inc(*up("ws", (tag, ci)))
                        pe.wait_ge(*when("v_new", (tag, ci)))
                        if ci < 3:
                            for h in range(GH):
                                last_ = mm(pair(0)[:, h, :], W[7][r, h, :], W[6][r, h, :])
                            last_.then_inc(*up("kv", (tag, ci)))
                        for h in range(GH):
                            o = pair(6)[r, h, :]
                            if ci > 0:
                                mm(o, W[5][:, h, r], state[:, h, :], True, False)
                            last_ = mm(o, W[2][r, h, r], W[6][r, h, :], ci == 0, True)
                        last_.then_inc(*up("o", (tag, ci)))

            def gla(tag, j):
                for c in range(8):
                    if c >= 4:
                        pe.wait_ge(*when("lqk", (tag, c - 4)))
                    s = next_unit()
                    last_ = feature_chunk(s, ps[:, c % 4, 0:SEQ], h_hi, h_lo, KC, ready=tag if c == 0 else None)
                    last_.then_inc(*up("w_used", ("lqk", tag, c)))
                project(tag + ".v", 4)
                project(tag + ".r", 0, more=("lqk", (tag, 7)))
                pe.wait_ge(*when("evacuated", (tag + ".r", 1)))
                project16(tag)
                pe.wait_ge(*when("lg", tag))
                for t in range(NT):
                    last_ = mm(ps[0:16, 2, t * P:(t + 1) * P], lg[:, t, :], ident)
                last_.then_inc(*up("lgT", tag))
                pe.wait_ge(*when("lgT_out", tag))
                pe.wait_ge(*when("wgu_in", tag))
                for t in range(NT):
                    last_ = mm(ps[:, t, :], lgT[:, t * P:(t + 1) * P], wgu[:, :])
                last_.then_inc(*up("lgate", tag))
                pe.wait_ge(*when("la", tag))
                for h in range(LH):
                    for t in range(NT):
                        last_ = mm(ps[:, 2 + h // 2, (h % 2) * SEQ + t * P:(h % 2) * SEQ + (t + 1) * P],
                                   la[:, t, h * P:(h + 1) * P], const[:, C_INC, :])
                last_.then_inc(*up("lsum", tag))
                for n in range(1 + len(LEVELS)):
                    if n >= 1:
                        pe.wait_ge(*when("lke", (tag, n)))
                    for t in range(NT):
                        if n >= 1:
                            pe.wait_ge(*when("lscore", (tag, n - 1, t)))
                        for h in range(LH):
                            tok = slice(t * P, (t + 1) * P)
                            a, b = (lkT, lqT) if n == 0 else (lke, lqe)
                            last_ = mm(ps[:, t, h * P:(h + 1) * P], a[:, h, tok], b[:, h, tok])
                        last_.then_inc(*up("lsq", (tag, n, t)))
                pe.wait_ge(*when("lkd", tag))
                for t in range(NT):
                    for h in range(LH):
                        last_ = nc.tensor.transpose(ps[:, 2 + t, h * P:(h + 1) * P], lke[:, h, t * P:(t + 1) * P], ident)
                    last_.then_inc(*up("lkdT", (tag, t)))
                for ci in range(4):
                    t, r = ci // 2, slice((ci % 2) * CH, (ci % 2 + 1) * CH)
                    if ci == 0:
                        pe.wait_ge(*when("evacuated", (tag + ".v", 1)))
                        pe.wait_ge(*when("lscore", (tag, len(LEVELS), 1)))
                    pe.wait_ge(*when("lkd_out", (tag, t)))
                    if ci >= 1:
                        pe.wait_ge(*when("lst", (tag, ci - 1)))
                    if ci < 3:
                        for h in range(LH):
                            last_ = mm(ps[:, h // 2, (h % 2) * LDV:(h % 2 + 1) * LDV], lkd[r, t, h, :],
                                       lv[r, t, h * LDV:(h + 1) * LDV])
                        last_.then_inc(*up("lkv", (tag, ci)))
                    for h in range(LH):
                        o = ps[r, 4 + 2 * t + h // 2, (h % 2) * LDV:(h % 2 + 1) * LDV]
                        if ci > 0:
                            mm(o, lqe[:, h, ci * CH:(ci + 1) * CH], lst[:, h, :], True, False)
                        last_ = mm(o, lsc[r, t, h, r], lv[r, t, h * LDV:(h + 1) * LDV], ci == 0, True)
                    last_.then_inc(*up("lo", (tag, ci)))
                turn(tag + ".y", xn, ("y", tag + ".y"))

            def mla(tag, j):
                for k in range(0, KC, 2):
                    s = next_unit()
                    for kk in range(2):
                        pe.wait_ge(*when("h_lo", (tag, k + kk)))
                        last_ = row_chunk(s, lambda t, n: ps[:, 4 + t, :], h_hi[:, k + kk, :], h_lo[:, k + kk, :],
                                          kk * 512, k + kk == 0, k + kk == KC - 1, 512, 1)
                    last_.then_inc(*up("w_used", *([("mc", tag)] if k == KC - 2 else [])))
                s = next_unit()
                for t in range(NT):
                    for k in range(KC):
                        tok, c = slice(t * P, (t + 1) * P), slice(k * MR, (k + 1) * MR)
                        out = ps[:, 6, t * MR:(t + 1) * MR]
                        mm(out, h_hi[:, k, tok], w_hi[:, s, c], k == 0, False)
                        mm(out, h_hi[:, k, tok], w_lo[:, s, c], False, False)
                        last_ = mm(out, h_lo[:, k, tok], w_hi[:, s, c], False, k == KC - 1)
                last_.then_inc(*up("w_used", ("mkr", tag)))
                for t in range(NT):
                    pe.wait_ge(*when("mcn", (tag, t)))
                    for c in range(4):
                        at = (c % 2) * SEQ + t * P
                        last_ = nc.tensor.transpose(ps[:, c // 2, at:at + P], mcn[:, t, c * P:(c + 1) * P], ident)
                        if t == NT - 1:
                            last_.then_inc(*up("turned", (tag + ".c", c)))
                for n, first in ((0, 0), (1, 2)):
                    for c0 in range(0, MH, 4):
                        s = next_unit()
                        for c in range(c0, c0 + 4):
                            if n == 0 and c < 4:
                                pe.wait_ge(*when("h_lo", (tag + ".c", 3)))
                            g = n * MH + c
                            if g >= 4:
                                pe.wait_ge(*when("mT", (tag, g - 4)))
                            last_ = feature_chunk(s, ps[:, g % 4, 0:SEQ], h_hi[:, first:first + 2], h_lo[:, first:first + 2],
                                                  2, (c - c0) * 2)
                        last_.then_inc(*up("w_used", *[("mT", tag, n * MH + c) for c in range(c0, c0 + 4)]))
                    if n == 0:
                        s = next_unit()
                        pe.wait_ge(*when("mc_out", (tag, 1)))
                        for k in range(2):
                            last_ = row_chunk(s, lambda t, m: ps[:, 4 + t, :], h_hi[:, k, :], h_lo[:, k, :],
                                              k * 512, k == 0, k == 1, 512, 1)
                        last_.then_inc(*up("w_used", ("mqr", tag)))
                pe.wait_ge(*when("mqr_out", (tag, 1)))
                pe.wait_ge(*when("mkr_out", tag))
                for k in range(2):
                    s = next_unit()
                    last_ = row_chunk(s, lambda t, n: ps[:, 4 + 2 * t + n, :], h_hi[:, 2 + k, :], h_lo[:, 2 + k, :],
                                      0, k == 0, k == 1)
                    last_.then_inc(*up("w_used", *([("product", tag + ".v")] if k == 1 else [])))
                pe.wait_ge(*when("mT", (tag, 2 * MH - 1)))
                pe.wait_ge(*when("roped", tag))
                for t in range(NT):
                    for c in range(4):
                        nc.tensor.transpose(ps[:, c // 2, (c % 2) * SEQ + t * P:(c % 2) * SEQ + (t + 1) * P],
                                            mqr2[:, t, c * P:(c + 1) * P], ident)
                    last_ = nc.tensor.transpose(ps[:, 2, t * P:(t + 1) * P], mkr[:, t, :], ident)
                last_.then_inc(*up("turned", (tag + ".r", 0)))
                pe.wait_ge(*when("rT_out", tag))
                pe.wait_ge(*when("evacuated", (tag + ".v", 1)))
                for t in range(NT):
                    tok = slice(t * P, (t + 1) * P)
                    if t == 1:
                        pe.wait_ge(*when("msm", (tag, 0)))
                    for h in range(MH):
                        p = slot_of(h)
                        o = ps[:, p // 2, (p % 2) * SEQ:(p % 2 + 1) * SEQ]
                        b = (h % 2) * MR
                        mm(o, mqnT[:, h, tok], mknT[:, h, :], True, False)
                        last_ = mm(o, mqrT[b:b + MR, h // 2, tok], mkrT[b:b + MR, :], False, True)
                    last_.then_inc(*up("mscore", (tag, t)))
                    pe.wait_ge(*when("mexp", (tag, t)))
                    nk = NT
                    for h in range(MH):
                        for k in range(nk):
                            at = (h % 2) * SEQ + k * P
                            last_ = nc.tensor.transpose(ps[:, 4 + h // 2, at:at + P], msc[:, h, k * P:(k + 1) * P], ident)
                    last_.then_inc(*up("mpT", (tag, t)))
                    pe.wait_ge(*when("mpT_out", (tag, t)))
                    for h in range(MH):
                        for k in range(nk):
                            last_ = mm(pair(0)[:, slot_of(h), :], mpT[:, slot_of(h), k, :],
                                       mv[:, k, h * P:(h + 1) * P], k == 0, k == nk - 1)
                    last_.then_inc(*up("mo", (tag, t)))
                    pe.wait_ge(*when("y", (tag + ".y", t)))
                turn(tag + ".y", xn, ("y", tag + ".y"))

            def conv(tag, j):
                for c in range(KC):
                    if c >= 4:
                        pe.wait_ge(*when("cu", (tag, c - 4)))
                    s = next_unit()
                    feature_chunk(s, ps[:, c % 4, 0:SEQ], h_hi, h_lo, KC, ready=tag if c == 0 else None).then_inc(*up("w_used"))
                    s = next_unit()
                    feature_chunk(s, ps[:, c % 4, SEQ:2 * SEQ], h_hi, h_lo, KC).then_inc(*up("w_used", ("cu", tag, c)))
                for c in range(KC):
                    if c < 4:
                        pe.wait_ge(*when("cu", (tag, c + 4)))
                    else:
                        pe.wait_ge(*when("cbz", (tag, c - 4)))
                    s = next_unit()
                    feature_chunk(s, ps[:, c % 4, 0:SEQ], h_hi, h_lo, KC).then_inc(*up("w_used", ("cb", tag, c)))

            def ple(tag, i):
                pe.wait_ge(*when("ple_lo", tag))
                for k in range(2):
                    s = next_unit()
                    last_ = row_chunk(s, lambda t, n: ps[:, 2 * t + n, :], ple_hi[:, k, :], ple_lo[:, k, :],
                                      0, k == 0, k == 1)
                    last_.then_inc(*up("w_used", *([("product", tag)] if k == 1 else [])))

            def project_(tag, bank):
                main = tag.rsplit(".", 1)[0]
                ready = {"out": main + (".o" if main.startswith("mix") else ".y"), "cnv": main + ".c",
                         "gdn": main + ".y", "g": main}.get(tag.rsplit(".", 1)[1])
                more = {"ga": ("small", main), "gb": ("evacuated", (main + ".z", 1)),
                        "cnv": ("evacuated", (main + ".gb", 1))}.get(tag.rsplit(".", 1)[1])
                project(tag, bank, ready=ready, more=more)

            pe.wait_ge(sg.sem("const_in"), 16)
            table = dict(norm=norm, turn_x=turn_x, turn=turn_y, ffn=ffn, post=post, ln=ln, qkv=qkv, project=project_,
                         project16=project16, glu=glu_, conv31=conv31, cnv_end=cnv_end, delta=delta, blend=blend,
                         gla=gla, mla=mla, conv=conv, ple=ple)
            for name, *args in STAGES:
                table[name](*args)
            sg.at["units"] = used[0]

        @block.scalar
        def _(act):
            made, pos = [0], [0]
            A = nc.scalar.activation

            def weights(n):
                pos[0] += n
                while made[0] < min(pos[0] + NS, NU):
                    u, s = made[0], made[0] % NS
                    made[0] += 1
                    wd = unit_width(UNITS[u])
                    act.wait_ge(w_in[s], 16 * (u // NS + 1))
                    if u >= NS:
                        act.wait_ge(sg.sem("w_used"), u - NS + 1)
                    A(w_hi[:, s, 0:wd], w_raw[:, s, 0:wd], ACT.Copy).then_inc(*up("w_hi", u))

            def take(tag, scale=None, n=KC):
                for c in range(n):
                    act.wait_ge(*when("turned", (tag, c | 1)))
                    src = ps[:, c // 2, (c % 2) * SEQ:(c % 2 + 1) * SEQ]
                    sc = 1.0 if scale is None else scale(c)
                    A(h_hi[:, c, :], src, ACT.Copy, scale=sc).then_inc(*up("h_hi", (tag, c)))

            def turn(tag, key=None):
                take(tag)

            def squares(tag, src, out):
                for t in range(NT):
                    A(out(t), src(t), ACT.Square, accum_out=st[:, 0, t:t + 1]).then_inc(*up("sumsq", (tag, t)))

            def norm(tag, prev, key):
                for t in range(NT):
                    act.wait_ge(*when("x_new", (prev, t)))
                    A(xn[:, t, :], x[:, t, :], ACT.Square, accum_out=st[:, 0, t:t + 1]).then_inc(*up("sumsq", (tag, t)))
                take(tag, lambda c: col(key, c))

            def turn_x(tag, prev):
                take(tag)
                if tag.startswith("ple"):
                    act.wait_ge(*when("ple_in", tag))
                    A(ple_hi[:, :, :], ple_p[:, :, :], ACT.Copy).then_inc(*up("ple_hi", tag))

            def ffn(tag, n, half, gated):
                chunk = 0
                for first in range(0, n, half):
                    part = range(first, min(first + half, n))
                    for c in part:
                        act.wait_ge(*when("w_used", ("up", tag, chunk)))
                        s = chunk % 2
                        if chunk >= 2:
                            act.wait_ge(*when("hid_gated" if gated else "hid_lo", (tag, chunk - 2)))
                        if gated:
                            A(act_out[:, s, :], ps[:, chunk % 4, 0:SEQ], ACT.Silu).then_inc(*up("silu", (tag, chunk)))
                        else:
                            A(act_out[:, s, :], ps[:, chunk % 4, 0:SEQ], ACT.Relu).then_inc(*up("relu", (tag, chunk)))
                        weights(2 if gated else 1)
                        if not gated:
                            act.wait_ge(*when("relu", (tag, chunk)))
                            A(hid[:, s, :], act_out[:, s, :], ACT.Square).then_inc(*up("hid_square", (tag, chunk)))
                        chunk += 1
                    for c in part:
                        weights(1)

            def post(tag, r, factor):
                name = tag + ".out" if tag.startswith("mix") else tag
                act.wait_ge(*when("w_used", ("product", name)))
                squares(tag + ".p", lambda t: acc(4, t), lambda t: xn[:, t, :])

            def ln(tag, r):
                for t in range(NT):
                    act.wait_ge(*when("centered", (tag, t)))
                    A(x[:, t, :], xn[:, t, :], ACT.Square, accum_out=st[:, 0, t:t + 1]).then_inc(*up("sumsq", (tag, t)))

            def qkv(tag, i):
                for c in range(25):
                    if c < 24:
                        act.wait_ge(*when("w_used", ("qkv", tag, c)))
                        if c >= 2:
                            act.wait_ge(*when("conv4", (tag, c - 2)))
                        src = ps[:, c % 4, 0:SEQ]
                        A(pre[:, c % 2, CONV1 - 1:], src, ACT.Copy).then_inc(*up("pre_in", (tag, c)))
                        if c >= 2:
                            act.wait_ge(*when("silu_qkv", (tag, c - 2)))
                        A(cacc[:, c % 2, :], src, ACT.Copy, scale=col(("convw", i), c * CONV1 + CONV1 - 1)).then_inc(*up("pre", (tag, c)))
                        weights(1)
                    if c >= 1:
                        act.wait_ge(*when("conv4", (tag, c - 1)))
                        A(qkvT[:, c - 1, :], cacc[:, (c - 1) % 2, :], ACT.Silu).then_inc(*up("silu_qkv", (tag, c - 1)))

            def project(tag, bank):
                main, what = tag.rsplit(".", 1)
                for k in range(KC):
                    weights(1)
                out, f = {"z": (zs, ACT.Silu), "ga": (ga, ACT.Sigmoid), "gb": (gb, ACT.Sigmoid),
                          "v": (lv, ACT.Copy), "r": (lr, ACT.Silu), "g": (ple_g, ACT.Sigmoid)}.get(what, (None, None))
                if out is not None:
                    act.wait_ge(*when("w_used", ("product", tag)))
                    for t in range(NT):
                        A(out[:, t, :], acc(bank, t), f).then_inc(*up("evacuated", (tag, t)))

            def project16(tag):
                weights(1)
                if tag.startswith("gla"):
                    act.wait_ge(*when("w_used", ("small", tag)))
                    A(lg[:, :, :], ps[:, 0:2, 0:16], ACT.Copy).then_inc(*up("lg", tag))
                    return
                act.wait_ge(*when("small", tag))
                A(gate[:, 0:3:2, 0:GH], small[:, 0:2, 0:GH], ACT.Sigmoid).then_inc(*up("beta", tag))
                act.wait_ge(*when("a_in", tag))
                A(small[:, 10, 0:GH], gate[:, 5, 0:GH], ACT.Exp).then_inc(*up("a_exp", tag))
                A(small[:, 4:6, 0:GH], small[:, 2:4, 0:GH], ACT.Abs).then_inc(*up("s_step", ("abs", tag)))
                act.wait_ge(*when("s_step", ("abs", tag)))
                A(small[:, 6:8, 0:GH], small[:, 4:6, 0:GH], ACT.Exp, scale=-1.0).then_inc(*up("s_step", ("exp", tag)))
                act.wait_ge(*when("s_step", ("exp", tag)))
                A(small[:, 8:10, 0:GH], small[:, 6:8, 0:GH], ACT.Ln, bias=1.0).then_inc(*up("softplus", tag))

            def glu_(tag, i):
                for c in range(KC):
                    act.wait_ge(*when("w_used", ("glu", tag, c)))
                    if c >= 2:
                        act.wait_ge(*when("glu", (tag, c - 2)))
                    A(sig[:, c % 2, :], ps[:, c % 4, SEQ:2 * SEQ], ACT.Sigmoid, bias=col(("pw1b", i), KC + c)).then_inc(*up("sig", (tag, c)))
                    weights(2)

            def conv31(tag, i):
                act.wait_ge(*when("ln_center", tag))
                A(hsq[:, :, :], hc[:, :, :], ACT.Square).then_inc(*up("ln_square", tag))
                act.wait_ge(*when("ln_norm", tag))
                for c in range(KC):
                    A(hsq[:, c, :], hc[:, c, :], ACT.Silu, bias=col(("lnb", i), c), scale=col(("lng", i), c)).then_inc(*up("cnv_act", (tag, c)))
                for c in range(KC):
                    act.wait_ge(*when("cnv_act", (tag, c)))
                    A(h_hi[:, c, :], hsq[:, c, :], ACT.Copy).then_inc(*up("h_hi", (tag + ".c", c)))

            def nothing(*args):
                pass

            def delta(tag, i):
                for t in range(NT):
                    key = (tag, t)
                    for n, w in enumerate((6, 3)):
                        act.wait_ge(*when("turned", ("tm", key, n)))
                        if t == 1 and n == 0:
                            act.wait_ge(*when("y_raw", (tag, 0)))
                        A(W[w][:, :, :], pair(2 * n), ACT.Square).then_inc(*up("head_square", (key, n)))
                    act.wait_ge(*when("kdiff", key))
                    A(gate[:, 8 + t, :], gate[:, 6 + t, :], ACT.Exp).then_inc(*up("gexp", key))
                    act.wait_ge(*when("dif_min", key))
                    A(W[2][:, :, :], W[2][:, :, :], ACT.Exp).then_inc(*up("dec", key))
                    act.wait_ge(*when("rhs", key))
                    for n, w in enumerate((0, 1, 4, 5)):
                        act.wait_ge(*when("turned", ("hm", key, n)))
                        A(W[w][:, :, :], pair(2 * n), ACT.Copy).then_inc(*up("hm", (key, n)))
                    for n in range(len(LEVELS)):
                        act.wait_ge(*when("mt", (key, n)))
                        A(W[6][:, :, :], pair(0), ACT.Copy).then_inc(*up("x_out", (key, n)))
                    act.wait_ge(*when("u", key))
                    A(W[0][:, :, :], pair(0), ACT.Copy).then_inc(*up("u_out", key))
                    act.wait_ge(*when("wT", key))
                    A(W[4][:, :, :], pair(2), ACT.Copy).then_inc(*up("wT_out", key))
                    act.wait_ge(*when("o", (tag, 2 * t + 1)))
                    A(W[6][:, :, :], pair(6), ACT.Square).then_inc(*up("out_square", key))

            def gla(tag, j):
                for c in range(8):
                    act.wait_ge(*when("w_used", ("lqk", tag, c)))
                    out = lqT[:, c, :] if c < 4 else lkT[:, c - 4, :]
                    A(out, ps[:, c % 4, 0:SEQ], ACT.Copy, scale=NORM_SCALE if c < 4 else 1.0).then_inc(*up("lqk", (tag, c)))
                    weights(1)
                project(tag + ".v", 4)
                project(tag + ".r", 0)
                project16(tag)
                act.wait_ge(*when("lgT", tag))
                act.wait_ge(*when("lgT_one", tag))
                A(lgT[0:16, :], ps[0:16, 2, 0:SEQ], ACT.Copy).then_inc(*up("lgT_out", tag))
                act.wait_ge(*when("lgate", tag))
                A(la[:, :, :], ps[:, 0:2, :], ACT.Abs).then_inc(*up("s_step", ("abs", tag)))
                act.wait_ge(*when("s_step", ("abs", tag)))
                A(la[:, :, :], la[:, :, :], ACT.Exp, scale=-1.0).then_inc(*up("s_step", ("exp", tag)))
                act.wait_ge(*when("s_step", ("exp", tag)))
                A(la[:, :, :], la[:, :, :], ACT.Ln, bias=1.0).then_inc(*up("softplus", tag))
                for n in range(1, 1 + len(LEVELS)):
                    act.wait_ge(*when("ld", (tag, n)))
                    A(ld[:, :, :], ld[:, :, :], ACT.Abs).then_inc(*up("s_step", ("ld", tag, n)))
                    act.wait_ge(*when("s_step", ("ld", tag, n)))
                    A(ld[:, :, :], ld[:, :, :], ACT.Exp, scale=-1.0).then_inc(*up("le", (tag, n)))
                act.wait_ge(*when("lke", (tag, len(LEVELS))))
                A(ld[:, :, :], LT[:, :, :], ACT.Exp).then_inc(*up("le", (tag, "q")))
                A(lend[:, :, :], LT[:, :, CH - 1::CH], ACT.Exp).then_inc(*up("lend", tag))
                act.wait_ge(*when("ld", (tag, "k")))
                A(ld[:, :, :], ld[:, :, :], ACT.Exp).then_inc(*up("le", (tag, "k")))
                for t in range(NT):
                    act.wait_ge(*when("lkdT", (tag, t)))
                    A(lkd[:, t], ps[:, 2 + t, :].rearrange("p (h k) -> p h k", k=P), ACT.Copy).then_inc(*up("lkd_out", (tag, t)))
                for t in range(NT):
                    act.wait_ge(*when("lo", (tag, 2 * t + 1)))
                    A(xn[:, t, :], acc(4, t), ACT.Square).then_inc(*up("out_square", (tag, t)))
                take(tag + ".y")

            def mla(tag, j):
                act.wait_ge(*when("angle", tag))
                for n in range(2):
                    A(rope[:, :, n, :], rope[:, :, n + 2, :], ACT.Sin).then_inc(*up("sine", tag))
                for k in range(0, KC, 2):
                    weights(1)
                act.wait_ge(*when("w_used", ("mc", tag)))
                for t in range(NT):
                    A(mc[:, t, :], ps[:, 4 + t, :], ACT.Copy).then_inc(*up("mc_out", (tag, t)))
                    for n in range(2):
                        A(mcn[:, t, n * 256:(n + 1) * 256], ps[:, 4 + t, n * 256:(n + 1) * 256], ACT.Square, accum_out=st[:, 0, 2 * t + n:2 * t + n + 1]).then_inc(*up("sumsq", (tag + ".c", t)))
                weights(1)
                act.wait_ge(*when("w_used", ("mkr", tag)))
                A(mkr[:, :, MR:], ps[:, 6, 0:P].rearrange("p (t n) -> p t n", t=NT), ACT.Copy).then_inc(*up("mkr_out", tag))
                take(tag + ".c", lambda c: col(("qnorm", 0), c) if c < 2 else col(("kvnorm", 0), c - 2), 4)
                for n in range(2):
                    for c in range(MH):
                        g = n * MH + c
                        act.wait_ge(*when("w_used", ("mT", tag, g)))
                        out = (mqnT if n == 0 else mknT)[:, c, :]
                        A(out, ps[:, g % 4, 0:SEQ], ACT.Copy).then_inc(*up("mT", (tag, g)))
                        if c % 4 == 3:
                            weights(1)
                    if n == 0:
                        weights(1)
                        act.wait_ge(*when("w_used", ("mqr", tag)))
                        for t in range(NT):
                            A(mqr[:, t, :], ps[:, 4 + t, :], ACT.Copy).then_inc(*up("mqr_out", (tag, t)))
                weights(2)
                act.wait_ge(*when("w_used", ("product", tag + ".v")))
                for t in range(NT):
                    A(mv[:, t, :], acc(4, t), ACT.Copy).then_inc(*up("evacuated", (tag + ".v", t)))
                act.wait_ge(*when("turned", (tag + ".r", 0)))
                A(mqrT[:, :, :], acc(0, 0).rearrange("p (c t) -> p c t", t=SEQ), ACT.Copy).then_inc(*up("rT_out", "half"))
                A(mkrT[:, :], ps[:, 2, 0:SEQ], ACT.Copy).then_inc(*up("rT_out", tag))
                for t in range(NT):
                    act.wait_ge(*when("mmax", (tag, t)))
                    for h in range(MH):
                        A(msc[:, h, :], msc[:, h, :], ACT.Exp, scale=MLA_SCALE, bias=mst[:, 1, h:h + 1], accum_out=mst[:, 2, h:h + 1]).then_inc(*up("mexp", (tag, t)))
                    act.wait_ge(*when("mpT", (tag, t)))
                    A(mpT[:, :, :, :], ps[:, 4:8, :].rearrange("p b (h k q) -> p (b h) k q", h=2, k=NT), ACT.Copy).then_inc(*up("mpT_out", (tag, t)))
                take(tag + ".y")

            def conv(tag, j):
                for c in range(KC):
                    act.wait_ge(*when("w_used", ("cu", tag, c)))
                    if c >= 2:
                        act.wait_ge(*when("cu", (tag, c - 2)))
                    A(ctmp[:, c % 2, :], ps[:, c % 4, 0:SEQ], ACT.Copy).then_inc(*up("ctmp", (tag, c)))
                    weights(2)
                for c in range(KC):
                    weights(1)
                act.wait_ge(*when("w_used", ("cb", tag, KC - 1)))
                for c in range(KC):
                    act.wait_ge(*when("cbz", (tag, c)))
                    A(h_hi[:, c, :], cz[:, c, :], ACT.Copy).then_inc(*up("h_hi", (tag + ".y", c)))

            def ple(tag, i):
                weights(2)

            act.wait_ge(sg.sem("cols_in"), 16)
            weights(0)
            table = dict(norm=norm, turn_x=turn_x, turn=turn, ffn=ffn, post=post, ln=ln, qkv=qkv, project=project,
                         project16=project16, glu=glu_, conv31=conv31, cnv_end=nothing, delta=delta, blend=nothing,
                         gla=gla, mla=mla, conv=conv, ple=ple)
            for name, *args in STAGES:
                table[name](*args)
            weights(0)

        @block.vector
        def _(dve):
            made, pos, steps = [0], [0], [0]
            V = nc.vector

            def link(ins):
                steps[0] += 1
                ins.then_inc(*up("v_step", steps[0]))
                dve.wait_ge(sg.sem("v_step"), steps[0])

            def weights(n):
                pos[0] += n
                while made[0] < min(pos[0] + NS, NU):
                    u, s = made[0], made[0] % NS
                    made[0] += 1
                    wd = unit_width(UNITS[u])
                    dve.wait_ge(*when("w_hi", u))
                    V.tensor_tensor(w_lo[:, s, 0:wd], w_raw[:, s, 0:wd], w_hi[:, s, 0:wd].bitcast(F32), ALU.subtract).then_inc(*up("w_lo", u))

            def take(tag, scale=None, n=KC):
                for c in range(n):
                    dve.wait_ge(*when("h_hi", (tag, c | 1)))
                    src = ps[:, c // 2, (c % 2) * SEQ:(c % 2 + 1) * SEQ]
                    hi = h_hi[:, c, :].bitcast(F32)
                    if scale is None:
                        ins = V.tensor_tensor(h_lo[:, c, :], src, hi, ALU.subtract)
                    else:
                        ins = V.scalar_tensor_tensor(h_lo[:, c, :], src, scale(c), hi, ALU.mult, ALU.subtract)
                    ins.then_inc(*up("h_lo", (tag, c)))

            def turn(tag, key=None):
                take(tag)

            def root(tag, n, scale, eps):
                V.tensor_scalar(st[:, 1, 0:n], st[:, 0, 0:n], scale, eps, ALU.mult, ALU.add).then_inc(*up("mean", tag))
                dve.wait_ge(*when("root", tag))

            def norm(tag, prev, key):
                dve.wait_ge(*when("sumsq", (tag, 1)))
                root(tag, NT, 1.0 / D, RMS_EPS)
                for t in range(NT):
                    V.tensor_scalar(xn[:, t, :], x[:, t, :], st[:, 2, t:t + 1], None, ALU.mult).then_inc(*up("xn", (tag, t)))
                take(tag, lambda c: col(key, c))

            def turn_x(tag, prev):
                take(tag)
                if tag.startswith("ple"):
                    dve.wait_ge(*when("ple_hi", tag))
                    V.tensor_tensor(ple_lo[:, :, :], ple_p[:, :, :], ple_hi[:, :, :].bitcast(F32), ALU.subtract).then_inc(*up("ple_lo", tag))

            def ffn(tag, n, half, gated):
                chunk = 0
                for first in range(0, n, half):
                    part = range(first, min(first + half, n))
                    for j, c in enumerate(part):
                        s = chunk % 2
                        if gated:
                            dve.wait_ge(*when("silu", (tag, chunk)))
                            V.tensor_tensor(hid[:, s, :], act_out[:, s, :], ps[:, chunk % 4, SEQ:2 * SEQ], ALU.mult).then_inc(*up("hid_gated", (tag, chunk)))
                        weights(2 if gated else 1)
                        dve.wait_ge(*when("hid_gated" if gated else "hid_square", (tag, chunk)))
                        V.tensor_copy(hid_hi[:, j, :], hid[:, s, :]).then_inc(*up("hid_hi", (tag, chunk)))
                        dve.wait_ge(*when("hid_hi", (tag, chunk)))
                        V.tensor_tensor(hid_lo[:, j, :], hid[:, s, :], hid_hi[:, j, :].bitcast(F32), ALU.subtract).then_inc(*up("hid_lo", (tag, chunk)))
                        chunk += 1
                    for c in part:
                        weights(1)

            def post(tag, r, factor):
                dve.wait_ge(*when("sumsq", (tag + ".p", 1)))
                root(tag + ".p", NT, 1.0 / D / factor ** 2, RMS_EPS / factor ** 2)
                dve.wait_ge(*when(f"row_in{r % 2}", r))
                for t in range(NT):
                    link(V.scalar_tensor_tensor(xn[:, t, :], acc(4, t), st[:, 2, t:t + 1], row[:, r % 2, 0, :],
                                                ALU.mult, ALU.mult))
                    V.tensor_tensor(x[:, t, :], x[:, t, :], xn[:, t, :], ALU.add).then_inc(*up("x_new", (tag, t), ("row", r), ("end", t)))

            def ln(tag, r):
                name = tag if tag.startswith("mlp") else tag + ".out"
                dve.wait_ge(*when("w_used", ("product", name)))
                for t in range(NT):
                    link(V.scalar_tensor_tensor(x[:, t, :], x[:, t, :], ALPHA, acc(4, t), ALU.mult, ALU.add,
                                                accum_out=st[:, 3, t:t + 1]))
                    link(V.tensor_scalar(st[:, 3, 8 + t:9 + t], st[:, 3, t:t + 1], 1.0 / D, None, ALU.mult))
                    V.tensor_scalar(xn[:, t, :], x[:, t, :], st[:, 3, 8 + t:9 + t], None, ALU.subtract).then_inc(*up("centered", (tag, t)))
                dve.wait_ge(*when("sumsq", (tag, 1)))
                root(tag, NT, 1.0 / D, LN_EPS)
                dve.wait_ge(*when(f"row_in{r % 2}", r))
                for t in range(NT):
                    link(V.scalar_tensor_tensor(xn[:, t, :], xn[:, t, :], st[:, 2, t:t + 1], row[:, r % 2, 0, :],
                                                ALU.mult, ALU.mult))
                    V.tensor_tensor(x[:, t, :], xn[:, t, :], row[:, r % 2, 1, :], ALU.add).then_inc(*up("x_new", (tag, t), ("row", r), ("end", t)))

            def qkv(tag, i):
                link(V.memset(pre[:, :, 0:CONV1 - 1], 0.0))
                for c in range(24):
                    dve.wait_ge(*when("pre", (tag, c)))
                    for k in range(CONV1 - 2, -1, -1):
                        ins = V.scalar_tensor_tensor(cacc[:, c % 2, :], pre[:, c % 2, k:k + SEQ],
                                                     col(("convw", i), c * CONV1 + k), cacc[:, c % 2, :],
                                                     ALU.mult, ALU.add)
                        if k:
                            link(ins)
                        else:
                            ins.then_inc(*up("conv4", (tag, c)))
                    weights(1)

            def project(tag, bank):
                for k in range(KC):
                    weights(1)

            def project16(tag):
                weights(1)
                if tag.startswith("gla"):
                    return
                dve.wait_ge(*when("w_used", ("small", tag)))
                V.tensor_copy(small[:, 0:2, :], ps[:, 0:2, 0:16]).then_inc(*up("small", tag))
                dve.wait_ge(*when("small", tag))
                dve.wait_ge(*when("gate_in", tag))
                dt = over(gate[:, 4, 0:GH], NT)
                V.tensor_tensor(small[:, 2:4, 0:GH], small[:, 0:2, GH:2 * GH], dt, ALU.add).then_inc(*up("a_in", tag))
                dve.wait_ge(*when("a_in", tag))
                link(V.tensor_scalar(small[:, 12:14, 0:GH], small[:, 2:4, 0:GH], 0.0, None, ALU.max))
                dve.wait_ge(*when("softplus", tag))
                link(V.tensor_tensor(small[:, 14:16, 0:GH], small[:, 12:14, 0:GH], small[:, 8:10, 0:GH], ALU.add))
                ea = over(small[:, 10, 0:GH], NT)
                V.scalar_tensor_tensor(gate[:, 1:4:2, 0:GH], small[:, 14:16, 0:GH], -1.0, ea, ALU.mult, ALU.mult).then_inc(*up("decays", tag))

            def glu_(tag, i):
                link(V.memset(glu[:, :, 0:CONVB - 1], 0.0))
                for c in range(KC):
                    dve.wait_ge(*when("sig", (tag, c)))
                    V.scalar_tensor_tensor(glu[:, c, CONVB - 1:], ps[:, c % 4, 0:SEQ], col(("pw1b", i), c), sig[:, c % 2, :], ALU.add, ALU.mult).then_inc(*up("glu", (tag, c)))
                    weights(2)

            def conv_taps(tag, i):
                dve.wait_ge(*when("glu", (tag, KC - 1)))
                for first in range(0, KC, 4):
                    for k in range(CONVB):
                        for c in range(first, first + 4):
                            w = col(("dww", i), c * CONVB + k)
                            if k == 0:
                                ins = V.tensor_scalar(hc[:, c, :], glu[:, c, 0:SEQ], w, col(("dwb", i), c),
                                                      ALU.mult, ALU.add)
                            else:
                                dve.wait_ge(*when("conv", ("tap", tag, c, k - 1)))
                                ins = V.scalar_tensor_tensor(hc[:, c, :], glu[:, c, k:k + SEQ], w, hc[:, c, :],
                                                             ALU.mult, ALU.add)
                            ins.then_inc(*up("conv", ("tap", tag, c, k), *([(tag, c)] if k == CONVB - 1 else [])))
                        yield

            def conv31(tag, i):
                for _ in conv_taps(tag, i):
                    pass
                dve.wait_ge(*when("ln_mean", tag))
                m = over(ps[:, 0, 0:SEQ], KC)
                V.tensor_tensor(hc[:, :, :], hc[:, :, :], m, ALU.subtract).then_inc(*up("ln_center", tag))
                dve.wait_ge(*when("ln_var", tag))
                V.tensor_scalar(lnr[:, :], ps[:, 1, 0:SEQ], LN_EPS, None, ALU.add).then_inc(*up("mean", tag + ".c"))
                dve.wait_ge(*when("root", tag + ".c"))
                V.tensor_tensor(hc[:, :, :], hc[:, :, :], over(lnr[:, :], KC), ALU.mult).then_inc(*up("ln_norm", tag))
                for c in range(KC):
                    dve.wait_ge(*when("h_hi", (tag + ".c", c)))
                    V.tensor_tensor(h_lo[:, c, :], hsq[:, c, :], h_hi[:, c, :].bitcast(F32), ALU.subtract).then_inc(*up("h_lo", (tag + ".c", c)))

            def cnv_end(tag, r):
                dve.wait_ge(*when("w_used", ("product", tag + ".cnv")))
                dve.wait_ge(*when(f"row_in{r % 2}", r))
                for t in range(NT):
                    V.tensor_tensor(xn[:, t, :], acc(4, t), row[:, r % 2, 0, :], ALU.add).then_inc(*up("cnv_y", (tag, t), ("row", r)))
                    dve.wait_ge(*when("cnv_y", (tag, t)))
                    link(V.tensor_tensor(gb[:, t, :], gb[:, t, :], xn[:, t, :], ALU.mult))

            def delta(tag, i):
                TT_ = V.tensor_tensor
                for t in range(NT):
                    key = (tag, t)
                    sums, exps = gate[:, 6 + t, :], gate[:, 8 + t, :]
                    beta = gate[:, 2 * t, 0:GH]
                    sc = gate[:, 10, :]
                    for n, w in enumerate((6, 3)):
                        dve.wait_ge(*when("head_square", (key, n)))
                        link(V.tensor_reduce(sc[:, n * GH:(n + 1) * GH], W[w][:, :, :], AX.X, ALU.add))
                    link(V.tensor_scalar(sc[:, 16:24], sc[:, 0:8], L2_EPS, float(GDK), ALU.add, ALU.mult))
                    V.tensor_scalar(sc[:, 24:32], sc[:, 8:16], L2_EPS, None, ALU.add).then_inc(*up("mean", ("g", key)))
                    dve.wait_ge(*when("sums", key))
                    V.tensor_copy(sums[:, 0:32], ps[:, 6, 0:32]).then_inc(*up("sums_out", key))
                    dve.wait_ge(*when("sums_out", key))
                    TT_(sums[:, 32:40], sums[:, 8:16], sums[:, 0:8], ALU.subtract).then_inc(*up("kdiff", key))
                    dve.wait_ge(*when("root", ("g", key)))
                    TT_(W[0][:, :, :], pair(0), wide(sc[:, 16:24], GDK), ALU.mult).then_inc(*up("qn", key))
                    TT_(W[1][:, :, :], pair(2), wide(sc[:, 24:32], GDK), ALU.mult).then_inc(*up("kn", key))
                    if t == 0:
                        dve.wait_ge(*when("beta", tag))
                    TT_(rhs[:, :, 0:GDK], pair(4), wide(beta, GDK), ALU.mult).then_inc(*up("vb", key))
                    dve.wait_ge(*when("gexp", key))
                    link(TT_(sc[:, 32:40], beta, exps[:, 0:8], ALU.mult))
                    TT_(W[4][:, :, :], W[1][:, :, :], wide(beta, GDK), ALU.mult).then_inc(*up("kb", key))
                    TT_(W[5][:, :, :], W[0][:, :, :], wide(exps[:, 0:8], GDK), ALU.mult).then_inc(*up("qd", key))
                    TT_(rhs[:, :, GDK:], W[1][:, :, :], wide(sc[:, 32:40], GDK), ALU.mult).then_inc(*up("rhs_k", key))
                    TT_(W[7][:, :, :], W[1][:, :, :], wide(exps[:, 32:40], GDK), ALU.mult).then_inc(*up("rhs", key))
                    dve.wait_ge(*when("grow", key))
                    TT_(W[2][:, :, :], pair(6), wide(sums[:, 0:8], P), ALU.subtract).then_inc(*up("dif", key))
                    dve.wait_ge(*when("dif", key))
                    V.tensor_scalar(W[2][:, :, :], W[2][:, :, :], 0.0, None, ALU.min).then_inc(*up("dif_min", key))
                    dve.wait_ge(*when("dec", key))
                    link(TT_(W[3][:, :, :], W[2][:, :, :], over(const[:, C_STRICT, :], GH), ALU.mult))
                    link(TT_(W[2][:, :, :], W[2][:, :, :], over(const[:, C_INC, :], GH), ALU.mult))
                    dve.wait_ge(*when("kk", key))
                    link(TT_(W[3][:, :, :], pair(0), W[3][:, :, :], ALU.mult))
                    dve.wait_ge(*when("qk", key))
                    TT_(W[2][:, :, :], pair(2), W[2][:, :, :], ALU.mult).then_inc(*up("qk_out", key))
                    for w in (0, 1):
                        link(V.tensor_copy(W[w][:, :, :], over(ident, GH)))
                    for n in range(len(LEVELS)):
                        if n:
                            dve.wait_ge(*when("mt", (key, n - 1)))
                        TT_(W[4][:, :, :], W[3][:, :, :], over(const[:, C_LVL + n, :], GH), ALU.mult).then_inc(*up("level_m", (key, n)))
                        if n < len(LEVELS) - 1:
                            dve.wait_ge(*when("tmt", (key, n)))
                            link(TT_(W[0][:, :, :], W[0][:, :, :], pair(2), ALU.subtract))
                        dve.wait_ge(*when("tmtT", (key, n)))
                        TT_(W[1][:, :, :], W[1][:, :, :], pair(4), ALU.subtract).then_inc(*up("tt", (key, n)))
                    for j in range(2):
                        ci = 2 * t + j
                        r = slice(j * CH, (j + 1) * CH)
                        dve.wait_ge(*when("u_out", key))
                        if ci == 0:
                            ins = V.tensor_copy(W[6][r], W[0][r])
                        else:
                            dve.wait_ge(*when("ws", (tag, ci)))
                            ins = TT_(W[6][r], W[0][r], pair(4)[r], ALU.subtract)
                        ins.then_inc(*up("v_new", (tag, ci)))
                        if ci < 3:
                            dve.wait_ge(*when("o", (tag, ci)))
                            if ci == 0:
                                ins = V.tensor_copy(state[:, :, :], pair(0))
                            else:
                                link(TT_(state[:, :, :], state[:, :, :],
                                         wide(exps[:, 16 + 8 * j:24 + 8 * j], GDK), ALU.mult))
                                ins = TT_(state[:, :, :], state[:, :, :], pair(0), ALU.add)
                            ins.then_inc(*up("state", (tag, ci)))
                    dve.wait_ge(*when("out_square", key))
                    so = gate[:, 11, :]
                    link(V.tensor_reduce(so[:, 0:8], W[6][:, :, :], AX.X, ALU.add))
                    V.tensor_scalar(so[:, 8:16], so[:, 0:8], 1.0 / GDK, RMS_EPS, ALU.mult, ALU.add).then_inc(*up("mean", ("o", key)))
                    dve.wait_ge(*when("root", ("o", key)))
                    y = xn[:, t, :].rearrange("p (h k) -> p h k", k=GDK)
                    TT_(y, pair(6), wide(so[:, 8:16], GDK), ALU.mult).then_inc(*up("y_raw", (tag, t)))
                    dve.wait_ge(*when("y_raw", (tag, t)))
                    link(TT_(y, y, gnw[:, :, :].to_broadcast([P, GH, GDK]), ALU.mult))
                    if t == 0:
                        dve.wait_ge(*when("evacuated", (tag + ".z", 1)))
                    TT_(xn[:, t, :], xn[:, t, :], zs[:, t, :], ALU.mult).then_inc(*up("y", (tag + ".y", t)))

            def blend(tag):
                dve.wait_ge(*when("w_used", ("product", tag + ".gdn")))
                for t in range(NT):
                    link(V.tensor_tensor(ga[:, t, :], ga[:, t, :], acc(4, t), ALU.mult))
                    V.tensor_tensor(xn[:, t, :], ga[:, t, :], gb[:, t, :], ALU.add).then_inc(*up("y", (tag + ".o", t)))

            def gla(tag, j):
                V.memset(lgT[:, :], 1.0).then_inc(*up("lgT_one", tag))
                link(V.memset(lsc[:, :, :, :], 0.0))
                weights(8)
                project(tag + ".v", 4)
                project(tag + ".r", 0)
                project16(tag)
                dve.wait_ge(*when("s_step", ("abs", tag)))
                link(V.tensor_scalar(lb_[:, :, :], ps[:, 0:2, :], 0.0, None, ALU.min))
                dve.wait_ge(*when("softplus", tag))
                V.tensor_tensor(la[:, :, :], lb_[:, :, :], la[:, :, :], ALU.subtract).then_inc(*up("la", tag))
                dve.wait_ge(*when("lsum", tag))
                flat = LT[:, :, :].rearrange("p h t -> p (h t)")
                link(V.tensor_scalar(flat, acc(2, 0), 1.0 / TAU, None, ALU.mult))
                for n in range(1 + len(LEVELS)):
                    if n:
                        b = LEVELS[n - 1]
                        L = LT[:, :, :].rearrange("p h (c b) -> p (h c) b", b=2 * b)
                        o = ld[:, :, :].rearrange("p h (c b) -> p (h c) b", b=2 * b)
                        mid = L[:, :, b - 1:b].to_broadcast([P, LH * SEQ // (2 * b), 2 * b])
                        V.tensor_tensor(o, L, mid, ALU.subtract).then_inc(*up("ld", (tag, n)))
                        dve.wait_ge(*when("le", (tag, n)))
                        if n >= 2:
                            dve.wait_ge(*when("lsq", (tag, n - 1, 1)))
                        link(V.tensor_tensor(lqe[:, :, :], lqT[:, :, :], ld[:, :, :], ALU.mult))
                        V.tensor_tensor(lke[:, :, :], lkT[:, :, :], ld[:, :, :], ALU.mult).then_inc(*up("lke", (tag, n)))
                    m = const[:, C_ID if n == 0 else C_SYM + n - 1, :].bitcast(I32)
                    for t in range(NT):
                        dve.wait_ge(*when("lsq", (tag, n, t)))
                        src = ps[:, t, :].rearrange("p (h k) -> p h k", k=P)
                        V.copy_predicated(lsc[:, t], over(m, LH), src).then_inc(*up("lscore", (tag, n, t)))
                dve.wait_ge(*when("le", (tag, "q")))
                link(V.tensor_tensor(lqe[:, :, :], lqT[:, :, :], ld[:, :, :], ALU.mult))
                L = LT[:, :, :].rearrange("p h (c b) -> p (h c) b", b=CH)
                o = ld[:, :, :].rearrange("p h (c b) -> p (h c) b", b=CH)
                end = L[:, :, CH - 1:CH].to_broadcast([P, LH * 4, CH])
                V.tensor_tensor(o, end, L, ALU.subtract).then_inc(*up("ld", (tag, "k")))
                dve.wait_ge(*when("le", (tag, "k")))
                V.tensor_tensor(lke[:, :, :], lkT[:, :, :], ld[:, :, :], ALU.mult).then_inc(*up("lkd", tag))
                for t in range(NT):
                    for ci in (2 * t, 2 * t + 1):
                        if ci == 3:
                            continue
                        dve.wait_ge(*when("lo", (tag, ci)))
                        if ci == 0:
                            dve.wait_ge(*when("lend", tag))
                            V.tensor_copy(lst[:, :, :].rearrange("p h v -> p (h v)"), acc(0, 0)).then_inc(*up("lst", (tag, ci)))
                        else:
                            for h in range(LH):
                                V.scalar_tensor_tensor(lst[:, h, :], lst[:, h, :], lend[:, h, ci:ci + 1], acc(0, 0)[:, h * LDV:(h + 1) * LDV], ALU.mult, ALU.add).then_inc(*up("lst", (tag, ci)))
                    dve.wait_ge(*when("out_square", (tag, t)))
                    y = xn[:, t, :].rearrange("p (h k) -> p h k", k=LDV)
                    link(V.tensor_reduce(st[:, 0, 0:LH], y, AX.X, ALU.add))
                    root(("l", tag, t), LH, 1.0 / LDV, RMS_EPS)
                    link(V.tensor_tensor(y, acc(4, t).rearrange("p (h k) -> p h k", k=LDV), wide(st[:, 2, 0:LH], LDV),
                                         ALU.mult))
                    if t == 0:
                        dve.wait_ge(*when("wgu_in", tag))
                    link(V.tensor_tensor(y, y, gln[:, :, :].to_broadcast([P, LH, LDV]), ALU.mult))
                    V.tensor_tensor(xn[:, t, :], xn[:, t, :], lr[:, t, :], ALU.mult).then_inc(*up("y", (tag + ".y", t)))
                take(tag + ".y")

            def mla(tag, j):
                dve.wait_ge(*when("mla_in", tag))
                link(V.tensor_copy(posf[:, :], posi[:, :]))
                for t in range(NT):
                    link(V.tensor_scalar(rope[:, t, 4, :], invf[:, :], posf[:, t:t + 1], None, ALU.mult))
                for n, shift in enumerate((0.0, 0.25)):
                    a, q, red = rope[:, :, 4, :], rope[:, :, 5, :], rope[:, :, n + 2, :]
                    link(V.tensor_scalar(q, a, 1.0 / TWO_PI, shift, ALU.mult, ALU.add))
                    link(V.tensor_scalar(q, q, ROUND, None, ALU.add))
                    link(V.tensor_scalar(q, q, ROUND, None, ALU.subtract))
                    link(V.scalar_tensor_tensor(red, q, -PI_PARTS[0], a, ALU.mult, ALU.add))
                    for part in PI_PARTS[1:]:
                        link(V.scalar_tensor_tensor(red, q, -part, red, ALU.mult, ALU.add))
                    link(V.tensor_scalar(red, red, shift * TWO_PI, None, ALU.add))
                    V.tensor_scalar(red, red, PI_IN, -PI_IN, ALU.min, ALU.max).then_inc(*up("angle", tag))
                weights(4)
                for t in range(NT):
                    dve.wait_ge(*when("sumsq", (tag + ".c", t)))
                root(tag + ".c", 4, 1.0 / 256, RMS_EPS)
                for t in range(NT):
                    for n in range(2):
                        c = slice(n * 256, (n + 1) * 256)
                        dve.wait_ge(*when("mc_out", (tag, t)))
                        V.tensor_scalar(mcn[:, t, c], mc[:, t, c], st[:, 2, 2 * t + n:2 * t + n + 1], None, ALU.mult).then_inc(*up("mcn", (tag, t)))
                weights(1)
                take(tag + ".c", lambda c: col(("qnorm", 0), c) if c < 2 else col(("kvnorm", 0), c - 2), 4)
                weights(7)
                dve.wait_ge(*when("sine", tag))

                def rotate(src, out, tmp, t, n):
                    cos = over(rope[:, t, 1, :], n)
                    sin = over(rope[:, t, 0, :], n)
                    x1, x2, o1, o2 = src[:, :, 0:32], src[:, :, 32:64], out[:, :, 0:32], out[:, :, 32:64]
                    t1, t2 = tmp[:, :, 0:32], tmp[:, :, 32:64]
                    link(V.tensor_tensor(o1, x1, cos, ALU.mult))
                    link(V.tensor_tensor(t1, x2, sin, ALU.mult))
                    link(V.tensor_tensor(o2, x2, cos, ALU.mult))
                    link(V.tensor_tensor(t2, x1, sin, ALU.mult))
                    link(V.tensor_tensor(o1, o1, t1, ALU.subtract))
                    return V.tensor_tensor(o2, o2, t2, ALU.add)

                def heads_of(ap):
                    return ap.rearrange("p (h d) -> p h d", d=MR)

                dve.wait_ge(*when("mkr_out", tag))
                for t in range(NT):
                    link(rotate(heads_of(mkr[:, t, MR:]), heads_of(mkr[:, t, 0:MR]), heads_of(mcn[:, t, 0:MR]), t, 1))
                    link(V.tensor_copy(mkr[:, t, MR:], mkr[:, t, 0:MR]))
                for t in range(NT):
                    dve.wait_ge(*when("mqr_out", (tag, t)))
                    rotate(heads_of(mqr[:, t, :]), heads_of(mqr2[:, t, :]), heads_of(mcn[:, t, :]), t, MH).then_inc(*up("roped", tag))
                for t in range(NT):
                    dve.wait_ge(*when("mscore", (tag, t)))
                    s = ps[:, 0:4, :].rearrange("p b (h k) -> p (b h) k", k=SEQ)
                    V.tensor_tensor(msc[:, :, :], s, over(mask[:, t, :], MH), ALU.add).then_inc(*up("msm", (tag, t)))
                    dve.wait_ge(*when("msm", (tag, t)))
                    link(V.tensor_reduce(mst[:, 0, :], msc[:, :, :], AX.X, ALU.max))
                    V.tensor_scalar(mst[:, 1, :], mst[:, 0, :], -MLA_SCALE, None, ALU.mult).then_inc(*up("mmax", (tag, t)))
                    dve.wait_ge(*when("mexp", (tag, t)))
                    link(V.reciprocal(mst[:, 3, :], mst[:, 2, :]))
                    dve.wait_ge(*when("mo", (tag, t)))
                    for b in range(2):
                        y = xn[:, t, :].rearrange("p (a b k) -> p b a k", b=2, k=P)[:, b]
                        V.tensor_tensor(y, pair(0)[:, 4 * b:4 * b + 4, :], wide(mst[:, 3, 4 * b:4 * b + 4], P), ALU.mult).then_inc(*up("y", (tag + ".y", t)))
                take(tag + ".y")

            def conv(tag, j):
                link(V.memset(cpad[:, :, 0:2], 0.0))
                for c in range(KC):
                    dve.wait_ge(*when("ctmp", (tag, c)))
                    V.tensor_tensor(cpad[:, c, 2:], ctmp[:, c % 2, :], ps[:, c % 4, SEQ:2 * SEQ], ALU.mult).then_inc(*up("cu", (tag, c)))
                    weights(2)
                for c in range(KC):
                    for k in range(3):
                        w = col(("conv3", 0), c * 3 + k)
                        if k == 0:
                            dve.wait_ge(*when("cu", (tag, c)))
                            link(V.tensor_scalar(cz[:, c, :], cpad[:, c, 0:SEQ], w, None, ALU.mult))
                        else:
                            link(V.scalar_tensor_tensor(cz[:, c, :], cpad[:, c, k:k + SEQ], w, cz[:, c, :],
                                                        ALU.mult, ALU.add))
                    dve.wait_ge(*when("w_used", ("cb", tag, c)))
                    V.tensor_tensor(cz[:, c, :], cz[:, c, :], ps[:, c % 4, 0:SEQ], ALU.mult).then_inc(*up("cbz", (tag, c)))
                    weights(1)
                for c in range(KC):
                    dve.wait_ge(*when("h_hi", (tag + ".y", c)))
                    V.tensor_tensor(h_lo[:, c, :], cz[:, c, :], h_hi[:, c, :].bitcast(F32), ALU.subtract).then_inc(*up("h_lo", (tag + ".y", c)))

            def ple(tag, i):
                weights(2)
                dve.wait_ge(*when("w_used", ("product", tag)))
                dve.wait_ge(*when("evacuated", (tag + ".g", 1)))
                for t in range(NT):
                    link(V.tensor_tensor(xn[:, t, :], ple_g[:, t, :], acc(0, t), ALU.mult))
                    V.tensor_tensor(x[:, t, :], x[:, t, :], xn[:, t, :], ALU.add).then_inc(*up("x_new", (tag, t), ("end", t)))

            dve.wait_ge(sg.sem("cols_in"), 16)
            dve.wait_ge(sg.sem("const_in"), 16)
            dve.wait_ge(sg.sem("x_in"), 16)
            for t in range(NT):
                V.memset(neghalf[:, t * P:(t + 1) * P], -0.5).then_inc(*up("x_new", ("x_in", t)))
            weights(0)
            table = dict(norm=norm, turn_x=turn_x, turn=turn, ffn=ffn, post=post, ln=ln, qkv=qkv, project=project,
                         project16=project16, glu=glu_, conv31=conv31, cnv_end=cnv_end, delta=delta, blend=blend,
                         gla=gla, mla=mla, conv=conv, ple=ple)
            for name, *args in STAGES:
                table[name](*args)
            weights(0)

        @block.gpsimd
        def _(pool):
            loaded = [0]

            def rows_in(r):
                if r >= len(ROWS):
                    return
                if r >= 2:
                    pool.wait_ge(*when("cnv_y" if ROWS[r - 2][0][0] == "cnv_b_o" else "x_new", ("row", r - 2)))
                n = len(ROWS[r])
                pool.dma_start(row[:, r % 2, 0:n, :], io["rows"][r:r + 1, 0:n, :].to_broadcast([P, n, D])).then_inc(*up(f"row_in{r % 2}", r, by=16))

            def root(tag, n, out=None):
                pool.wait_ge(*when("mean", tag))
                src = st[:, 1, 0:n] if out is None else out
                dst = st[:, 2, 0:n] if out is None else out
                nc.gpsimd.tensor_tensor(dst, src, neghalf[:, 0:n], ALU.pow).then_inc(*up("root", tag))

            def norm(tag, prev, key):
                root(tag, NT)

            def post(tag, r, factor):
                root(tag + ".p", NT)
                rows_in(r + 2)

            def ln(tag, r):
                root(tag, NT)
                rows_in(r + 2)

            def conv31(tag, i):
                root(tag + ".c", SEQ, lnr[:, :])

            def cnv_end(tag, r):
                rows_in(r + 2)

            def qkv(tag, i):
                pool.wait_ge(*when("x_new", (f"ffn1.{i}", 1)))
                pool.dma_start(gate[:, 4:6, 0:GH], io["gate_rows"][i:i + 1].to_broadcast([P, 2, GH])).then_inc(*up("gate_in", tag, by=16))
                pool.dma_start(gnw[:, :, :], io["gdn_norm"][i:i + 1].to_broadcast([P, 1, GDK])).then_inc(*up("gate_in", tag, by=16))

            def delta(tag, i):
                for t in range(NT):
                    root(("g", (tag, t)), 16, gate[:, 10, 16:32])
                    root(("o", (tag, t)), 8, gate[:, 11, 8:16])

            def gla(tag, j):
                n = int(tag.split(".")[1])
                pool.wait_ge(*when("x_new", (f"ffn2.{L1 - 1}" if n == 0 else f"ple.{n - 1}", 1)))
                pool.dma_start(wgu[:, :], io["gla_gate"][j]).then_inc(*up("wgu_in", tag, by=16))
                pool.dma_start(gln[:, :, :], io["gla_norm"][j:j + 1].to_broadcast([P, 1, LDV])).then_inc(*up("wgu_in", tag, by=16))
                for t in range(NT):
                    root(("l", tag, t), LH)

            def mla(tag, j):
                pool.wait_ge(*when("x_new", ("ple.0", 1)))
                pool.dma_start(posi[:, :], io["positions"]).then_inc(*up("mla_in", tag, by=16))
                pool.dma_start(invf[:, :], io["inv_freq"]).then_inc(*up("mla_in", tag, by=16))
                pool.dma_start(mask[:, :, :], io["mask"]).then_inc(*up("mla_in", tag, by=16))
                root(tag + ".c", 4)

            def turn_x(tag, prev):
                if tag.startswith("ple"):
                    i = int(tag.split(".")[1])
                    pool.dma_start(ple_p[:, :, :], io["p"][i]).then_inc(*up("ple_in", tag, by=16))

            def nothing(*args):
                pass

            rows_in(0)
            rows_in(1)
            table = dict(norm=norm, post=post, ln=ln, conv31=conv31, cnv_end=cnv_end, qkv=qkv, delta=delta, gla=gla,
                         mla=mla, turn_x=turn_x)
            for name, *args in STAGES:
                table.get(name, nothing)(*args)

        memory = dict(sg.at)
    return memory


TWO_PI = 2 * np.pi
PI_PARTS = [6.28125, 0.0019350051879882812, 3.019916050561e-07]
ROUND = 1.5 * 2.0 ** 23
PI_IN = 3.1415925


def unit_width(u):
    kind, w, i, a, b, n = u
    if kind == "T":
        return b * n * P
    k_all = K_OF.get(w, D) // P
    return min(k_all - a, UW // n) * n


K_OF = {"mla_uq_rope": 256, "mla_uv": 256, "ple_w_proj_2": 256, "ffn1_w_out": FF1, "ffn2_w_out": FF1,
        "mlp_w2_2": 4 * D}


def pack(inputs):
    f = {k: np.asarray(v) for k, v in inputs.items()}
    uq = f["mla_w_uq_2"].reshape(-1, 256, MH, MN + MR)
    ukv = f["mla_w_ukv_2"].reshape(-1, 256, MH, 2 * MN)
    f["mla_uq_nope"] = np.ascontiguousarray(uq[..., :MN]).reshape(-1, 256, MH * MN)
    f["mla_uq_rope"] = np.ascontiguousarray(uq[..., MN:]).reshape(-1, 256, MH * MR)
    f["mla_uk"] = np.ascontiguousarray(ukv[..., :MN]).reshape(-1, 256, MH * MN)
    f["mla_uv"] = np.ascontiguousarray(ukv[..., MN:]).reshape(-1, 256, MH * MN)
    units = unit_list()
    w = np.zeros((len(units), P, UW), np.float32)
    for n, (kind, name, i, a, b, c) in enumerate(units):
        src = f[name][i]
        if kind == "T":
            for m in range(c):
                blocks = src[:b * P, a + m * P:a + (m + 1) * P].reshape(b, P, P)
                w[n, :, m * b * P:(m + 1) * b * P] = blocks.transpose(1, 0, 2).reshape(P, b * P)
        else:
            k = min(src.shape[0] // P - a, UW // c)
            rows = src[a * P:(a + k) * P, b:b + c].reshape(k, P, c)
            w[n, :, :k * c] = rows.transpose(1, 0, 2).reshape(P, k * c)
    lay = column_layout()
    cols = np.zeros((P, lay.n), np.float32)
    for name, (key, i), n in lay.parts:
        at, v = lay.at[key, i], f[name][i]
        taps = v if v.ndim == 2 else v[None]
        cols[:, at:at + n] = taps.reshape(taps.shape[0], -1, P).transpose(2, 1, 0).reshape(P, n)
    places = row_layout()
    rows = np.zeros((len(places), 2, D), np.float32)
    for r, place in enumerate(places):
        for n, (name, *at) in enumerate(place):
            rows[r, n] = f[name][tuple(at)]
    inv_freq = (10000.0 ** (-np.arange(MR // 2) * 2.0 / MR)).astype(np.float32)
    return {
        "weights": w,
        "x": np.ascontiguousarray(f["x"][0].reshape(NT, P, D).transpose(1, 0, 2)),
        "const": constants(),
        "cols": cols,
        "rows": rows,
        "gate_rows": np.ascontiguousarray(np.stack([f["gdn_dt_bias"], f["gdn_a_log"]], 1)),
        "gdn_norm": np.ascontiguousarray(f["gdn_norm_w"][:, None]),
        "gla_gate": np.ascontiguousarray(np.concatenate([f["gla_w_gate_up_2"], f["gla_b_gate_2"][:, None]], 1)),
        "gla_norm": np.ascontiguousarray(f["gla_norm_g_2"][:, None]),
        "positions": np.ascontiguousarray(f["positions_2"].reshape(NT, P).T),
        "inv_freq": np.ascontiguousarray(np.broadcast_to(inv_freq, (P, 32))),
        "mask": attention_mask(),
        "p": np.ascontiguousarray(f["p_2"][:, 0].reshape(L2, SEQ, 2, P).transpose(0, 3, 2, 1)),
    }


def build(new_core, arrays, last=None):
    plan = None
    for _ in range(2):
        nc = new_core()
        io = {n: nc.dram_tensor("in_" + n, a.shape, mybir.dt.from_np(a.dtype), kind="ExternalInput").ap()
              for n, a in arrays.items()}
        io["out"] = nc.dram_tensor("out", (P, NT, D), F32, kind="ExternalOutput").ap()
        plan = emit(nc, io, plan, last)
    return nc


def kernel(**inputs):
    import concourse.bacc as bacc
    from concourse.bass_utils import run_bass_kernel_spmd

    arrays = pack(inputs)
    nc = build(lambda: bacc.Bacc("TRN2", target_bir_lowering=False, num_devices=1), arrays)
    r = run_bass_kernel_spmd(nc, [{"in_" + n: a for n, a in arrays.items()}], core_ids=[0])
    out = np.asarray(r.results[0]["out"])
    return np.ascontiguousarray(out.transpose(1, 0, 2)).reshape(1, SEQ, D)
```

```python
from contextlib import ExitStack

import numpy as np

import concourse.bass as bass
from concourse import mybir

F32 = mybir.dt.float32
F32R = mybir.dt.float32r
I32 = mybir.dt.int32
ALU = mybir.AluOpType
ACT = mybir.ActivationFunctionType
AX = mybir.AxisListType

P = 128
D = 1024
SEQ = 256
NT = SEQ // P
KC = D // P
UW = 1024
NS = 4
LAST = 2
BANK = 512

L1, L2 = 2, 4
FF1 = 2816
FF1_C = FF1 // P
FF1_HALF = FF1_C // 2
FF2_C = 4 * D // P
FF2_HALF = 11
GH, GDK = 8, 128
CH = 64
CONV1 = 4
CONVB = 31
LH, LDV = 4, 256
MH, MN, MR = 8, 128, 64
RMS_EPS, LN_EPS, L2_EPS = 1e-6, 1e-5, 1e-6
ALPHA = (2 * L2) ** 0.25
TAU = 16.0
KINDS = ["gla", "mla", "conv", "gla"]
LEVELS = [1, 2, 4, 8, 16, 32]
NORM_SCALE = float(GDK) ** -0.5
MLA_SCALE = float(MN + MR) ** -0.5


class Columns:

    def __init__(self):
        self.at, self.n, self.parts = {}, 0, []

    def add(self, name, key, count):
        self.at[key] = self.n
        self.parts.append((name, key, count))
        self.n += count


def column_layout():
    c = Columns()
    for i in range(L1):
        c.add("ffn1_norm_pre", ("ffn1", i), KC)
        c.add("mix_norm_pre", ("mix", i), KC)
        c.add("ffn2_norm_pre", ("ffn2", i), KC)
        c.add("gdn_conv_w", ("convw", i), 24 * CONV1)
        c.add("cnv_pw1_b", ("pw1b", i), 16)
        c.add("cnv_dw_w", ("dww", i), KC * CONVB)
        c.add("cnv_dw_b", ("dwb", i), KC)
        c.add("cnv_ln_g", ("lng", i), KC)
        c.add("cnv_ln_b", ("lnb", i), KC)
    c.add("mla_q_norm_2", ("qnorm", 0), 2)
    c.add("mla_kv_norm_2", ("kvnorm", 0), 2)
    c.add("conv_w_2", ("conv3", 0), KC * 3)
    return c


def row_layout():
    rows = []
    for i in range(L1):
        rows.append([("ffn1_norm_post", i)])
        rows.append([("cnv_b_o", i)])
        rows.append([("mix_norm_post", i)])
        rows.append([("ffn2_norm_post", i)])
    for i in range(L2):
        rows.append([("ln_g_2", i, 0), ("ln_b_2", i, 0)])
        rows.append([("ln_g_2", i, 1), ("ln_b_2", i, 1)])
    return rows


def unit_list():
    u = []

    def feature(w, i, col, k=KC, chunks=1):
        u.append(("T", w, i, col, k, chunks))

    def rows(w, i, kc, col=0, width=UW):
        u.append(("R", w, i, kc, col, width))

    def ffn1(a, b, i):
        for half in range(2):
            for c in range(half * FF1_HALF, (half + 1) * FF1_HALF):
                feature(a, i, c * P)
                feature(a, i, FF1 + c * P)
            for c in range(half * FF1_HALF, (half + 1) * FF1_HALF):
                rows(b, i, c)

    for i in range(L1):
        ffn1("ffn1_w_in", "ffn1_w_out", i)
        for c in range(KC):
            feature("mix_w_in", i, 4112 + c * P)
            feature("mix_w_in", i, 4112 + 1024 + c * P)
        rows("mix_w_in", i, 0, 4096, 16)
        for c in range(24):
            feature("mix_w_in", i, c * P)
        for col in (3072, 4112 + 2048, 4112 + 3072):
            for k in range(KC):
                rows("mix_w_in", i, k, col)
        for w in ("cnv_w_o", "gdn_w_o", "mix_w_out"):
            for k in range(KC):
                rows(w, i, k)
        ffn1("ffn2_w_in", "ffn2_w_out", i)
    for i, kind in enumerate(KINDS):
        j = i // 3
        if kind == "gla":
            for c in range(8):
                feature("gla_w_in_2", j, c * P)
                if c == 0:
                    rows("gla_w_in_2", j, 0, 3072, 16)
            for k in range(KC):
                rows("gla_w_in_2", j, k, 1024)
            for k in range(KC):
                rows("gla_w_in_2", j, k, 2048)
            for k in range(KC):
                rows("gla_w_out_2", j, k)
        elif kind == "mla":
            for k in range(0, KC, 2):
                rows("mla_w_in_2", j, k, 0, 512)
            rows("mla_w_in_2", j, 0, 512, MR)
            for c in range(0, MH, 4):
                feature("mla_uq_nope", j, c * P, 2, 4)
            rows("mla_uq_rope", j, 0, 0, 512)
            for c in range(0, MH, 4):
                feature("mla_uk", j, c * P, 2, 4)
            for k in range(2):
                rows("mla_uv", j, k)
            for k in range(KC):
                rows("mla_w_out_2", j, k)
        else:
            for c in range(KC):
                feature("conv_w_in_2", j, D + c * P)
                feature("conv_w_in_2", j, 2 * D + c * P)
            for c in range(KC):
                feature("conv_w_in_2", j, c * P)
            for k in range(KC):
                rows("conv_w_out_2", j, k)
        for first in range(0, FF2_C, FF2_HALF):
            part = range(first, min(first + FF2_HALF, FF2_C))
            for c in part:
                feature("mlp_w1_2", i, c * P)
            for c in part:
                rows("mlp_w2_2", i, c)
        for k in range(KC):
            rows("ple_w_gate_2", i, k)
        for k in range(2):
            rows("ple_w_proj_2", i, k)
    return u


C_ID, C_INC, C_STRICT, C_SAME, C_IND0, C_IND1, C_MEAN, C_LVL, C_SYM, N_CONST = 0, 1, 2, 3, 4, 5, 6, 7, 13, 19


def constants():
    s, c = np.arange(P)[:, None], np.arange(P)[None, :]
    same = (s // CH) == (c // CH)
    mats = [s == c, same & (s <= c), same & (s < c), same, (s < CH) & (c >= 0), (s >= CH) & (c >= 0)]
    out = [m.astype(np.float32) for m in mats] + [np.full((P, P), 1.0 / D, np.float32)]
    lower = [((s // (2 * b)) == (c // (2 * b))) & (s % (2 * b) < b) & (c % (2 * b) >= b) for b in LEVELS]
    out += [m.astype(np.float32) for m in lower]
    out += [(m | m.T).astype(np.float32) for m in lower]
    return np.ascontiguousarray(np.stack(out, 1))


def attention_mask():
    q, k = np.arange(SEQ)[:, None] // CH, np.arange(SEQ)[None, :] // CH
    m = np.where(k <= q, 0.0, -1e30).astype(np.float32)
    return np.ascontiguousarray(m.reshape(NT, P, SEQ).transpose(1, 0, 2))


def stage_list():
    s, prev = [], "x_in"
    r = 0
    for i in range(L1):
        for part in ("ffn1", "mix", "ffn2"):
            tag = f"{part}.{i}"
            s.append(("norm", tag, prev, (part, i)))
            then = f"mix.{i}" if part == "ffn1" else f"ffn1.{i + 1}" if i + 1 < L1 else None
            if part == "mix":
                s += [("glu", tag, i), ("project16", tag), ("qkv", tag, i), ("mixer", tag, i, r),
                      ("turn", tag + ".y", None), ("project", tag + ".gdn", 4), ("blend", tag),
                      ("turn", tag + ".o", None), ("project", tag + ".out", 4), ("post", tag, r + 1, 1.0, f"ffn2.{i}")]
                r += 2
            else:
                s += [("ffn", tag, FF1_C, FF1_HALF, True), ("post", tag, r, 0.5, then)]
                r += 1
            prev = tag
    for i, kind in enumerate(KINDS):
        tag = f"{kind}.{i}"
        s += [("turn_x", tag, prev), (kind, tag, i // 3), ("project", tag + ".out", 4), ("ln", tag, r),
              ("turn_x", f"mlp.{i}", tag), ("ffn", f"mlp.{i}", FF2_C, FF2_HALF, False), ("ln", f"mlp.{i}", r + 1),
              ("turn_x", f"ple.{i}", f"mlp.{i}"), ("project", f"ple.{i}.g", 4), ("ple", f"ple.{i}", i)]
        prev, r = f"ple.{i}", r + 2
    return s


GROUP = 4
GROUPS = GH // GROUP
GROUP_STEPS = 10 + 2 * len(LEVELS)
MAIN_STEPS = NT * GROUPS * GROUP_STEPS
LN_STEPS = 6
SIDE_STEPS = 4 * (KC + 1) + LN_STEPS


def interleave(main, side):
    taken = 0
    for n, _ in enumerate(main):
        while taken < SIDE_STEPS and taken * MAIN_STEPS <= n * SIDE_STEPS:
            next(side)
            taken += 1
    assert n + 1 == MAIN_STEPS and taken == SIDE_STEPS
    for _ in side:
        assert False


class Signals:

    def __init__(self, nc, ctx, plan):
        self.nc, self.ctx, self.plan = nc, ctx, plan
        self.sems, self.count, self.at = {}, {}, {}

    def sem(self, name):
        if name not in self.sems:
            self.sems[name] = self.ctx.enter_context(self.nc.semaphore(name))
            self.count[name] = 0
        return self.sems[name]

    def up(self, name, *keys, by=1):
        sem = self.sem(name)
        self.count[name] += by
        for key in keys:
            self.at[name, key] = self.count[name]
        return sem, by

    def reached(self, name, key):
        return self.sem(name), self.plan[name, key] if self.plan else 1


def emit(nc, io, plan, last=None):
    UNITS = unit_list()
    STAGES = stage_list()[:last]
    NU = plan["units"] if plan else len(UNITS)
    COLS, ROWS = column_layout(), row_layout()
    ctx = ExitStack()
    with ctx:
        sg = Signals(nc, ctx, plan)
        up, when = sg.up, sg.reached

        def sb(name, shape, dt=F32, stack=ctx):
            return stack.enter_context(nc.sbuf_tensor(name, shape, dt))

        w_raw = sb("w_raw", [P, NS, UW])
        w_hi = sb("w_hi_part", [P, NS, UW], F32R)
        w_lo = sb("w_lo_part", [P, NS, UW], F32R)
        x = sb("x_res", [P, NT, D])
        xn = sb("xn", [P, NT, D])
        h_hi = sb("h_hi_part", [P, KC, SEQ], F32R)
        h_lo = sb("h_lo_part", [P, KC, SEQ], F32R)
        const = sb("const", [P, N_CONST, P])
        cols = sb("cols", [P, COLS.n])
        row = sb("row", [P, 2, 2, D])
        neghalf = sb("neghalf", [P, 16])
        st = sb("stats", [P, 4, 32])
        ident = const[:, C_ID, :]

        ff = ExitStack()
        hid_hi = sb("hid_hi_part", [P, FF2_HALF, SEQ], F32R, ff)
        hid_lo = sb("hid_lo_part", [P, FF2_HALF, SEQ], F32R, ff)
        act_out = sb("act_out", [P, 2, SEQ], F32, ff)
        hid = sb("hid", [P, 2, SEQ], F32, ff)
        ple_g = sb("ple_g", [P, NT, D], F32, ff)
        ple_p = sb("ple_p", [P, 2, SEQ], F32, ff)
        ple_hi = sb("ple_hi_part", [P, 2, SEQ], F32R, ff)
        ple_lo = sb("ple_lo_part", [P, 2, SEQ], F32R, ff)
        ff.close()

        m1 = ExitStack()
        qkvT = sb("qkvT", [P, 24, SEQ], F32, m1)
        zs = sb("zs", [P, NT, D], F32, m1)
        ga = sb("ga", [P, NT, D], F32, m1)
        gb = sb("gb", [P, NT, D], F32, m1)
        small = sb("small", [P, 24, 16], F32, m1)
        gate = sb("gdn_gate", [P, 12, 40], F32, m1)
        gnw = sb("gdn_norm", [P, 1, GDK], F32, m1)
        pre = sb("conv_pre", [P, 2, CONV1 - 1 + SEQ], F32, m1)
        cacc = sb("conv_acc", [P, 2, SEQ], F32, m1)
        sig = cacc
        glu = sb("glu", [P, KC, CONVB - 1 + SEQ], F32, m1)
        hc = sb("hc", [P, KC, SEQ], F32, m1)
        hsq = xn[:, :, :].rearrange("p t (c s) -> p (t c) s", s=SEQ)
        lnm = sb("conv_ln", [P, 8], F32, m1)
        W = [sb(f"gdn_w{n}", [P, GROUP, GDK], F32, m1) for n in range(8)]
        rhs = sb("gdn_rhs", [P, GROUP, 2 * GDK], F32, m1)
        state = sb("gdn_state", [P, GH, GDK], F32, m1)
        m1.close()

        m2 = ExitStack()
        lqT = sb("lqT", [P, LH, SEQ], F32, m2)
        lkT = sb("lkT", [P, LH, SEQ], F32, m2)
        lv = sb("lv", [P, NT, D], F32, m2)
        lr = sb("lr", [P, NT, D], F32, m2)
        lg = sb("lg", [P, NT, 16], F32, m2)
        lgT = sb("lgT", [17, SEQ], F32, m2)
        wgu = sb("wgu", [17, 512], F32, m2)
        la = sb("la", [P, NT, 512], F32, m2)
        lb_ = sb("lb", [P, NT, 512], F32, m2)
        LT = sb("LT", [P, LH, SEQ], F32, m2)
        ld = sb("ld", [P, LH, SEQ], F32, m2)
        lqe = sb("lqe", [P, LH, SEQ], F32, m2)
        lke = sb("lke", [P, LH, SEQ], F32, m2)
        lsc = sb("lsc", [P, NT, LH, P], F32, m2)
        lkd = sb("lkd", [P, NT, LH, P], F32, m2)
        lst = sb("lst", [P, LH, LDV], F32, m2)
        lend = sb("lend", [P, LH, 4], F32, m2)
        gln = sb("gla_norm", [P, 1, LDV], F32, m2)
        m2.close()

        m3 = ExitStack()
        mc = sb("mc", [P, NT, 512], F32, m3)
        mkr = sb("mkr", [P, NT, 2 * MR], F32, m3)
        mkrT = sb("mkrT", [P, SEQ], F32, m3)
        mcn = sb("mcn", [P, NT, 512], F32, m3)
        mqnT = sb("mqnT", [P, MH, SEQ], F32, m3)
        mknT = sb("mknT", [P, MH, SEQ], F32, m3)
        mqr = sb("mqr", [P, NT, 512], F32, m3)
        mqr2 = sb("mqr2", [P, NT, 512], F32, m3)
        mqrT = sb("mqrT", [P, 4, SEQ], F32, m3)
        mv = sb("mv", [P, NT, D], F32, m3)
        msc = sb("msc", [P, MH, SEQ], F32, m3)
        mpT = sb("mpT", [P, MH, NT, P], F32, m3)
        mask = sb("mask", [P, NT, SEQ], F32, m3)
        rope = sb("rope", [P, NT, 8, 32], F32, m3)
        invf = sb("invf", [P, 32], F32, m3)
        posi = sb("posi", [P, NT], I32, m3)
        posf = sb("posf", [P, NT], F32, m3)
        mst = sb("mst", [P, 4, MH], F32, m3)
        m3.close()

        m4 = ExitStack()
        cpad = sb("cpad", [P, KC, 2 + SEQ], F32, m4)
        cz = sb("cz", [P, KC, SEQ], F32, m4)
        ctmp = sb("ctmp", [P, 2, SEQ], F32, m4)
        m4.close()

        ps = ctx.enter_context(nc.psum_tensor("ps", [P, 8, BANK], F32))

        def acc(bank, t):
            return ps[:, bank + 2 * t:bank + 2 * t + 2, :].rearrange("p a b -> p (a b)")

        def heads_in(bank):
            return ps[:, bank, :].rearrange("p (h k) -> p h k", k=P)

        def pair(bank):
            return ps[:, bank:bank + 2, :].rearrange("p a (b c) -> p (a b) c", c=P)

        w_in = [sg.sem(f"w_in{n}") for n in range(NS)]

        def col(key, n):
            at = COLS.at[key] + n
            return cols[:, at:at + 1]

        def wide(ap, n):
            return ap.rearrange("p (a b) -> p a b", b=1).to_broadcast([P, ap.shape[1], n])

        def slot_of(h):
            return (h % 2) * (MH // 2) + h // 2

        def over(ap, n):
            return ap.rearrange("p (a b) -> p a b", a=1).to_broadcast([P, n, ap.shape[1]])

        block = ctx.enter_context(nc.Block())

        @block.sync
        def _(sp):
            sp.dma_start(x[:, :, :], io["x"]).then_inc(sg.sem("x_in"), 16)
            sp.dma_start(const[:, :, :], io["const"]).then_inc(sg.sem("const_in"), 16)
            sp.dma_start(cols[:, :], io["cols"]).then_inc(sg.sem("cols_in"), 16)
            for s in range(NS):
                sp.dma_start(w_raw[:, s, :], io["weights"][s]).then_inc(w_in[s], 16)
            rounds = NU // NS
            with sp.Fori(1, rounds) as r:
                for s in range(NS):
                    sp.wait_ge(sg.sem("w_lo"), r * NS + (s + 1 - NS))
                    sp.dma_start(w_raw[:, s, :], io["weights"][r * NS + s]).then_inc(w_in[s], 16)
            for n in range(rounds * NS, NU):
                sp.wait_ge(sg.sem("w_lo"), n + 1 - NS)
                sp.dma_start(w_raw[:, n % NS, :], io["weights"][n]).then_inc(w_in[n % NS], 16)
            for t in range(NT):
                sp.wait_ge(*when("x_new", ("end", t)))
                sp.dma_start(io["out"][:, t], x[:, t, :]).then_inc(sg.sem("stored"), 16)
            sp.wait_ge(sg.sem("stored"), 16 * NT)

        @block.tensor
        def _(pe):
            used = [0]

            def mm(out, lhsT, rhs_, start=True, stop=True):
                return nc.tensor.matmul(out, lhsT, rhs_, start=start, stop=stop, skip_group_check=True)

            def next_unit():
                u = used[0]
                used[0] += 1
                pe.wait_ge(sg.sem("w_lo"), u + 1)
                return u % NS

            def feature_chunk(s, out, hi, lo, k_n, first=0, ready=None):
                for k in range(k_n):
                    if ready:
                        pe.wait_ge(*when("h_lo", (ready, k | 1)))
                    b = slice((first + k) * P, (first + k + 1) * P)
                    mm(out, w_hi[:, s, b], hi[:, k, :], k == 0, False)
                    mm(out, w_hi[:, s, b], lo[:, k, :], False, False)
                    last_ = mm(out, w_lo[:, s, b], hi[:, k, :], False, k == k_n - 1)
                return last_

            def row_chunk(s, outs, hi, lo, first, start, stop_, width=BANK, n_out=2, tiles=range(NT)):
                for t in tiles:
                    tok = slice(t * P, (t + 1) * P)
                    for n in range(n_out):
                        c = slice(first + n * width, first + (n + 1) * width)
                        mm(outs(t, n), hi[:, tok], w_hi[:, s, c], start, False)
                        mm(outs(t, n), hi[:, tok], w_lo[:, s, c], False, False)
                        last_ = mm(outs(t, n), lo[:, tok], w_hi[:, s, c], False, stop_)
                return last_

            def last_units(tag, parts):
                slots = []
                for t in range(NT):
                    for n, (hi, lo, ready) in enumerate(parts):
                        if t == 0:
                            if ready:
                                pe.wait_ge(*when(*ready))
                            slots.append(next_unit())
                        last_ = row_chunk(slots[n], lambda t, m: ps[:, 4 + 2 * t + m, :], hi, lo, 0, False,
                                          n == LAST - 1, tiles=[t])
                        if t == NT - 1:
                            last_.then_inc(*up("w_used", *([("product", tag)] if n == LAST - 1 else [])))
                    if t == 0:
                        last_.then_inc(*up("product_0", tag))

            def project(tag, bank, source=None, ready=None, more=None):
                if more:
                    pe.wait_ge(*when(*more))
                for k in range(KC - LAST):
                    if ready:
                        pe.wait_ge(*when("h_lo", (ready, k | 1)))
                    s = next_unit()
                    last_ = row_chunk(s, lambda t, n: ps[:, bank + 2 * t + n, :], h_hi[:, k, :], h_lo[:, k, :],
                                      0, k == 0, False)
                    last_.then_inc(*up("w_used"))
                last_units(tag, [(h_hi[:, k, :], h_lo[:, k, :], ("h_lo", (ready, k | 1)) if ready else None)
                                 for k in range(KC - LAST, KC)])

            def turn(tag, src, ready):
                for t in range(NT):
                    pe.wait_ge(*when(ready[0], (ready[1], t)))
                    for c in range(KC):
                        at = (c % 2) * SEQ + t * P
                        last_ = nc.tensor.transpose(ps[:, c // 2, at:at + P], src[:, t, c * P:(c + 1) * P], ident)
                        if t == NT - 1:
                            last_.then_inc(*up("turned", (tag, c)))

            def norm(tag, prev, key):
                turn(tag, xn, ("xn", tag))

            def turn_x(tag, prev):
                if prev.startswith("ple"):
                    pe.wait_ge(*when("x_new", (prev, 1)))
                turn(tag, x, ("x_new", prev))

            def turn_y(tag, key):
                turn(tag, zs if tag.startswith("mix") and tag.endswith(".y") else xn, ("y", tag))

            def ffn(tag, n, half, gated):
                chunk = 0
                for first in range(0, n, half):
                    part = range(first, min(first + half, n))
                    for c in part:
                        if chunk >= 4:
                            pe.wait_ge(*when("hid_gated" if gated else "relu", (tag, chunk - 4)))
                        s = next_unit()
                        last_ = feature_chunk(s, ps[:, chunk % 4, 0:SEQ], h_hi, h_lo, KC,
                                              ready=tag if chunk == 0 else None)
                        if gated:
                            last_.then_inc(*up("w_used"))
                            s = next_unit()
                            last_ = feature_chunk(s, ps[:, chunk % 4, SEQ:2 * SEQ], h_hi, h_lo, KC)
                        last_.then_inc(*up("w_used", ("up", tag, chunk)))
                        chunk += 1
                    final = part[-1] == n - 1
                    for j, c in enumerate(part[:len(part) - LAST] if final else part):
                        pe.wait_ge(*when("hid_lo", (tag, c)))
                        s = next_unit()
                        last_ = row_chunk(s, lambda t, m: ps[:, 4 + 2 * t + m, :], hid_hi[:, j, :], hid_lo[:, j, :],
                                          0, c == 0, False)
                        last_.then_inc(*up("w_used"))
                    if final:
                        last_units(tag, [(hid_hi[:, j, :], hid_lo[:, j, :], ("hid_lo", (tag, part[j])))
                                         for j in range(len(part) - LAST, len(part))])

            def post(tag, r, factor, then):
                pass

            def ln(tag, r):
                pass

            def qkv(tag, i):
                for c in range(24):
                    if c >= 4:
                        pe.wait_ge(*when("pre", (tag, c - 4)))
                    else:
                        pe.wait_ge(*when("glu", (tag, c + 4)))
                    s = next_unit()
                    last_ = feature_chunk(s, ps[:, c % 4, 0:SEQ], h_hi, h_lo, KC)
                    last_.then_inc(*up("w_used", ("qkv", tag, c)))

            def project16(tag, bank=4):
                s = next_unit()
                for t in range(NT):
                    for k in range(KC):
                        tok, c = slice(t * P, (t + 1) * P), slice(k * 16, (k + 1) * 16)
                        out = ps[:, bank + t, 0:16]
                        mm(out, h_hi[:, k, tok], w_hi[:, s, c], k == 0, False)
                        mm(out, h_hi[:, k, tok], w_lo[:, s, c], False, False)
                        last_ = mm(out, h_lo[:, k, tok], w_hi[:, s, c], False, k == KC - 1)
                last_.then_inc(*up("w_used", ("small", tag)))

            def glu_(tag, i):
                for c in range(KC):
                    if c >= 4:
                        pe.wait_ge(*when("glu", (tag, c - 4)))
                    s = next_unit()
                    last_ = feature_chunk(s, ps[:, c % 4, 0:SEQ], h_hi, h_lo, KC, ready=tag if c == 0 else None)
                    last_.then_inc(*up("w_used"))
                    s = next_unit()
                    last_ = feature_chunk(s, ps[:, c % 4, SEQ:2 * SEQ], h_hi, h_lo, KC)
                    last_.then_inc(*up("w_used", ("glu", tag, c)))

            def blend(tag):
                pass

            def heads(bank, f):
                for h in range(GROUP):
                    last_ = f(heads_in(bank)[:, h, :], h)
                return last_

            def side(tag):
                def product(what):
                    for k in range(KC):
                        if what == "cnv":
                            pe.wait_ge(*when("h_lo", (tag + ".c", k | 1)))
                        s = next_unit()
                        last_ = row_chunk(s, lambda t, n: ps[:, 4 + 2 * t + n, :], h_hi[:, k, :], h_lo[:, k, :],
                                          0, k == 0, k == KC - 1)
                        last_.then_inc(*up("w_used", *([("product", f"{tag}.{what}")] if k == KC - 1 else [])))
                        yield
                    yield

                pe.wait_ge(*when("small", tag))
                yield from product("z")
                pe.wait_ge(*when("evacuated", (tag + ".z", 1)))
                yield from product("ga")
                pe.wait_ge(*when("evacuated", (tag + ".ga", 1)))
                yield from product("gb")
                pe.wait_ge(*when("evacuated", (tag + ".gb", 1)))
                for n, src in enumerate((hc, hsq)):
                    for t in range(NT):
                        for c in range(KC):
                            if n == 0:
                                pe.wait_ge(*when("conv", (tag, c)))
                            elif c == 0 and t == 0:
                                pe.wait_ge(*when("ln_square", tag))
                            last_ = mm(ps[:, 4 + 2 * n, t:t + 1], src[:, c, t * P:(t + 1) * P],
                                       const[:, C_MEAN, 0:1], c == 0, c == KC - 1)
                    last_.then_inc(*up("ln_mean", (tag, n)))
                    yield
                    pe.wait_ge(*(when("ln_mean_out", tag) if n == 0 else when("root", tag + ".c")))
                    for t in range(NT):
                        last_ = mm(ps[:, 5 + 2 * n, t * P:(t + 1) * P],
                                   lnm[:, 2 * n + t:2 * n + t + 1].to_broadcast([P, P]), ident)
                    last_.then_inc(*up("ln_spread", (tag, n)))
                    yield
                yield
                yield
                pe.wait_ge(*when("ln_norm", tag))
                yield from product("cnv")

            def delta(tag, i):
                before = None
                for t, g in ((t, g) for t in range(NT) for g in range(GROUPS)):
                    tok = slice(t * P, (t + 1) * P)
                    key = (tag, t, g)
                    tr = nc.tensor.transpose
                    if before is None:
                        pe.wait_ge(*when("silu_qkv", (tag, 23)))
                        pe.wait_ge(*when("decays", tag))
                    else:
                        pe.wait_ge(*when("state", (tag, before[1], min(2 * before[0] + 1, 2))))
                    for n in range(3):
                        last_ = heads(n, lambda o, h: tr(o, qkvT[:, n * GH + g * GROUP + h, tok], ident))
                        last_.then_inc(*up("turned", ("tm", key, n)))
                    gs = gate[:, 2 * t + 1, 0:GH]
                    if g == 0:
                        if before:
                            pe.wait_ge(*when("y_raw", (tag, *before)))
                        for n, m in enumerate((C_INC, C_SAME, C_IND0, C_IND1)):
                            last_ = mm(ps[:, 3, n * GH:(n + 1) * GH], const[:, m, :], gs)
                        last_.then_inc(*up("sums", (tag, t)))
                    yield
                    if g == 0:
                        pe.wait_ge(*when("sums_out", (tag, t)))
                    else:
                        pe.wait_ge(*when("y_raw", (tag, *before)))
                    last_ = heads(3, lambda o, h: mm(o, gs[:, g * GROUP + h:g * GROUP + h + 1].to_broadcast([P, P]),
                                                     const[:, C_INC, :]))
                    last_.then_inc(*up("grow", key))
                    yield
                    for n, (w, name) in enumerate(((0, "qn"), (1, "kn"), (4, "kb"), (5, "qd"))):
                        pe.wait_ge(*when(name, key))
                        if n == 2:
                            pe.wait_ge(*when("vb", key))
                        if n == 3:
                            pe.wait_ge(*when("dif_min", key))
                        last_ = heads(n, lambda o, h: tr(o, W[w][:, h, :], ident))
                        last_.then_inc(*up("turned", ("hm", key, n)))
                        if n == 1:
                            yield
                    yield
                    pe.wait_ge(*when("hm", (key, 2)))
                    heads(0, lambda o, h: mm(o, W[1][:, h, :], W[4][:, h, :])).then_inc(*up("kk", key))
                    heads(1, lambda o, h: mm(o, W[1][:, h, :], W[0][:, h, :])).then_inc(*up("qk", key))
                    yield
                    pe.wait_ge(*when("level_m", (key, 0)))
                    pe.wait_ge(*when("qk_out", key))
                    heads(1, lambda o, h: tr(o, W[4][:, h, :], ident)).then_inc(*up("tmt", (key, 0)))
                    yield
                    for n in range(1, len(LEVELS)):
                        pe.wait_ge(*when("level_m", (key, n)))
                        pe.wait_ge(*when("t0", (key, n - 1)))
                        heads(0, lambda o, h: mm(o, W[4][:, h, :], W[0][:, h, :])).then_inc(*up("mt", (key, n)))
                        yield
                        pe.wait_ge(*when("x_out", (key, n)))
                        pe.wait_ge(*when("tt", (key, n - 1)))
                        if n == 1:
                            pe.wait_ge(*when("hm", (key, 3)))
                        if n < len(LEVELS) - 1:
                            heads(1, lambda o, h: mm(o, W[1][:, h, :], W[6][:, h, :])).then_inc(*up("tmt", (key, n)))
                        heads(2, lambda o, h: mm(o, W[6][:, h, :], W[1][:, h, :])).then_inc(*up("tmtT", (key, n)))
                        yield
                    pe.wait_ge(*when("tt", (key, len(LEVELS) - 1)))
                    heads(0, lambda o, h: mm(o, W[1][:, h, :], rhs[:, h, 0:GDK])).then_inc(*up("u", key))
                    heads(1, lambda o, h: mm(o, rhs[:, h, GDK:2 * GDK], W[1][:, h, :])).then_inc(*up("wT", key))
                    yield
                    for j in range(2):
                        ci = 2 * t + j
                        r = slice(j * CH, (j + 1) * CH)
                        if ci > 0:
                            pe.wait_ge(*when("wT_out", key))
                            pe.wait_ge(*when("state", (tag, g, ci - 1)))
                            for h in range(GROUP):
                                last_ = mm(heads_in(2)[r, h, :], W[4][:, h, r], state[:, g * GROUP + h, :])
                            last_.then_inc(*up("ws", (tag, g, ci)))
                        yield
                        pe.wait_ge(*when("v_new", (tag, g, ci)))
                        if ci < 3:
                            for h in range(GROUP):
                                last_ = mm(heads_in(0)[:, h, :], W[7][r, h, :], W[6][r, h, :])
                            last_.then_inc(*up("kv", (tag, g, ci)))
                        for h in range(GROUP):
                            o = heads_in(3)[r, h, :]
                            if ci > 0:
                                mm(o, W[5][:, h, r], state[:, g * GROUP + h, :], True, False)
                            last_ = mm(o, W[2][r, h, r], W[6][r, h, :], ci == 0, True)
                        last_.then_inc(*up("o", (tag, g, ci)))
                        yield
                    yield
                    before = (t, g)

            def mixer(tag, i, r):
                interleave(delta(tag, i), side(tag))
                pe.wait_ge(*when("y_raw", (tag, NT - 1, GROUPS - 1)))

            def gla(tag, j):
                def chunk(c):
                    if c >= 4:
                        pe.wait_ge(*when("lqk", (tag, c - 4)))
                    s = next_unit()
                    last_ = feature_chunk(s, ps[:, c % 4, 0:SEQ], h_hi, h_lo, KC, ready=tag if c == 0 else None)
                    last_.then_inc(*up("w_used", ("lqk", tag, c)))

                def side():
                    for what in ("v", "r"):
                        pe.wait_ge(*(when("lsum_out", tag) if what == "v" else when("evacuated", (tag + ".v", 1))))
                        for k in range(KC):
                            s = next_unit()
                            last_ = row_chunk(s, lambda t, n: ps[:, 4 + 2 * t + n, :], h_hi[:, k, :], h_lo[:, k, :],
                                              0, k == 0, k == KC - 1)
                            last_.then_inc(*up("w_used", *([("product", f"{tag}.{what}")] if k == KC - 1 else [])))
                            yield
                        yield

                chunk(0)
                project16(tag)
                chunk(1)
                pe.wait_ge(*when("lg", tag))
                for t in range(NT):
                    last_ = mm(ps[0:16, 6, t * P:(t + 1) * P], lg[:, t, :], ident)
                last_.then_inc(*up("lgT", tag))
                chunk(2)
                pe.wait_ge(*when("lgT_out", tag))
                pe.wait_ge(*when("wgu_in", tag))
                for t in range(NT):
                    last_ = mm(ps[:, 4 + t, :], lgT[:, t * P:(t + 1) * P], wgu[:, :])
                last_.then_inc(*up("lgate", tag))
                for c in range(3, 7):
                    chunk(c)
                pe.wait_ge(*when("la", tag))
                for h in range(LH):
                    for t in range(NT):
                        last_ = mm(ps[:, 6 + h // 2, (h % 2) * SEQ + t * P:(h % 2) * SEQ + (t + 1) * P],
                                   la[:, t, h * P:(h + 1) * P], const[:, C_INC, :])
                last_.then_inc(*up("lsum", tag))
                chunk(7)
                pe.wait_ge(*when("lqk", (tag, 7)))
                beside = side()
                for n in range(1 + len(LEVELS)):
                    if n >= 1:
                        pe.wait_ge(*when("lke", (tag, n)))
                    for t in range(NT):
                        if n >= 1:
                            pe.wait_ge(*when("lscore", (tag, n - 1, t)))
                        for h in range(LH):
                            tok = slice(t * P, (t + 1) * P)
                            a, b = (lkT, lqT) if n == 0 else (lke, lqe)
                            last_ = mm(ps[:, t, h * P:(h + 1) * P], a[:, h, tok], b[:, h, tok])
                        last_.then_inc(*up("lsq", (tag, n, t)))
                    next(beside)
                    next(beside)
                for _ in beside:
                    pass
                pe.wait_ge(*when("lkd", tag))
                for t in range(NT):
                    for h in range(LH):
                        last_ = nc.tensor.transpose(ps[:, 2 + t, h * P:(h + 1) * P], lke[:, h, t * P:(t + 1) * P], ident)
                    last_.then_inc(*up("lkdT", (tag, t)))
                for ci in range(4):
                    t, r = ci // 2, slice((ci % 2) * CH, (ci % 2 + 1) * CH)
                    if ci == 0:
                        pe.wait_ge(*when("evacuated", (tag + ".r", 1)))
                        pe.wait_ge(*when("lscore", (tag, len(LEVELS), 1)))
                    pe.wait_ge(*when("lkd_out", (tag, t)))
                    if ci >= 1:
                        pe.wait_ge(*when("lst", (tag, ci - 1)))
                    if ci < 3:
                        for h in range(LH):
                            last_ = mm(ps[:, h // 2, (h % 2) * LDV:(h % 2 + 1) * LDV], lkd[r, t, h, :],
                                       lv[r, t, h * LDV:(h + 1) * LDV])
                        last_.then_inc(*up("lkv", (tag, ci)))
                    for h in range(LH):
                        o = ps[r, 4 + 2 * t + h // 2, (h % 2) * LDV:(h % 2 + 1) * LDV]
                        if ci > 0:
                            mm(o, lqe[:, h, ci * CH:(ci + 1) * CH], lst[:, h, :], True, False)
                        last_ = mm(o, lsc[r, t, h, r], lv[r, t, h * LDV:(h + 1) * LDV], ci == 0, True)
                    last_.then_inc(*up("lo", (tag, ci)))
                turn(tag + ".y", xn, ("y", tag + ".y"))

            def mla(tag, j):
                for k in range(0, KC, 2):
                    s = next_unit()
                    for kk in range(2):
                        pe.wait_ge(*when("h_lo", (tag, k + kk)))
                        last_ = row_chunk(s, lambda t, n: ps[:, 4 + t, :], h_hi[:, k + kk, :], h_lo[:, k + kk, :],
                                          kk * 512, k + kk == 0, k + kk == KC - 1, 512, 1)
                    last_.then_inc(*up("w_used", *([("mc", tag)] if k == KC - 2 else [])))
                s = next_unit()
                for t in range(NT):
                    for k in range(KC):
                        tok, c = slice(t * P, (t + 1) * P), slice(k * MR, (k + 1) * MR)
                        out = ps[:, 6, t * MR:(t + 1) * MR]
                        mm(out, h_hi[:, k, tok], w_hi[:, s, c], k == 0, False)
                        mm(out, h_hi[:, k, tok], w_lo[:, s, c], False, False)
                        last_ = mm(out, h_lo[:, k, tok], w_hi[:, s, c], False, k == KC - 1)
                last_.then_inc(*up("w_used", ("mkr", tag)))
                for t in range(NT):
                    pe.wait_ge(*when("mcn", (tag, t)))
                    for c in range(4):
                        at = (c % 2) * SEQ + t * P
                        last_ = nc.tensor.transpose(ps[:, c // 2, at:at + P], mcn[:, t, c * P:(c + 1) * P], ident)
                        if t == NT - 1:
                            last_.then_inc(*up("turned", (tag + ".c", c)))
                for n, first in ((0, 0), (1, 2)):
                    for c0 in range(0, MH, 4):
                        s = next_unit()
                        for c in range(c0, c0 + 4):
                            if n == 0 and c < 4:
                                pe.wait_ge(*when("h_lo", (tag + ".c", 3)))
                            g = n * MH + c
                            if g >= 4:
                                pe.wait_ge(*when("mT", (tag, g - 4)))
                            last_ = feature_chunk(s, ps[:, g % 4, 0:SEQ], h_hi[:, first:first + 2], h_lo[:, first:first + 2],
                                                  2, (c - c0) * 2)
                        last_.then_inc(*up("w_used", *[("mT", tag, n * MH + c) for c in range(c0, c0 + 4)]))
                    if n == 0:
                        s = next_unit()
                        pe.wait_ge(*when("mc_out", (tag, 1)))
                        for k in range(2):
                            last_ = row_chunk(s, lambda t, m: ps[:, 4 + t, :], h_hi[:, k, :], h_lo[:, k, :],
                                              k * 512, k == 0, k == 1, 512, 1)
                        last_.then_inc(*up("w_used", ("mqr", tag)))
                pe.wait_ge(*when("mqr_out", (tag, 1)))
                pe.wait_ge(*when("mkr_out", tag))
                for k in range(2):
                    s = next_unit()
                    last_ = row_chunk(s, lambda t, n: ps[:, 4 + 2 * t + n, :], h_hi[:, 2 + k, :], h_lo[:, 2 + k, :],
                                      0, k == 0, k == 1)
                    last_.then_inc(*up("w_used", *([("product", tag + ".v")] if k == 1 else [])))
                pe.wait_ge(*when("mT", (tag, 2 * MH - 1)))
                pe.wait_ge(*when("roped", tag))
                for t in range(NT):
                    for c in range(4):
                        nc.tensor.transpose(ps[:, c // 2, (c % 2) * SEQ + t * P:(c % 2) * SEQ + (t + 1) * P],
                                            mqr2[:, t, c * P:(c + 1) * P], ident)
                    last_ = nc.tensor.transpose(ps[:, 2, t * P:(t + 1) * P], mkr[:, t, :], ident)
                last_.then_inc(*up("turned", (tag + ".r", 0)))
                pe.wait_ge(*when("rT_out", tag))
                pe.wait_ge(*when("evacuated", (tag + ".v", 1)))
                for t in range(NT):
                    tok = slice(t * P, (t + 1) * P)
                    if t == 1:
                        pe.wait_ge(*when("msm", (tag, 0)))
                    for h in range(MH):
                        p = slot_of(h)
                        o = ps[:, p // 2, (p % 2) * SEQ:(p % 2 + 1) * SEQ]
                        b = (h % 2) * MR
                        mm(o, mqnT[:, h, tok], mknT[:, h, :], True, False)
                        last_ = mm(o, mqrT[b:b + MR, h // 2, tok], mkrT[b:b + MR, :], False, True)
                    last_.then_inc(*up("mscore", (tag, t)))
                    pe.wait_ge(*when("mexp", (tag, t)))
                    nk = NT
                    for h in range(MH):
                        for k in range(nk):
                            at = (h % 2) * SEQ + k * P
                            last_ = nc.tensor.transpose(ps[:, 4 + h // 2, at:at + P], msc[:, h, k * P:(k + 1) * P], ident)
                    last_.then_inc(*up("mpT", (tag, t)))
                    pe.wait_ge(*when("mpT_out", (tag, t)))
                    for h in range(MH):
                        for k in range(nk):
                            last_ = mm(pair(0)[:, slot_of(h), :], mpT[:, slot_of(h), k, :],
                                       mv[:, k, h * P:(h + 1) * P], k == 0, k == nk - 1)
                    last_.then_inc(*up("mo", (tag, t)))
                    pe.wait_ge(*when("y", (tag + ".y", t)))
                turn(tag + ".y", xn, ("y", tag + ".y"))

            def conv(tag, j):
                for c in range(KC):
                    if c >= 4:
                        pe.wait_ge(*when("cu", (tag, c - 4)))
                    s = next_unit()
                    feature_chunk(s, ps[:, c % 4, 0:SEQ], h_hi, h_lo, KC, ready=tag if c == 0 else None).then_inc(*up("w_used"))
                    s = next_unit()
                    feature_chunk(s, ps[:, c % 4, SEQ:2 * SEQ], h_hi, h_lo, KC).then_inc(*up("w_used", ("cu", tag, c)))
                for c in range(KC):
                    if c < 4:
                        pe.wait_ge(*when("cu", (tag, c + 4)))
                    else:
                        pe.wait_ge(*when("cbz", (tag, c - 4)))
                    s = next_unit()
                    feature_chunk(s, ps[:, c % 4, 0:SEQ], h_hi, h_lo, KC).then_inc(*up("w_used", ("cb", tag, c)))

            def ple(tag, i):
                pe.wait_ge(*when("ple_lo", tag))
                for k in range(2):
                    s = next_unit()
                    last_ = row_chunk(s, lambda t, n: ps[:, 2 * t + n, :], ple_hi[:, k, :], ple_lo[:, k, :],
                                      0, k == 0, k == 1)
                    last_.then_inc(*up("w_used", *([("product", tag)] if k == 1 else [])))

            def project_(tag, bank):
                main = tag.rsplit(".", 1)[0]
                ready = {"out": main + (".o" if main.startswith("mix") else ".y"),
                         "gdn": main + ".y", "g": main}.get(tag.rsplit(".", 1)[1])
                more = ("cnv_y", (main, 1)) if tag.endswith("gdn") else None
                project(tag, bank, ready=ready, more=more)

            pe.wait_ge(sg.sem("const_in"), 16)
            table = dict(norm=norm, turn_x=turn_x, turn=turn_y, ffn=ffn, post=post, ln=ln, qkv=qkv, project=project_,
                         project16=project16, glu=glu_, mixer=mixer, blend=blend,
                         gla=gla, mla=mla, conv=conv, ple=ple)
            for name, *args in STAGES:
                table[name](*args)
            sg.at["units"] = used[0]

        @block.scalar
        def _(act):
            made, pos, owed = [0], [0], [0]
            A = nc.scalar.activation

            def weights(n):
                pos[0] += n
                while made[0] < min(pos[0] + NS, NU):
                    u, s = made[0], made[0] % NS
                    made[0] += 1
                    wd = unit_width(UNITS[u])
                    act.wait_ge(w_in[s], 16 * (u // NS + 1))
                    if u >= NS:
                        act.wait_ge(sg.sem("w_used"), u - NS + 1)
                    A(w_hi[:, s, 0:wd], w_raw[:, s, 0:wd], ACT.Copy).then_inc(*up("w_hi", u))

            def ahead(n, last):
                for k in range(n - LAST if last else n):
                    weights(1)
                owed[0] = LAST if last else 0

            def take(tag, scale=None, n=KC):
                for c in range(n):
                    act.wait_ge(*when("turned", (tag, c | 1)))
                    src = ps[:, c // 2, (c % 2) * SEQ:(c % 2 + 1) * SEQ]
                    sc = 1.0 if scale is None else scale(c)
                    A(h_hi[:, c, :], src, ACT.Copy, scale=sc).then_inc(*up("h_hi", (tag, c)))
                weights(owed[0])
                owed[0] = 0

            def turn(tag, key=None):
                take(tag)

            def norm(tag, prev, key):
                if prev == "x_in":
                    for t in range(NT):
                        act.wait_ge(*when("x_new", (prev, t)))
                        A(xn[:, t, :], x[:, t, :], ACT.Square,
                          accum_out=st[:, 0, 4 + t:5 + t]).then_inc(*up("sumsq", (tag, t)))
                take(tag, lambda c: col(key, c))

            def product_wait(name, t):
                if t == 0:
                    act.wait_ge(*when("product_0", name))
                else:
                    act.wait_ge(*when("w_used", ("product", name)))

            def turn_x(tag, prev):
                take(tag)
                if tag.startswith("ple"):
                    act.wait_ge(*when("ple_in", tag))
                    A(ple_hi[:, :, :], ple_p[:, :, :], ACT.Copy).then_inc(*up("ple_hi", tag))

            def ffn(tag, n, half, gated):
                chunk = 0
                for first in range(0, n, half):
                    part = range(first, min(first + half, n))
                    for c in part:
                        act.wait_ge(*when("w_used", ("up", tag, chunk)))
                        s = chunk % 2
                        if chunk >= 2:
                            act.wait_ge(*when("hid_gated" if gated else "hid_lo", (tag, chunk - 2)))
                        if gated:
                            A(act_out[:, s, :], ps[:, chunk % 4, 0:SEQ], ACT.Silu).then_inc(*up("silu", (tag, chunk)))
                        else:
                            A(act_out[:, s, :], ps[:, chunk % 4, 0:SEQ], ACT.Relu).then_inc(*up("relu", (tag, chunk)))
                        weights(2 if gated else 1)
                        if not gated:
                            act.wait_ge(*when("relu", (tag, chunk)))
                            A(hid[:, s, :], act_out[:, s, :], ACT.Square).then_inc(*up("hid_square", (tag, chunk)))
                        chunk += 1
                    ahead(len(part), part[-1] == n - 1)

            def post(tag, r, factor, then):
                for t in range(NT):
                    product_wait(tag + ".out" if tag.startswith("mix") else tag, t)
                    for n in range(2):
                        if n:
                            act.wait_ge(*when("scaled", (tag, t, 1)))
                        elif t:
                            act.wait_ge(*when("sumsq", (tag + ".p", 0, 1)))
                        A(row[:, r % 2, 1, n * BANK:(n + 1) * BANK], ps[:, 4 + 2 * t + n, :], ACT.Square,
                          accum_out=st[:, 0, 2 * t + n:2 * t + n + 1]).then_inc(*up("sumsq", (tag + ".p", t, n)))
                    if then:
                        act.wait_ge(*when("x_new", (tag, t)))
                        A(xn[:, t, :], x[:, t, :], ACT.Square,
                          accum_out=st[:, 0, 4 + t:5 + t]).then_inc(*up("sumsq", (then, t)))

            def ln(tag, r):
                for t in range(NT):
                    act.wait_ge(*when("less_mean", (tag, t)))
                    A(ple_g[:, t, :], x[:, t, :], ACT.Square, bias=st[:, 3, 8 + t:9 + t],
                      accum_out=st[:, 0, t:t + 1]).then_inc(*up("sumsq", (tag, t)))

            def qkv(tag, i):
                act.wait_ge(*when("glu", (tag, KC - 1)))
                for c in range(25):
                    if c < 24:
                        act.wait_ge(*when("w_used", ("qkv", tag, c)))
                        if c >= 2:
                            act.wait_ge(*when("conv4", (tag, c - 2)))
                        src = ps[:, c % 4, 0:SEQ]
                        A(pre[:, c % 2, CONV1 - 1:], src, ACT.Copy).then_inc(*up("pre_in", (tag, c)))
                        if c >= 2:
                            act.wait_ge(*when("silu_qkv", (tag, c - 2)))
                        A(cacc[:, c % 2, :], src, ACT.Copy, scale=col(("convw", i), c * CONV1 + CONV1 - 1)).then_inc(*up("pre", (tag, c)))
                        weights(1)
                    if c >= 1:
                        act.wait_ge(*when("conv4", (tag, c - 1)))
                        A(qkvT[:, c - 1, :], cacc[:, (c - 1) % 2, :], ACT.Silu).then_inc(*up("silu_qkv", (tag, c - 1)))

            def project(tag, bank):
                main, what = tag.rsplit(".", 1)
                ahead(KC, what in ("out", "gdn"))
                out, f = {"z": (zs, ACT.Silu), "ga": (ga, ACT.Sigmoid), "gb": (gb, ACT.Sigmoid),
                          "v": (lv, ACT.Copy), "r": (lr, ACT.Silu), "g": (ple_g, ACT.Sigmoid)}.get(what, (None, None))
                if out is not None:
                    act.wait_ge(*when("w_used", ("product", tag)))
                    for t in range(NT):
                        A(out[:, t, :], acc(bank, t), f).then_inc(*up("evacuated", (tag, t)))

            def project16(tag):
                weights(1)
                if tag.startswith("gla"):
                    act.wait_ge(*when("w_used", ("small", tag)))
                    A(lg[:, :, :], ps[:, 4:6, 0:16], ACT.Copy).then_inc(*up("lg", tag))
                    return
                act.wait_ge(*when("small", tag))
                A(gate[:, 0:3:2, 0:GH], small[:, 0:2, 0:GH], ACT.Sigmoid).then_inc(*up("beta", tag))
                act.wait_ge(*when("a_in", tag))
                A(small[:, 10, 0:GH], gate[:, 5, 0:GH], ACT.Exp).then_inc(*up("a_exp", tag))
                A(small[:, 4:6, 0:GH], small[:, 2:4, 0:GH], ACT.Abs).then_inc(*up("s_step", ("abs", tag)))
                act.wait_ge(*when("s_step", ("abs", tag)))
                A(small[:, 6:8, 0:GH], small[:, 4:6, 0:GH], ACT.Exp, scale=-1.0).then_inc(*up("s_step", ("exp", tag)))
                act.wait_ge(*when("s_step", ("exp", tag)))
                A(small[:, 8:10, 0:GH], small[:, 6:8, 0:GH], ACT.Ln, bias=1.0).then_inc(*up("softplus", tag))

            def glu_(tag, i):
                for c in range(KC):
                    act.wait_ge(*when("w_used", ("glu", tag, c)))
                    if c >= 2:
                        act.wait_ge(*when("glu", (tag, c - 2)))
                    A(sig[:, c % 2, :], ps[:, c % 4, SEQ:2 * SEQ], ACT.Sigmoid, bias=col(("pw1b", i), KC + c)).then_inc(*up("sig", (tag, c)))
                    weights(2)

            def nothing(*args):
                pass

            def side(tag, i):
                def product(what, out=None, f=None):
                    for k in range(KC):
                        if k:
                            weights(1)
                        yield
                    weights(1)
                    if out is not None:
                        act.wait_ge(*when("w_used", ("product", f"{tag}.{what}")))
                        for t in range(NT):
                            A(out[:, t, :], acc(4, t), f).then_inc(*up("evacuated", (f"{tag}.{what}", t)))
                    yield

                def channels(first):
                    for c in range(first, first + KC // 2):
                        A(hsq[:, c, :], hc[:, c, :], ACT.Silu, bias=col(("lnb", i), c),
                          scale=col(("lng", i), c)).then_inc(*up("cnv_act", (tag, c)))
                    for c in range(first, first + KC // 2):
                        act.wait_ge(*when("cnv_act", (tag, c)))
                        A(h_hi[:, c, :], hsq[:, c, :], ACT.Copy).then_inc(*up("h_hi", (tag + ".c", c)))

                yield from product("z", zs, ACT.Silu)
                yield from product("ga", ga, ACT.Sigmoid)
                yield from product("gb", gb, ACT.Sigmoid)
                yield
                act.wait_ge(*when("ln_center", tag))
                A(hsq, hc[:, :, :], ACT.Square).then_inc(*up("ln_square", tag))
                yield
                yield
                yield
                act.wait_ge(*when("ln_norm", tag))
                channels(0)
                yield
                channels(KC // 2)
                yield
                yield from product("cnv")

            def delta(tag, i):
                for t, g in ((t, g) for t in range(NT) for g in range(GROUPS)):
                    key = (tag, t, g)
                    if t or g:
                        act.wait_ge(*when("out_square", (tag, t if g else 0, 0 if g else 1)))
                    for n, w in enumerate((6, 3)):
                        act.wait_ge(*when("turned", ("tm", key, n)))
                        for h in range(GROUP):
                            at = n * GROUP + h
                            A(W[w][:, h, :], heads_in(n)[:, h, :], ACT.Square,
                              accum_out=gate[:, 10, at:at + 1]).then_inc(*up("head_square", (key, n)))
                    yield
                    if g == 0:
                        act.wait_ge(*when("kdiff", (tag, t)))
                        A(gate[:, 8 + t, :], gate[:, 6 + t, :], ACT.Exp).then_inc(*up("gexp", (tag, t)))
                    act.wait_ge(*when("dif_min", key))
                    A(W[2][:, :, :], W[2][:, :, :], ACT.Exp).then_inc(*up("dec", key))
                    yield
                    act.wait_ge(*when("rhs", key))
                    for n, w in enumerate((0, 1, 4, 5)):
                        act.wait_ge(*when("turned", ("hm", key, n)))
                        A(W[w][:, :, :], heads_in(n), ACT.Copy).then_inc(*up("hm", (key, n)))
                        if n == 1:
                            yield
                    yield
                    yield
                    yield
                    for n in range(1, len(LEVELS)):
                        act.wait_ge(*when("mt", (key, n)))
                        A(W[6][:, :, :], heads_in(0), ACT.Copy).then_inc(*up("x_out", (key, n)))
                        yield
                        yield
                    act.wait_ge(*when("u", key))
                    A(W[0][:, :, :], heads_in(0), ACT.Copy).then_inc(*up("u_out", key))
                    act.wait_ge(*when("wT", key))
                    A(W[4][:, :, :], heads_in(1), ACT.Copy).then_inc(*up("wT_out", key))
                    yield
                    for _ in range(4):
                        yield
                    act.wait_ge(*when("o", (tag, g, 2 * t + 1)))
                    for h in range(GROUP):
                        A(W[6][:, h, :], heads_in(3)[:, h, :], ACT.Square,
                          accum_out=gate[:, 11, h:h + 1]).then_inc(*up("out_square", key))
                    yield

            def mixer(tag, i, r):
                interleave(delta(tag, i), side(tag, i))

            def gla(tag, j):
                def chunk(c):
                    act.wait_ge(*when("w_used", ("lqk", tag, c)))
                    out = lqT[:, c, :] if c < 4 else lkT[:, c - 4, :]
                    A(out, ps[:, c % 4, 0:SEQ], ACT.Copy,
                      scale=NORM_SCALE if c < 4 else 1.0).then_inc(*up("lqk", (tag, c)))
                    weights(1)

                def side():
                    for what, out, f in (("v", lv, ACT.Copy), ("r", lr, ACT.Silu)):
                        for k in range(KC):
                            if k:
                                weights(1)
                            yield
                        weights(1)
                        act.wait_ge(*when("w_used", ("product", f"{tag}.{what}")))
                        for t in range(NT):
                            A(out[:, t, :], acc(4, t), f).then_inc(*up("evacuated", (f"{tag}.{what}", t)))
                        yield

                chunk(0)
                project16(tag)
                chunk(1)
                act.wait_ge(*when("lgT", tag))
                act.wait_ge(*when("lgT_one", tag))
                A(lgT[0:16, :], ps[0:16, 6, 0:SEQ], ACT.Copy).then_inc(*up("lgT_out", tag))
                chunk(2)
                act.wait_ge(*when("lgate", tag))
                A(la[:, :, :], ps[:, 4:6, :], ACT.Abs).then_inc(*up("s_step", ("abs", tag)))
                chunk(3)
                act.wait_ge(*when("s_step", ("abs", tag)))
                A(la[:, :, :], la[:, :, :], ACT.Exp, scale=-1.0).then_inc(*up("s_step", ("exp", tag)))
                act.wait_ge(*when("s_step", ("exp", tag)))
                A(la[:, :, :], la[:, :, :], ACT.Ln, bias=1.0).then_inc(*up("softplus", tag))
                for c in range(4, 8):
                    chunk(c)
                beside = side()
                for n in range(1 + len(LEVELS)):
                    if n:
                        act.wait_ge(*when("ld", (tag, n)))
                        A(ld[:, :, :], ld[:, :, :], ACT.Abs).then_inc(*up("s_step", ("ld", tag, n)))
                        act.wait_ge(*when("s_step", ("ld", tag, n)))
                        A(ld[:, :, :], ld[:, :, :], ACT.Exp, scale=-1.0).then_inc(*up("le", (tag, n)))
                    next(beside)
                    next(beside)
                for _ in beside:
                    pass
                act.wait_ge(*when("lke", (tag, len(LEVELS))))
                A(ld[:, :, :], LT[:, :, :], ACT.Exp).then_inc(*up("le", (tag, "q")))
                A(lend[:, :, :], LT[:, :, CH - 1::CH], ACT.Exp).then_inc(*up("lend", tag))
                act.wait_ge(*when("ld", (tag, "k")))
                A(ld[:, :, :], ld[:, :, :], ACT.Exp).then_inc(*up("le", (tag, "k")))
                for t in range(NT):
                    act.wait_ge(*when("lkdT", (tag, t)))
                    A(lkd[:, t], ps[:, 2 + t, :].rearrange("p (h k) -> p h k", k=P), ACT.Copy).then_inc(*up("lkd_out", (tag, t)))
                for t in range(NT):
                    act.wait_ge(*when("lo", (tag, 2 * t + 1)))
                    A(xn[:, t, :], acc(4, t), ACT.Square).then_inc(*up("out_square", (tag, t)))
                take(tag + ".y")

            def mla(tag, j):
                act.wait_ge(*when("angle", tag))
                for n in range(2):
                    A(rope[:, :, n, :], rope[:, :, n + 2, :], ACT.Sin).then_inc(*up("sine", tag))
                for k in range(0, KC, 2):
                    weights(1)
                act.wait_ge(*when("w_used", ("mc", tag)))
                for t in range(NT):
                    A(mc[:, t, :], ps[:, 4 + t, :], ACT.Copy).then_inc(*up("mc_out", (tag, t)))
                    for n in range(2):
                        A(mcn[:, t, n * 256:(n + 1) * 256], ps[:, 4 + t, n * 256:(n + 1) * 256], ACT.Square, accum_out=st[:, 0, 2 * t + n:2 * t + n + 1]).then_inc(*up("sumsq", (tag + ".c", t)))
                weights(1)
                act.wait_ge(*when("w_used", ("mkr", tag)))
                A(mkr[:, :, MR:], ps[:, 6, 0:P].rearrange("p (t n) -> p t n", t=NT), ACT.Copy).then_inc(*up("mkr_out", tag))
                take(tag + ".c", lambda c: col(("qnorm", 0), c) if c < 2 else col(("kvnorm", 0), c - 2), 4)
                for n in range(2):
                    for c in range(MH):
                        g = n * MH + c
                        act.wait_ge(*when("w_used", ("mT", tag, g)))
                        out = (mqnT if n == 0 else mknT)[:, c, :]
                        A(out, ps[:, g % 4, 0:SEQ], ACT.Copy).then_inc(*up("mT", (tag, g)))
                        if c % 4 == 3:
                            weights(1)
                    if n == 0:
                        weights(1)
                        act.wait_ge(*when("w_used", ("mqr", tag)))
                        for t in range(NT):
                            A(mqr[:, t, :], ps[:, 4 + t, :], ACT.Copy).then_inc(*up("mqr_out", (tag, t)))
                weights(2)
                act.wait_ge(*when("w_used", ("product", tag + ".v")))
                for t in range(NT):
                    A(mv[:, t, :], acc(4, t), ACT.Copy).then_inc(*up("evacuated", (tag + ".v", t)))
                act.wait_ge(*when("turned", (tag + ".r", 0)))
                A(mqrT[:, :, :], acc(0, 0).rearrange("p (c t) -> p c t", t=SEQ), ACT.Copy).then_inc(*up("rT_out", "half"))
                A(mkrT[:, :], ps[:, 2, 0:SEQ], ACT.Copy).then_inc(*up("rT_out", tag))
                for t in range(NT):
                    act.wait_ge(*when("mmax", (tag, t)))
                    for h in range(MH):
                        A(msc[:, h, :], msc[:, h, :], ACT.Exp, scale=MLA_SCALE, bias=mst[:, 1, h:h + 1], accum_out=mst[:, 2, h:h + 1]).then_inc(*up("mexp", (tag, t)))
                    act.wait_ge(*when("mpT", (tag, t)))
                    A(mpT[:, :, :, :], ps[:, 4:8, :].rearrange("p b (h k q) -> p (b h) k q", h=2, k=NT), ACT.Copy).then_inc(*up("mpT_out", (tag, t)))
                take(tag + ".y")

            def conv(tag, j):
                for c in range(KC):
                    act.wait_ge(*when("w_used", ("cu", tag, c)))
                    if c >= 2:
                        act.wait_ge(*when("cu", (tag, c - 2)))
                    A(ctmp[:, c % 2, :], ps[:, c % 4, 0:SEQ], ACT.Copy).then_inc(*up("ctmp", (tag, c)))
                    weights(2)
                for c in range(KC):
                    weights(1)
                act.wait_ge(*when("w_used", ("cb", tag, KC - 1)))
                for c in range(KC):
                    act.wait_ge(*when("cbz", (tag, c)))
                    A(h_hi[:, c, :], cz[:, c, :], ACT.Copy).then_inc(*up("h_hi", (tag + ".y", c)))

            def ple(tag, i):
                weights(2)

            act.wait_ge(sg.sem("cols_in"), 16)
            weights(0)
            table = dict(norm=norm, turn_x=turn_x, turn=turn, ffn=ffn, post=post, ln=ln, qkv=qkv, project=project,
                         project16=project16, glu=glu_, mixer=mixer, blend=nothing,
                         gla=gla, mla=mla, conv=conv, ple=ple)
            for name, *args in STAGES:
                table[name](*args)
            weights(0)

        @block.vector
        def _(dve):
            made, pos, owed, steps, taps = [0], [0], [0], [0], [None]
            V = nc.vector

            def link(ins):
                steps[0] += 1
                ins.then_inc(*up("v_step", steps[0]))
                dve.wait_ge(sg.sem("v_step"), steps[0])

            def weights(n):
                pos[0] += n
                while made[0] < min(pos[0] + NS, NU):
                    u, s = made[0], made[0] % NS
                    made[0] += 1
                    wd = unit_width(UNITS[u])
                    dve.wait_ge(*when("w_hi", u))
                    V.tensor_tensor(w_lo[:, s, 0:wd], w_raw[:, s, 0:wd], w_hi[:, s, 0:wd].bitcast(F32), ALU.subtract).then_inc(*up("w_lo", u))

            def ahead(n, last):
                for k in range(n - LAST if last else n):
                    weights(1)
                owed[0] = LAST if last else 0

            def take(tag, scale=None, n=KC):
                for c in range(n):
                    dve.wait_ge(*when("h_hi", (tag, c | 1)))
                    src = ps[:, c // 2, (c % 2) * SEQ:(c % 2 + 1) * SEQ]
                    hi = h_hi[:, c, :].bitcast(F32)
                    if scale is None:
                        ins = V.tensor_tensor(h_lo[:, c, :], src, hi, ALU.subtract)
                    else:
                        ins = V.scalar_tensor_tensor(h_lo[:, c, :], src, scale(c), hi, ALU.mult, ALU.subtract)
                    ins.then_inc(*up("h_lo", (tag, c)))
                weights(owed[0])
                owed[0] = 0

            def turn(tag, key=None):
                take(tag)

            def root(tag, n, scale, eps):
                V.tensor_scalar(st[:, 1, 0:n], st[:, 0, 0:n], scale, eps, ALU.mult, ALU.add).then_inc(*up("mean", tag))
                dve.wait_ge(*when("root", tag))

            def product_wait(name, t):
                if t == 0:
                    dve.wait_ge(*when("product_0", name))
                else:
                    dve.wait_ge(*when("w_used", ("product", name)))

            def norm_mean(tag, t):
                dve.wait_ge(*when("sumsq", (tag, t)))
                V.tensor_scalar(st[:, 1, 4 + t:5 + t], st[:, 0, 4 + t:5 + t], 1.0 / D, RMS_EPS, ALU.mult,
                                ALU.add).then_inc(*up("mean", (tag, t)))

            def normed(tag, t):
                dve.wait_ge(*when("root", (tag, t)))
                V.tensor_scalar(xn[:, t, :], x[:, t, :], st[:, 1, 4 + t:5 + t], None,
                                ALU.mult).then_inc(*up("xn", (tag, t)))

            def norm(tag, prev, key):
                if prev == "x_in":
                    for t in range(NT):
                        norm_mean(tag, t)
                        normed(tag, t)
                take(tag, lambda c: col(key, c))

            def turn_x(tag, prev):
                take(tag)
                if tag.startswith("ple"):
                    dve.wait_ge(*when("ple_hi", tag))
                    V.tensor_tensor(ple_lo[:, :, :], ple_p[:, :, :], ple_hi[:, :, :].bitcast(F32), ALU.subtract).then_inc(*up("ple_lo", tag))

            def ffn(tag, n, half, gated):
                chunk = 0
                for first in range(0, n, half):
                    part = range(first, min(first + half, n))
                    for j, c in enumerate(part):
                        s = chunk % 2
                        if gated:
                            dve.wait_ge(*when("silu", (tag, chunk)))
                            V.tensor_tensor(hid[:, s, :], act_out[:, s, :], ps[:, chunk % 4, SEQ:2 * SEQ], ALU.mult).then_inc(*up("hid_gated", (tag, chunk)))
                        weights(2 if gated else 1)
                        dve.wait_ge(*when("hid_gated" if gated else "hid_square", (tag, chunk)))
                        V.tensor_copy(hid_hi[:, j, :], hid[:, s, :]).then_inc(*up("hid_hi", (tag, chunk)))
                        dve.wait_ge(*when("hid_hi", (tag, chunk)))
                        V.tensor_tensor(hid_lo[:, j, :], hid[:, s, :], hid_hi[:, j, :].bitcast(F32), ALU.subtract).then_inc(*up("hid_lo", (tag, chunk)))
                        chunk += 1
                    ahead(len(part), part[-1] == n - 1)

            def post(tag, r, factor, then):
                weight = row[:, r % 2, 0, :]
                k = 1.0 / D / factor ** 2

                def scaled(t):
                    product_wait(tag + ".out" if tag.startswith("mix") else tag, t)
                    V.tensor_tensor(xn[:, t, BANK:], ps[:, 5 + 2 * t, :], weight[:, BANK:],
                                    ALU.mult).then_inc(*up("scaled", (tag, t, 1)))
                    dve.wait_ge(*when("sumsq", (tag + ".p", t, 0)))
                    V.tensor_tensor(xn[:, t, 0:BANK], ps[:, 4 + 2 * t, :], weight[:, 0:BANK],
                                    ALU.mult).then_inc(*up("scaled", (tag, t, 0)))
                    link(V.tensor_scalar(st[:, 3, t:t + 1], st[:, 0, 2 * t:2 * t + 1], k, RMS_EPS / factor ** 2,
                                         ALU.mult, ALU.add))
                    dve.wait_ge(*when("sumsq", (tag + ".p", t, 1)))
                    V.scalar_tensor_tensor(st[:, 1, t:t + 1], st[:, 0, 2 * t + 1:2 * t + 2], k, st[:, 3, t:t + 1],
                                           ALU.mult, ALU.add).then_inc(*up("mean", (tag + ".p", t)))

                def added(t):
                    dve.wait_ge(*when("root", (tag + ".p", t)))
                    V.scalar_tensor_tensor(x[:, t, :], xn[:, t, :], st[:, 1, t:t + 1], x[:, t, :], ALU.mult,
                                           ALU.add).then_inc(*up("x_new", (tag, t), ("row", r), ("end", t)))

                dve.wait_ge(*when(f"row_in{r % 2}", r))
                scaled(0)
                added(0)
                if then:
                    norm_mean(then, 0)
                scaled(1)
                if then:
                    normed(then, 0)
                added(1)
                if then:
                    norm_mean(then, 1)
                    normed(then, 1)

            def ln(tag, r):
                dve.wait_ge(*when(f"row_in{r % 2}", r))
                for t in range(NT):
                    product_wait(tag if tag.startswith("mlp") else tag + ".out", t)
                    link(V.scalar_tensor_tensor(x[:, t, :], x[:, t, :], ALPHA, acc(4, t), ALU.mult, ALU.add,
                                                accum_out=st[:, 3, t:t + 1]))
                    less = st[:, 3, 8 + t:9 + t]
                    V.tensor_scalar(less, st[:, 3, t:t + 1], -1.0 / D, None,
                                    ALU.mult).then_inc(*up("less_mean", (tag, t)))
                    dve.wait_ge(*when("less_mean", (tag, t)))
                    V.scalar_tensor_tensor(xn[:, t, :], x[:, t, :], less, row[:, r % 2, 0, :], ALU.add,
                                           ALU.mult).then_inc(*up("scaled", (tag, t)))
                    dve.wait_ge(*when("sumsq", (tag, t)))
                    V.tensor_scalar(st[:, 1, t:t + 1], st[:, 0, t:t + 1], 1.0 / D, LN_EPS, ALU.mult,
                                    ALU.add).then_inc(*up("mean", (tag, t)))
                    dve.wait_ge(*when("root", (tag, t)))
                    V.scalar_tensor_tensor(x[:, t, :], xn[:, t, :], st[:, 1, t:t + 1], row[:, r % 2, 1, :], ALU.mult,
                                           ALU.add).then_inc(*up("x_new", (tag, t), ("row", r), ("end", t)))

            def qkv(tag, i):
                link(V.memset(pre[:, :, 0:CONV1 - 1], 0.0))
                for c in range(24):
                    dve.wait_ge(*when("pre", (tag, c)))
                    for k in range(CONV1 - 2, -1, -1):
                        ins = V.scalar_tensor_tensor(cacc[:, c % 2, :], pre[:, c % 2, k:k + SEQ],
                                                     col(("convw", i), c * CONV1 + k), cacc[:, c % 2, :],
                                                     ALU.mult, ALU.add)
                        if k:
                            link(ins)
                        else:
                            ins.then_inc(*up("conv4", (tag, c)))
                    weights(1)
                    if c % 4 == 3:
                        next(taps[0])

            def project(tag, bank):
                ahead(KC, tag.rsplit(".", 1)[1] in ("out", "gdn"))

            def project16(tag):
                weights(1)
                if tag.startswith("gla"):
                    return
                dve.wait_ge(*when("w_used", ("small", tag)))
                V.tensor_copy(small[:, 0:2, :], ps[:, 4:6, 0:16]).then_inc(*up("small", tag))
                dve.wait_ge(*when("small", tag))
                dve.wait_ge(*when("gate_in", tag))
                dt = over(gate[:, 4, 0:GH], NT)
                V.tensor_tensor(small[:, 2:4, 0:GH], small[:, 0:2, GH:2 * GH], dt, ALU.add).then_inc(*up("a_in", tag))
                dve.wait_ge(*when("a_in", tag))
                link(V.tensor_scalar(small[:, 12:14, 0:GH], small[:, 2:4, 0:GH], 0.0, None, ALU.max))
                dve.wait_ge(*when("softplus", tag))
                link(V.tensor_tensor(small[:, 14:16, 0:GH], small[:, 12:14, 0:GH], small[:, 8:10, 0:GH], ALU.add))
                ea = over(small[:, 10, 0:GH], NT)
                V.scalar_tensor_tensor(gate[:, 1:4:2, 0:GH], small[:, 14:16, 0:GH], -1.0, ea, ALU.mult, ALU.mult).then_inc(*up("decays", tag))

            def glu_(tag, i):
                link(V.memset(glu[:, :, 0:CONVB - 1], 0.0))
                taps[0] = conv_taps(tag, i)
                for c in range(KC):
                    dve.wait_ge(*when("sig", (tag, c)))
                    V.scalar_tensor_tensor(glu[:, c, CONVB - 1:], ps[:, c % 4, 0:SEQ], col(("pw1b", i), c), sig[:, c % 2, :], ALU.add, ALU.mult).then_inc(*up("glu", (tag, c)))
                    weights(2)
                    if c >= 4:
                        next(taps[0])
                        next(taps[0])

            def conv_taps(tag, i):
                for first in range(0, KC, 4):
                    dve.wait_ge(*when("glu", (tag, first + 3)))
                    for k in range(CONVB):
                        for c in range(first, first + 4):
                            w = col(("dww", i), c * CONVB + k)
                            if k == 0:
                                ins = V.tensor_scalar(hc[:, c, :], glu[:, c, 0:SEQ], w, col(("dwb", i), c),
                                                      ALU.mult, ALU.add)
                            else:
                                dve.wait_ge(*when("conv", ("tap", tag, c, k - 1)))
                                ins = V.scalar_tensor_tensor(hc[:, c, :], glu[:, c, k:k + SEQ], w, hc[:, c, :],
                                                             ALU.mult, ALU.add)
                            ins.then_inc(*up("conv", ("tap", tag, c, k), *([(tag, c)] if k == CONVB - 1 else [])))
                        yield

            def side(tag, i, r):
                def product():
                    for k in range(KC):
                        if k:
                            weights(1)
                        yield
                    weights(1)
                    yield

                def channels(first):
                    for c in range(first, first + KC // 2):
                        dve.wait_ge(*when("h_hi", (tag + ".c", c)))
                        V.tensor_tensor(h_lo[:, c, :], hsq[:, c, :], h_hi[:, c, :].bitcast(F32),
                                        ALU.subtract).then_inc(*up("h_lo", (tag + ".c", c)))

                for _ in range(3):
                    yield from product()
                for _ in taps[0]:
                    pass
                dve.wait_ge(*when("ln_mean", (tag, 0)))
                V.tensor_copy(lnm[:, 0:2], ps[:, 4, 0:2]).then_inc(*up("ln_mean_out", tag))
                yield
                dve.wait_ge(*when("ln_spread", (tag, 0)))
                V.tensor_tensor(hc[:, :, :], hc[:, :, :], over(ps[:, 5, 0:SEQ], KC),
                                ALU.subtract).then_inc(*up("ln_center", tag))
                yield
                dve.wait_ge(*when("ln_mean", (tag, 1)))
                V.tensor_scalar(lnm[:, 2:4], ps[:, 6, 0:2], LN_EPS, None, ALU.add).then_inc(*up("mean", tag + ".c"))
                yield
                dve.wait_ge(*when("ln_spread", (tag, 1)))
                V.tensor_tensor(hc[:, :, :], hc[:, :, :], over(ps[:, 7, 0:SEQ], KC),
                                ALU.mult).then_inc(*up("ln_norm", tag))
                yield
                channels(0)
                yield
                channels(KC // 2)
                yield
                for k in range(KC):
                    if k:
                        weights(1)
                    yield
                weights(1)
                dve.wait_ge(*when("w_used", ("product", tag + ".cnv")))
                dve.wait_ge(*when(f"row_in{r % 2}", r))
                for t in range(NT):
                    V.tensor_tensor(xn[:, t, :], acc(4, t), row[:, r % 2, 0, :],
                                    ALU.add).then_inc(*up("cnv_y", (tag, t), ("row", r)))
                    dve.wait_ge(*when("cnv_y", (tag, t)))
                    link(V.tensor_tensor(gb[:, t, :], gb[:, t, :], xn[:, t, :], ALU.mult))
                yield

            def delta(tag, i):
                TT_ = V.tensor_tensor

                def step():
                    next(taps[0], None)

                for t, g in ((t, g) for t in range(NT) for g in range(GROUPS)):
                    key = (tag, t, g)
                    hs = slice(g * GROUP, (g + 1) * GROUP)
                    sums, exps = gate[:, 6 + t, :], gate[:, 8 + t, :]
                    beta = gate[:, 2 * t, hs]
                    sc = gate[:, 10, :]
                    if g == 0:
                        dve.wait_ge(*when("sums", (tag, t)))
                        V.tensor_copy(sums[:, 0:32], ps[:, 3, 0:32]).then_inc(*up("sums_out", (tag, t)))
                        dve.wait_ge(*when("sums_out", (tag, t)))
                        TT_(sums[:, 32:40], sums[:, 8:16], sums[:, 0:8], ALU.subtract).then_inc(*up("kdiff", (tag, t)))
                    for n in range(2):
                        dve.wait_ge(*when("head_square", (key, n)))
                    link(V.tensor_scalar(sc[:, 16:20], sc[:, 0:4], L2_EPS, float(GDK), ALU.add, ALU.mult))
                    V.tensor_scalar(sc[:, 20:24], sc[:, 4:8], L2_EPS, None, ALU.add).then_inc(*up("mean", ("g", key)))
                    step()
                    yield
                    dve.wait_ge(*when("grow", key))
                    for h in range(GROUP):
                        V.tensor_scalar(W[2][:, h, :], heads_in(3)[:, h, :], sums[:, g * GROUP + h:g * GROUP + h + 1], 0.0,
                                        ALU.subtract, ALU.min).then_inc(*up("dif_min", key))
                    dve.wait_ge(*when("root", ("g", key)))
                    TT_(W[0][:, :, :], heads_in(0), wide(sc[:, 16:20], GDK), ALU.mult).then_inc(*up("qn", key))
                    TT_(W[1][:, :, :], heads_in(1), wide(sc[:, 20:24], GDK), ALU.mult).then_inc(*up("kn", key))
                    if t == 0 and g == 0:
                        dve.wait_ge(*when("beta", tag))
                    TT_(rhs[:, :, 0:GDK], heads_in(2), wide(beta, GDK), ALU.mult).then_inc(*up("vb", key))
                    dve.wait_ge(*when("gexp", (tag, t)))
                    dve.wait_ge(*when("kn", key))
                    link(TT_(sc[:, 32:36], beta, exps[:, hs], ALU.mult))
                    TT_(W[4][:, :, :], W[1][:, :, :], wide(beta, GDK), ALU.mult).then_inc(*up("kb", key))
                    TT_(W[5][:, :, :], W[0][:, :, :], wide(exps[:, hs], GDK), ALU.mult).then_inc(*up("qd", key))
                    TT_(rhs[:, :, GDK:], W[1][:, :, :], wide(sc[:, 32:36], GDK), ALU.mult).then_inc(*up("rhs_k", key))
                    ke = exps[:, 32 + g * GROUP:32 + (g + 1) * GROUP]
                    TT_(W[7][:, :, :], W[1][:, :, :], wide(ke, GDK), ALU.mult).then_inc(*up("rhs", key))
                    step()
                    yield
                    dve.wait_ge(*when("dec", key))
                    link(TT_(W[3][:, :, :], W[2][:, :, :], over(const[:, C_STRICT, :], GROUP), ALU.mult))
                    step()
                    yield
                    link(TT_(W[2][:, :, :], W[2][:, :, :], over(const[:, C_INC, :], GROUP), ALU.mult))
                    step()
                    yield
                    dve.wait_ge(*when("kk", key))
                    link(TT_(W[3][:, :, :], heads_in(0), W[3][:, :, :], ALU.mult))
                    TT_(W[4][:, :, :], W[3][:, :, :], over(const[:, C_LVL, :], GROUP),
                        ALU.mult).then_inc(*up("level_m", (key, 0)))
                    dve.wait_ge(*when("qk", key))
                    TT_(W[2][:, :, :], heads_in(1), W[2][:, :, :], ALU.mult).then_inc(*up("qk_out", key))
                    dve.wait_ge(*when("level_m", (key, 0)))
                    TT_(W[1][:, :, :], over(ident, GROUP), W[4][:, :, :], ALU.subtract).then_inc(*up("tt", (key, 0)))
                    step()
                    yield
                    dve.wait_ge(*when("tmt", (key, 0)))
                    TT_(W[0][:, :, :], over(ident, GROUP), heads_in(1), ALU.subtract).then_inc(*up("t0", (key, 0)))
                    dve.wait_ge(*when("tt", (key, 0)))
                    TT_(W[4][:, :, :], W[3][:, :, :], over(const[:, C_LVL + 1, :], GROUP),
                        ALU.mult).then_inc(*up("level_m", (key, 1)))
                    step()
                    yield
                    for n in range(1, len(LEVELS)):
                        step()
                        yield
                        if n < len(LEVELS) - 1:
                            dve.wait_ge(*when("mt", (key, n)))
                            TT_(W[4][:, :, :], W[3][:, :, :], over(const[:, C_LVL + n + 1, :], GROUP),
                                ALU.mult).then_inc(*up("level_m", (key, n + 1)))
                            dve.wait_ge(*when("tmt", (key, n)))
                            dve.wait_ge(*when("t0", (key, n - 1)))
                            TT_(W[0][:, :, :], W[0][:, :, :], heads_in(1), ALU.subtract).then_inc(*up("t0", (key, n)))
                        dve.wait_ge(*when("tmtT", (key, n)))
                        dve.wait_ge(*when("tt", (key, n - 1)))
                        TT_(W[1][:, :, :], W[1][:, :, :], heads_in(2), ALU.subtract).then_inc(*up("tt", (key, n)))
                        step()
                        yield
                    step()
                    yield
                    for j in range(2):
                        ci = 2 * t + j
                        r = slice(j * CH, (j + 1) * CH)
                        dve.wait_ge(*when("u_out", key))
                        if ci == 0:
                            ins = V.tensor_copy(W[6][r], W[0][r])
                        else:
                            dve.wait_ge(*when("ws", (tag, g, ci)))
                            ins = TT_(W[6][r], W[0][r], heads_in(2)[r], ALU.subtract)
                        ins.then_inc(*up("v_new", (tag, g, ci)))
                        step()
                        yield
                        if ci < 3:
                            st_ = state[:, hs, :]
                            if ci > 0:
                                dve.wait_ge(*when("o", (tag, g, ci)))
                                link(TT_(st_, st_, wide(exps[:, 16 + 8 * j:24 + 8 * j][:, hs], GDK), ALU.mult))
                                ins = TT_(st_, st_, heads_in(0), ALU.add)
                            else:
                                dve.wait_ge(*when("kv", (tag, g, ci)))
                                ins = V.tensor_copy(st_, heads_in(0))
                            ins.then_inc(*up("state", (tag, g, ci)))
                        step()
                        yield
                    dve.wait_ge(*when("out_square", key))
                    so = gate[:, 11, :]
                    V.tensor_scalar(so[:, 8:12], so[:, 0:4], 1.0 / GDK, RMS_EPS, ALU.mult,
                                    ALU.add).then_inc(*up("mean", ("o", key)))
                    step()
                    dve.wait_ge(*when("root", ("o", key)))
                    TT_(W[0][:, :, :], heads_in(3), wide(so[:, 8:12], GDK), ALU.mult).then_inc(*up("y_raw", key))
                    dve.wait_ge(*when("y_raw", key))
                    link(TT_(W[0][:, :, :], W[0][:, :, :], gnw[:, :, :].to_broadcast([P, GROUP, GDK]), ALU.mult))
                    if t == 0 and g == 0:
                        dve.wait_ge(*when("evacuated", (tag + ".z", 1)))
                    z = zs[:, t, g * GROUP * GDK:(g + 1) * GROUP * GDK].rearrange("p (h k) -> p h k", k=GDK)
                    TT_(z, W[0][:, :, :], z, ALU.mult).then_inc(*up("y", (tag + ".y", t)))
                    yield

            def mixer(tag, i, r):
                interleave(delta(tag, i), side(tag, i, r))

            def blend(tag):
                for t in range(NT):
                    product_wait(tag + ".gdn", t)
                    link(V.tensor_tensor(ga[:, t, :], ga[:, t, :], acc(4, t), ALU.mult))
                    V.tensor_tensor(xn[:, t, :], ga[:, t, :], gb[:, t, :], ALU.add).then_inc(*up("y", (tag + ".o", t)))

            def gla(tag, j):
                V.memset(lgT[:, :], 1.0).then_inc(*up("lgT_one", tag))
                link(V.memset(lsc[:, :, :, :], 0.0))
                weights(4)
                dve.wait_ge(*when("s_step", ("abs", tag)))
                link(V.tensor_scalar(lb_[:, :, :], ps[:, 4:6, :], 0.0, None, ALU.min))
                weights(1)
                dve.wait_ge(*when("softplus", tag))
                V.tensor_tensor(la[:, :, :], lb_[:, :, :], la[:, :, :], ALU.subtract).then_inc(*up("la", tag))
                weights(3)
                dve.wait_ge(*when("lsum", tag))
                flat = LT[:, :, :].rearrange("p h t -> p (h t)")
                V.tensor_scalar(flat, acc(6, 0), 1.0 / TAU, None, ALU.mult).then_inc(*up("lsum_out", tag))
                dve.wait_ge(*when("lsum_out", tag))
                weights(1)

                def distance(n):
                    b = LEVELS[n - 1]
                    L = LT[:, :, :].rearrange("p h (c b) -> p (h c) b", b=2 * b)
                    o = ld[:, :, :].rearrange("p h (c b) -> p (h c) b", b=2 * b)
                    mid = L[:, :, b - 1:b].to_broadcast([P, LH * SEQ // (2 * b), 2 * b])
                    V.tensor_tensor(o, L, mid, ALU.subtract).then_inc(*up("ld", (tag, n)))

                def side():
                    for _ in range(2):
                        for k in range(KC):
                            if k:
                                weights(1)
                            yield
                        weights(1)
                        yield

                beside = side()
                for n in range(1 + len(LEVELS)):
                    if n:
                        dve.wait_ge(*when("le", (tag, n)))
                        if n >= 2:
                            dve.wait_ge(*when("lsq", (tag, n - 1, 1)))
                        link(V.tensor_tensor(lqe[:, :, :], lqT[:, :, :], ld[:, :, :], ALU.mult))
                        V.tensor_tensor(lke[:, :, :], lkT[:, :, :], ld[:, :, :], ALU.mult).then_inc(*up("lke", (tag, n)))
                    if n < len(LEVELS):
                        if n:
                            dve.wait_ge(*when("lke", (tag, n)))
                        distance(n + 1)
                    next(beside)
                    next(beside)
                    m = const[:, C_ID if n == 0 else C_SYM + n - 1, :].bitcast(I32)
                    for t in range(NT):
                        dve.wait_ge(*when("lsq", (tag, n, t)))
                        src = ps[:, t, :].rearrange("p (h k) -> p h k", k=P)
                        V.copy_predicated(lsc[:, t], over(m, LH), src).then_inc(*up("lscore", (tag, n, t)))
                for _ in beside:
                    pass
                dve.wait_ge(*when("le", (tag, "q")))
                link(V.tensor_tensor(lqe[:, :, :], lqT[:, :, :], ld[:, :, :], ALU.mult))
                L = LT[:, :, :].rearrange("p h (c b) -> p (h c) b", b=CH)
                o = ld[:, :, :].rearrange("p h (c b) -> p (h c) b", b=CH)
                end = L[:, :, CH - 1:CH].to_broadcast([P, LH * 4, CH])
                V.tensor_tensor(o, end, L, ALU.subtract).then_inc(*up("ld", (tag, "k")))
                dve.wait_ge(*when("le", (tag, "k")))
                V.tensor_tensor(lke[:, :, :], lkT[:, :, :], ld[:, :, :], ALU.mult).then_inc(*up("lkd", tag))
                for t in range(NT):
                    for ci in (2 * t, 2 * t + 1):
                        if ci == 3:
                            continue
                        dve.wait_ge(*when("lo", (tag, ci)))
                        if ci == 0:
                            dve.wait_ge(*when("lend", tag))
                            V.tensor_copy(lst[:, :, :].rearrange("p h v -> p (h v)"), acc(0, 0)).then_inc(*up("lst", (tag, ci)))
                        else:
                            for h in range(LH):
                                V.scalar_tensor_tensor(lst[:, h, :], lst[:, h, :], lend[:, h, ci:ci + 1], acc(0, 0)[:, h * LDV:(h + 1) * LDV], ALU.mult, ALU.add).then_inc(*up("lst", (tag, ci)))
                    dve.wait_ge(*when("out_square", (tag, t)))
                    y = xn[:, t, :].rearrange("p (h k) -> p h k", k=LDV)
                    link(V.tensor_reduce(st[:, 0, 0:LH], y, AX.X, ALU.add))
                    root(("l", tag, t), LH, 1.0 / LDV, RMS_EPS)
                    link(V.tensor_tensor(y, acc(4, t).rearrange("p (h k) -> p h k", k=LDV), wide(st[:, 2, 0:LH], LDV),
                                         ALU.mult))
                    if t == 0:
                        dve.wait_ge(*when("wgu_in", tag))
                    link(V.tensor_tensor(y, y, gln[:, :, :].to_broadcast([P, LH, LDV]), ALU.mult))
                    V.tensor_tensor(xn[:, t, :], xn[:, t, :], lr[:, t, :], ALU.mult).then_inc(*up("y", (tag + ".y", t)))
                take(tag + ".y")

            def mla(tag, j):
                dve.wait_ge(*when("mla_in", tag))
                link(V.tensor_copy(posf[:, :], posi[:, :]))
                for t in range(NT):
                    link(V.tensor_scalar(rope[:, t, 4, :], invf[:, :], posf[:, t:t + 1], None, ALU.mult))
                for n, shift in enumerate((0.0, 0.25)):
                    a, q, red = rope[:, :, 4, :], rope[:, :, 5, :], rope[:, :, n + 2, :]
                    link(V.tensor_scalar(q, a, 1.0 / TWO_PI, shift, ALU.mult, ALU.add))
                    link(V.tensor_scalar(q, q, ROUND, None, ALU.add))
                    link(V.tensor_scalar(q, q, ROUND, None, ALU.subtract))
                    link(V.scalar_tensor_tensor(red, q, -PI_PARTS[0], a, ALU.mult, ALU.add))
                    for part in PI_PARTS[1:]:
                        link(V.scalar_tensor_tensor(red, q, -part, red, ALU.mult, ALU.add))
                    link(V.tensor_scalar(red, red, shift * TWO_PI, None, ALU.add))
                    V.tensor_scalar(red, red, PI_IN, -PI_IN, ALU.min, ALU.max).then_inc(*up("angle", tag))
                weights(4)
                for t in range(NT):
                    dve.wait_ge(*when("sumsq", (tag + ".c", t)))
                root(tag + ".c", 4, 1.0 / 256, RMS_EPS)
                for t in range(NT):
                    for n in range(2):
                        c = slice(n * 256, (n + 1) * 256)
                        dve.wait_ge(*when("mc_out", (tag, t)))
                        V.tensor_scalar(mcn[:, t, c], mc[:, t, c], st[:, 2, 2 * t + n:2 * t + n + 1], None, ALU.mult).then_inc(*up("mcn", (tag, t)))
                weights(1)
                take(tag + ".c", lambda c: col(("qnorm", 0), c) if c < 2 else col(("kvnorm", 0), c - 2), 4)
                weights(7)
                dve.wait_ge(*when("sine", tag))

                def rotate(src, out, tmp, t, n):
                    cos = over(rope[:, t, 1, :], n)
                    sin = over(rope[:, t, 0, :], n)
                    x1, x2, o1, o2 = src[:, :, 0:32], src[:, :, 32:64], out[:, :, 0:32], out[:, :, 32:64]
                    t1, t2 = tmp[:, :, 0:32], tmp[:, :, 32:64]
                    link(V.tensor_tensor(o1, x1, cos, ALU.mult))
                    link(V.tensor_tensor(t1, x2, sin, ALU.mult))
                    link(V.tensor_tensor(o2, x2, cos, ALU.mult))
                    link(V.tensor_tensor(t2, x1, sin, ALU.mult))
                    link(V.tensor_tensor(o1, o1, t1, ALU.subtract))
                    return V.tensor_tensor(o2, o2, t2, ALU.add)

                def heads_of(ap):
                    return ap.rearrange("p (h d) -> p h d", d=MR)

                dve.wait_ge(*when("mkr_out", tag))
                for t in range(NT):
                    link(rotate(heads_of(mkr[:, t, MR:]), heads_of(mkr[:, t, 0:MR]), heads_of(mcn[:, t, 0:MR]), t, 1))
                    link(V.tensor_copy(mkr[:, t, MR:], mkr[:, t, 0:MR]))
                for t in range(NT):
                    dve.wait_ge(*when("mqr_out", (tag, t)))
                    rotate(heads_of(mqr[:, t, :]), heads_of(mqr2[:, t, :]), heads_of(mcn[:, t, :]), t, MH).then_inc(*up("roped", tag))
                for t in range(NT):
                    dve.wait_ge(*when("mscore", (tag, t)))
                    s = ps[:, 0:4, :].rearrange("p b (h k) -> p (b h) k", k=SEQ)
                    V.tensor_tensor(msc[:, :, :], s, over(mask[:, t, :], MH), ALU.add).then_inc(*up("msm", (tag, t)))
                    dve.wait_ge(*when("msm", (tag, t)))
                    link(V.tensor_reduce(mst[:, 0, :], msc[:, :, :], AX.X, ALU.max))
                    V.tensor_scalar(mst[:, 1, :], mst[:, 0, :], -MLA_SCALE, None, ALU.mult).then_inc(*up("mmax", (tag, t)))
                    dve.wait_ge(*when("mexp", (tag, t)))
                    link(V.reciprocal(mst[:, 3, :], mst[:, 2, :]))
                    dve.wait_ge(*when("mo", (tag, t)))
                    for b in range(2):
                        y = xn[:, t, :].rearrange("p (a b k) -> p b a k", b=2, k=P)[:, b]
                        V.tensor_tensor(y, pair(0)[:, 4 * b:4 * b + 4, :], wide(mst[:, 3, 4 * b:4 * b + 4], P), ALU.mult).then_inc(*up("y", (tag + ".y", t)))
                take(tag + ".y")

            def conv(tag, j):
                link(V.memset(cpad[:, :, 0:2], 0.0))
                for c in range(KC):
                    dve.wait_ge(*when("ctmp", (tag, c)))
                    V.tensor_tensor(cpad[:, c, 2:], ctmp[:, c % 2, :], ps[:, c % 4, SEQ:2 * SEQ], ALU.mult).then_inc(*up("cu", (tag, c)))
                    weights(2)
                for c in range(KC):
                    for k in range(3):
                        w = col(("conv3", 0), c * 3 + k)
                        if k == 0:
                            dve.wait_ge(*when("cu", (tag, c)))
                            link(V.tensor_scalar(cz[:, c, :], cpad[:, c, 0:SEQ], w, None, ALU.mult))
                        else:
                            link(V.scalar_tensor_tensor(cz[:, c, :], cpad[:, c, k:k + SEQ], w, cz[:, c, :],
                                                        ALU.mult, ALU.add))
                    dve.wait_ge(*when("w_used", ("cb", tag, c)))
                    V.tensor_tensor(cz[:, c, :], cz[:, c, :], ps[:, c % 4, 0:SEQ], ALU.mult).then_inc(*up("cbz", (tag, c)))
                    weights(1)
                for c in range(KC):
                    dve.wait_ge(*when("h_hi", (tag + ".y", c)))
                    V.tensor_tensor(h_lo[:, c, :], cz[:, c, :], h_hi[:, c, :].bitcast(F32), ALU.subtract).then_inc(*up("h_lo", (tag + ".y", c)))

            def ple(tag, i):
                weights(2)
                dve.wait_ge(*when("w_used", ("product", tag)))
                dve.wait_ge(*when("evacuated", (tag + ".g", 1)))
                for t in range(NT):
                    link(V.tensor_tensor(xn[:, t, :], ple_g[:, t, :], acc(0, t), ALU.mult))
                    V.tensor_tensor(x[:, t, :], x[:, t, :], xn[:, t, :], ALU.add).then_inc(*up("x_new", (tag, t), ("end", t)))

            dve.wait_ge(sg.sem("cols_in"), 16)
            dve.wait_ge(sg.sem("const_in"), 16)
            dve.wait_ge(sg.sem("x_in"), 16)
            for t in range(NT):
                V.memset(neghalf[:, t * 8:(t + 1) * 8], -0.5).then_inc(*up("x_new", ("x_in", t)))
            weights(0)
            table = dict(norm=norm, turn_x=turn_x, turn=turn, ffn=ffn, post=post, ln=ln, qkv=qkv, project=project,
                         project16=project16, glu=glu_, mixer=mixer, blend=blend,
                         gla=gla, mla=mla, conv=conv, ple=ple)
            for name, *args in STAGES:
                table[name](*args)
            weights(0)

        @block.gpsimd
        def _(pool):
            loaded = [0]

            def rows_in(r):
                if r >= len(ROWS):
                    return
                if r >= 2:
                    pool.wait_ge(*when("cnv_y" if ROWS[r - 2][0][0] == "cnv_b_o" else "x_new", ("row", r - 2)))
                n = len(ROWS[r])
                pool.dma_start(row[:, r % 2, 0:n, :], io["rows"][r:r + 1, 0:n, :].to_broadcast([P, n, D])).then_inc(*up(f"row_in{r % 2}", r, by=16))

            def root(tag, n, out=None):
                pool.wait_ge(*when("mean", tag))
                src = st[:, 1, 0:n] if out is None else out
                dst = st[:, 2, 0:n] if out is None else out
                nc.gpsimd.tensor_tensor(dst, src, neghalf[:, 0:n], ALU.pow).then_inc(*up("root", tag))

            def norm(tag, prev, key):
                if prev == "x_in":
                    for t in range(NT):
                        root((tag, t), 1, st[:, 1, 4 + t:5 + t])

            def post(tag, r, factor, then):
                for t in range(NT):
                    root((tag + ".p", t), 1, st[:, 1, t:t + 1])
                    if then:
                        root((then, t), 1, st[:, 1, 4 + t:5 + t])
                rows_in(r + 2)

            def ln(tag, r):
                for t in range(NT):
                    root((tag, t), 1, st[:, 1, t:t + 1])
                rows_in(r + 2)

            def glu_(tag, i):
                pool.wait_ge(*when("x_new", (f"ffn1.{i}", 1)))
                pool.dma_start(gate[:, 4:6, 0:GH], io["gate_rows"][i:i + 1].to_broadcast([P, 2, GH])).then_inc(*up("gate_in", tag, by=16))
                pool.dma_start(gnw[:, :, :], io["gdn_norm"][i:i + 1].to_broadcast([P, 1, GDK])).then_inc(*up("gate_in", tag, by=16))

            def delta(tag, i):
                for t, g in ((t, g) for t in range(NT) for g in range(GROUPS)):
                    root(("g", (tag, t, g)), 8, gate[:, 10, 16:24])
                    for _ in range(GROUP_STEPS - 1):
                        yield
                    root(("o", (tag, t, g)), GROUP, gate[:, 11, 8:12])
                    yield

            def side(tag):
                for n in range(SIDE_STEPS):
                    if n == 3 * (KC + 1) + 2:
                        root(tag + ".c", NT, lnm[:, 2:4])
                    yield

            def mixer(tag, i, r):
                interleave(delta(tag, i), side(tag))
                rows_in(r + 2)

            def gla(tag, j):
                n = int(tag.split(".")[1])
                pool.wait_ge(*when("x_new", (f"ffn2.{L1 - 1}" if n == 0 else f"ple.{n - 1}", 1)))
                pool.dma_start(wgu[:, :], io["gla_gate"][j]).then_inc(*up("wgu_in", tag, by=16))
                pool.dma_start(gln[:, :, :], io["gla_norm"][j:j + 1].to_broadcast([P, 1, LDV])).then_inc(*up("wgu_in", tag, by=16))
                for t in range(NT):
                    root(("l", tag, t), LH)

            def mla(tag, j):
                pool.wait_ge(*when("x_new", ("ple.0", 1)))
                pool.dma_start(posi[:, :], io["positions"]).then_inc(*up("mla_in", tag, by=16))
                pool.dma_start(invf[:, :], io["inv_freq"]).then_inc(*up("mla_in", tag, by=16))
                pool.dma_start(mask[:, :, :], io["mask"]).then_inc(*up("mla_in", tag, by=16))
                root(tag + ".c", 4)

            def turn_x(tag, prev):
                if tag.startswith("ple"):
                    i = int(tag.split(".")[1])
                    pool.dma_start(ple_p[:, :, :], io["p"][i]).then_inc(*up("ple_in", tag, by=16))

            def nothing(*args):
                pass

            rows_in(0)
            rows_in(1)
            table = dict(norm=norm, post=post, ln=ln, glu=glu_, mixer=mixer, gla=gla,
                         mla=mla, turn_x=turn_x)
            for name, *args in STAGES:
                table.get(name, nothing)(*args)

        memory = dict(sg.at)
    return memory


TWO_PI = 2 * np.pi
PI_PARTS = [6.28125, 0.0019350051879882812, 3.019916050561e-07]
ROUND = 1.5 * 2.0 ** 23
PI_IN = 3.1415925


def unit_width(u):
    kind, w, i, a, b, n = u
    if kind == "T":
        return b * n * P
    k_all = K_OF.get(w, D) // P
    return min(k_all - a, UW // n) * n


K_OF = {"mla_uq_rope": 256, "mla_uv": 256, "ple_w_proj_2": 256, "ffn1_w_out": FF1, "ffn2_w_out": FF1,
        "mlp_w2_2": 4 * D}


def pack(inputs):
    f = {k: np.asarray(v) for k, v in inputs.items()}
    uq = f["mla_w_uq_2"].reshape(-1, 256, MH, MN + MR)
    ukv = f["mla_w_ukv_2"].reshape(-1, 256, MH, 2 * MN)
    f["mla_uq_nope"] = np.ascontiguousarray(uq[..., :MN]).reshape(-1, 256, MH * MN)
    f["mla_uq_rope"] = np.ascontiguousarray(uq[..., MN:]).reshape(-1, 256, MH * MR)
    f["mla_uk"] = np.ascontiguousarray(ukv[..., :MN]).reshape(-1, 256, MH * MN)
    f["mla_uv"] = np.ascontiguousarray(ukv[..., MN:]).reshape(-1, 256, MH * MN)
    units = unit_list()
    w = np.zeros((len(units), P, UW), np.float32)
    for n, (kind, name, i, a, b, c) in enumerate(units):
        src = f[name][i]
        if kind == "T":
            for m in range(c):
                blocks = src[:b * P, a + m * P:a + (m + 1) * P].reshape(b, P, P)
                w[n, :, m * b * P:(m + 1) * b * P] = blocks.transpose(1, 0, 2).reshape(P, b * P)
        else:
            k = min(src.shape[0] // P - a, UW // c)
            rows = src[a * P:(a + k) * P, b:b + c].reshape(k, P, c)
            w[n, :, :k * c] = rows.transpose(1, 0, 2).reshape(P, k * c)
    lay = column_layout()
    cols = np.zeros((P, lay.n), np.float32)
    for name, (key, i), n in lay.parts:
        at, v = lay.at[key, i], f[name][i]
        taps = v if v.ndim == 2 else v[None]
        cols[:, at:at + n] = taps.reshape(taps.shape[0], -1, P).transpose(2, 1, 0).reshape(P, n)
    places = row_layout()
    rows = np.zeros((len(places), 2, D), np.float32)
    for r, place in enumerate(places):
        for n, (name, *at) in enumerate(place):
            rows[r, n] = f[name][tuple(at)]
    inv_freq = (10000.0 ** (-np.arange(MR // 2) * 2.0 / MR)).astype(np.float32)
    return {
        "weights": w,
        "x": np.ascontiguousarray(f["x"][0].reshape(NT, P, D).transpose(1, 0, 2)),
        "const": constants(),
        "cols": cols,
        "rows": rows,
        "gate_rows": np.ascontiguousarray(np.stack([f["gdn_dt_bias"], f["gdn_a_log"]], 1)),
        "gdn_norm": np.ascontiguousarray(f["gdn_norm_w"][:, None]),
        "gla_gate": np.ascontiguousarray(np.concatenate([f["gla_w_gate_up_2"], f["gla_b_gate_2"][:, None]], 1)),
        "gla_norm": np.ascontiguousarray(f["gla_norm_g_2"][:, None]),
        "positions": np.ascontiguousarray(f["positions_2"].reshape(NT, P).T),
        "inv_freq": np.ascontiguousarray(np.broadcast_to(inv_freq, (P, 32))),
        "mask": attention_mask(),
        "p": np.ascontiguousarray(f["p_2"][:, 0].reshape(L2, SEQ, 2, P).transpose(0, 3, 2, 1)),
    }


def build(new_core, arrays, last=None):
    plan = None
    for _ in range(2):
        nc = new_core()
        io = {n: nc.dram_tensor("in_" + n, a.shape, mybir.dt.from_np(a.dtype), kind="ExternalInput").ap()
              for n, a in arrays.items()}
        io["out"] = nc.dram_tensor("out", (P, NT, D), F32, kind="ExternalOutput").ap()
        plan = emit(nc, io, plan, last)
    return nc


def kernel(**inputs):
    import concourse.bacc as bacc
    from concourse.bass_utils import run_bass_kernel_spmd

    arrays = pack(inputs)
    nc = build(lambda: bacc.Bacc("TRN2", target_bir_lowering=False, num_devices=1), arrays)
    r = run_bass_kernel_spmd(nc, [{"in_" + n: a for n, a in arrays.items()}], core_ids=[0])
    out = np.asarray(r.results[0]["out"])
    return np.ascontiguousarray(out.transpose(1, 0, 2)).reshape(1, SEQ, D)
```
